# Optimizing a Trainium2 kernel written in Bass

```python
import jax
import jax.numpy as jnp
from jax import lax
import numpy as np

D_MODEL = 1024
BATCH = 1
SEQ = 1024
DEPTH = 1
DEC_BATCH = 1
DEC_SEQ = 64
PAST_LEN = 1024

CHUNK = 64
RET_HEADS = 4
RET_DK = 128
RET_DV = 128
RET_WIDTH = RET_HEADS * RET_DV
ATT_HEADS = 8
ATT_KV_HEADS = 2
ATT_HD = 64
ATT_REP = ATT_HEADS // ATT_KV_HEADS
ATT_WIDTH = ATT_HEADS * ATT_HD
WINDOW = 128
BAND_CHUNKS = WINDOW // CHUNK
MIX_WIDTH = RET_WIDTH + ATT_WIDTH
D_FF = 2816
CONV_W = 3
EPS = 1e-6
IN_SIZES = (RET_HEADS * RET_DK, RET_HEADS * RET_DK, RET_WIDTH, RET_WIDTH,
            ATT_WIDTH, ATT_KV_HEADS * ATT_HD, ATT_KV_HEADS * ATT_HD)
IN_WIDTH = sum(IN_SIZES)

kernel_name = 'hymba_retention_swa_convffn_stream_step'

def rmsnorm(x, g):
    xf = x.astype(jnp.float32)
    y = xf * lax.rsqrt(jnp.mean(xf * xf, axis=-1, keepdims=True) + EPS)
    return (y * g.astype(jnp.float32)).astype(x.dtype)

def modulate(h, shift, scale):
    return h * (1 + scale[:, None, :]) + shift[:, None, :]

def split_in(proj):
    idx = np.cumsum(IN_SIZES)[:-1].tolist()
    return jnp.split(proj, idx, axis=-1)

def ret_log_gamma():
    return jnp.log1p(-jnp.exp2(-5.0 - jnp.arange(RET_HEADS, dtype=jnp.float32)))

def retention_block(q, k, v, state):
    L = q.shape[1]
    lg = ret_log_gamma()
    i = jnp.arange(L, dtype=jnp.float32)
    diff = i[:, None] - i[None, :]
    decay = jnp.where(diff >= 0, jnp.exp(lg[:, None, None] * jnp.maximum(diff, 0.0)), 0.0)
    scores = jnp.einsum('blhd,bmhd->bhlm', q, k) * decay[None]
    intra = jnp.einsum('bhlm,bmhe->blhe', scores, v)
    q_decay = jnp.exp(lg[None, :] * (i[:, None] + 1.0))
    cross = jnp.einsum('blhd,bhde->blhe', q, state) * q_decay[None, :, :, None]
    k_decay = jnp.exp(lg[None, :] * (L - 1.0 - i[:, None]))
    new_state = (state * jnp.exp(lg * L)[None, :, None, None]
                 + jnp.einsum('blhd,blhe->bhde', k * k_decay[None, :, :, None], v))
    return intra + cross, new_state

def retention_qkv(rq, rk, rv):
    B, L = rq.shape[:2]
    q = rq.reshape(B, L, RET_HEADS, RET_DK).astype(jnp.float32)
    k = rk.reshape(B, L, RET_HEADS, RET_DK).astype(jnp.float32) * (RET_DK ** -0.5)
    v = rv.reshape(B, L, RET_HEADS, RET_DV).astype(jnp.float32)
    return q, k, v

def retention_out(o, rg):
    B, L = o.shape[:2]
    o = o * lax.rsqrt(jnp.mean(o * o, axis=-1, keepdims=True) + EPS)
    return (jax.nn.silu(rg.astype(jnp.float32)) * o.reshape(B, L, RET_WIDTH)).astype(rg.dtype)

def retention_prompt(rq, rk, rv, rg):
    B, S = rq.shape[:2]
    nc = S // CHUNK
    q, k, v = retention_qkv(rq, rk, rv)

    def to_chunks(t):
        return t.reshape(B, nc, CHUNK, *t.shape[2:]).swapaxes(0, 1)

    def step(state, blk):
        out, state = retention_block(blk[0], blk[1], blk[2], state)
        return state, out

    state0 = jnp.zeros((B, RET_HEADS, RET_DK, RET_DV), jnp.float32)
    state, outs = lax.scan(step, state0, (to_chunks(q), to_chunks(k), to_chunks(v)))
    o = outs.swapaxes(0, 1).reshape(B, S, RET_HEADS, RET_DV)
    return retention_out(o, rg), state

def retention_sample(rq, rk, rv, rg, state):
    q, k, v = retention_qkv(rq, rk, rv)
    o, new_state = retention_block(q, k, v, state.astype(jnp.float32))
    return retention_out(o, rg), new_state

def alibi_slopes():
    h = jnp.arange(1, ATT_HEADS + 1, dtype=jnp.float32)
    return jnp.exp2(-8.0 * h / ATT_HEADS)

def band_attention(q, k, v, sinks, q_pos, k_pos, k_valid):
    s = jnp.einsum('bnqgrd,bnkgd->bngrqk', q, k).astype(jnp.float32) * (ATT_HD ** -0.5)
    dist = jnp.abs(q_pos[:, :, None] - k_pos[:, None, :]).astype(jnp.float32)
    slopes = alibi_slopes().reshape(ATT_KV_HEADS, ATT_REP)
    s = s - slopes[None, None, :, :, None, None] * dist[None, :, None, None, :, :]
    s = jnp.where(k_valid[None, :, None, None, None, :], s, -jnp.inf)
    sink = sinks.astype(jnp.float32).reshape(ATT_KV_HEADS, ATT_REP)[None, None, :, :, None, None]
    m = jnp.maximum(jnp.max(s, axis=-1, keepdims=True), sink)
    p = jnp.exp(s - m)
    p = p / (jnp.sum(p, axis=-1, keepdims=True) + jnp.exp(sink - m))
    return jnp.einsum('bngrqk,bnkgd->bnqgrd', p.astype(v.dtype), v)

def band_view(t, nc):
    B = t.shape[0]
    tp = jnp.pad(t, ((0, 0), (BAND_CHUNKS * CHUNK, 0), (0, 0), (0, 0)))
    tc = tp.reshape(B, nc + BAND_CHUNKS, CHUNK, ATT_KV_HEADS, ATT_HD)
    return jnp.concatenate([tc[:, j:j + nc] for j in range(BAND_CHUNKS + 1)], axis=2)

def attention_prompt(aq, ak, av, sinks):
    B, S = aq.shape[:2]
    nc = S // CHUNK
    q = aq.reshape(B, nc, CHUNK, ATT_KV_HEADS, ATT_REP, ATT_HD)
    k = ak.reshape(B, S, ATT_KV_HEADS, ATT_HD)
    v = av.reshape(B, S, ATT_KV_HEADS, ATT_HD)
    q_pos = jnp.arange(S).reshape(nc, CHUNK)
    k_pos = ((jnp.arange(nc)[:, None] - BAND_CHUNKS) * CHUNK
             + jnp.arange((BAND_CHUNKS + 1) * CHUNK)[None, :])
    o = band_attention(q, band_view(k, nc), band_view(v, nc), sinks, q_pos, k_pos, k_pos >= 0)
    w = min(WINDOW, S)
    return o.reshape(B, S, ATT_WIDTH), k[:, S - w:], v[:, S - w:]

def attention_sample(aq, ak, av, sinks, cache_k, cache_v):
    B, L = aq.shape[:2]
    wc = cache_k.shape[1]
    q = aq.reshape(B, 1, L, ATT_KV_HEADS, ATT_REP, ATT_HD)
    k = ak.reshape(B, L, ATT_KV_HEADS, ATT_HD)
    v = av.reshape(B, L, ATT_KV_HEADS, ATT_HD)
    kk = jnp.concatenate([cache_k.astype(k.dtype), k], axis=1)[:, None]
    vv = jnp.concatenate([cache_v.astype(v.dtype), v], axis=1)[:, None]
    q_pos = (PAST_LEN + jnp.arange(L))[None, :]
    k_pos = (PAST_LEN - wc + jnp.arange(wc + L))[None, :]
    o = band_attention(q, kk, vv, sinks, q_pos, k_pos, k_pos >= 0)
    return o.reshape(B, L, ATT_WIDTH), k, v

def conv_ffn(h, w_up, conv_w, conv_b, w_down, conv_state):
    L = h.shape[1]
    a, b = jnp.split(h @ w_up, 2, axis=-1)
    ext = jnp.concatenate([conv_state.astype(a.dtype), a], axis=1)
    conv = conv_b[None, None, :] + sum(ext[:, j:j + L] * conv_w[j] for j in range(CONV_W))
    y = (jax.nn.silu(conv) * b) @ w_down
    return y, ext[:, L:]

def trunk_layer(x, c, ln1, ln2, w_ada, b_ada, w_in, w_out, sinks, w_up, conv_w, conv_b, w_down,
                cache_k=None, cache_v=None, ret_state=None, conv_state=None):
    is_prompt = cache_k is None
    B = x.shape[0]
    mod = jax.nn.silu(c) @ w_ada + b_ada
    sh1, sc1, g1, sh2, sc2, g2 = jnp.split(mod, 6, axis=-1)
    h = modulate(rmsnorm(x, ln1), sh1, sc1)
    rq, rk, rv, rg, aq, ak, av = split_in(h @ w_in)
    if is_prompt:
        ret_o, ret_new = retention_prompt(rq, rk, rv, rg)
        att_o, k_rows, v_rows = attention_prompt(aq, ak, av, sinks)
        conv_state = jnp.zeros((B, CONV_W - 1, D_FF), x.dtype)
    else:
        ret_o, ret_new = retention_sample(rq, rk, rv, rg, ret_state)
        att_o, k_rows, v_rows = attention_sample(aq, ak, av, sinks, cache_k, cache_v)
    mix = jnp.concatenate([ret_o, att_o], axis=-1) @ w_out
    x = x + g1[:, None, :] * mix
    h2 = modulate(rmsnorm(x, ln2), sh2, sc2)
    ffn, conv_new = conv_ffn(h2, w_up, conv_w, conv_b, w_down, conv_state)
    x = x + g2[:, None, :] * ffn
    return x, ret_new.astype(x.dtype), k_rows, v_rows, conv_new

def setup_inputs(seed: int = 0) -> dict:
    key = jax.random.key(seed)
    ks = jax.random.split(key, 24)
    f32 = jnp.float32

    def nrm(k, shape, s):
        return jax.random.normal(k, shape, f32) * s

    wc = min(WINDOW, PAST_LEN)
    return {
        'x_prompt': nrm(ks[0], (BATCH, SEQ, D_MODEL), 1.0),
        'x_sample': nrm(ks[1], (DEC_BATCH, DEC_SEQ, D_MODEL), 1.0),
        'cache_k': nrm(ks[2], (DEPTH, DEC_BATCH, wc, ATT_KV_HEADS, ATT_HD), 1.0),
        'cache_v': nrm(ks[3], (DEPTH, DEC_BATCH, wc, ATT_KV_HEADS, ATT_HD), 1.0),
        'state_ret': nrm(ks[4], (DEPTH, DEC_BATCH, RET_HEADS, RET_DK, RET_DV), 0.5),
        'state_conv': nrm(ks[5], (DEPTH, DEC_BATCH, CONV_W - 1, D_FF), 1.0),
        'c_prompt': nrm(ks[6], (BATCH, D_MODEL), 1.0),
        'c_sample': nrm(ks[7], (DEC_BATCH, D_MODEL), 1.0),
        'norm1_g': 1.0 + nrm(ks[8], (DEPTH, D_MODEL), 0.05),
        'norm2_g': 1.0 + nrm(ks[9], (DEPTH, D_MODEL), 0.05),
        'w_ada': nrm(ks[10], (DEPTH, D_MODEL, 6 * D_MODEL), 0.5 * D_MODEL ** -0.5),
        'b_ada': nrm(ks[11], (DEPTH, 6 * D_MODEL), 0.01),
        'w_in': nrm(ks[12], (DEPTH, D_MODEL, IN_WIDTH), D_MODEL ** -0.5),
        'w_out': nrm(ks[13], (DEPTH, MIX_WIDTH, D_MODEL), MIX_WIDTH ** -0.5),
        'attn_sinks': nrm(ks[14], (DEPTH, ATT_HEADS), 0.5),
        'w_up': nrm(ks[15], (DEPTH, D_MODEL, 2 * D_FF), D_MODEL ** -0.5),
        'conv_w': nrm(ks[16], (DEPTH, CONV_W, D_FF), CONV_W ** -0.5),
        'conv_b': nrm(ks[17], (DEPTH, D_FF), 0.01),
        'w_down': nrm(ks[18], (DEPTH, D_FF, D_MODEL), D_FF ** -0.5),
        'normf_g': 1.0 + nrm(ks[19], (D_MODEL,), 0.05),
        'w_ada_f': nrm(ks[20], (D_MODEL, 2 * D_MODEL), 0.5 * D_MODEL ** -0.5),
        'b_ada_f': nrm(ks[21], (2 * D_MODEL,), 0.01),
    }

def reference(x_prompt, x_sample, cache_k, cache_v, state_ret, state_conv, c_prompt, c_sample,
              norm1_g, norm2_g, w_ada, b_ada, w_in, w_out, attn_sinks, w_up, conv_w, conv_b,
              w_down, normf_g, w_ada_f, b_ada_f):
    yp, ys = x_prompt, x_sample
    p_ret, p_k, p_v, p_conv = [], [], [], []
    s_ret, s_k, s_v, s_conv = [], [], [], []
    for l in range(DEPTH):
        yp, r, kr, vr, cv = trunk_layer(yp, c_prompt, norm1_g[l], norm2_g[l], w_ada[l], b_ada[l],
                                        w_in[l], w_out[l], attn_sinks[l], w_up[l], conv_w[l],
                                        conv_b[l], w_down[l])
        p_ret.append(r); p_k.append(kr); p_v.append(vr); p_conv.append(cv)
        ys, r, kr, vr, cv = trunk_layer(ys, c_sample, norm1_g[l], norm2_g[l], w_ada[l], b_ada[l],
                                        w_in[l], w_out[l], attn_sinks[l], w_up[l], conv_w[l],
                                        conv_b[l], w_down[l], cache_k=cache_k[l], cache_v=cache_v[l],
                                        ret_state=state_ret[l], conv_state=state_conv[l])
        s_ret.append(r); s_k.append(kr); s_v.append(vr); s_conv.append(cv)
    shp, scp = jnp.split(jax.nn.silu(c_prompt) @ w_ada_f + b_ada_f, 2, axis=-1)
    shs, scs = jnp.split(jax.nn.silu(c_sample) @ w_ada_f + b_ada_f, 2, axis=-1)
    y_prompt = modulate(rmsnorm(yp, normf_g), shp, scp)
    y_sample = modulate(rmsnorm(ys, normf_g), shs, scs)
    p_state_ret = jnp.stack(p_ret)
    p_k_rows = jnp.stack(p_k)
    p_v_rows = jnp.stack(p_v)
    p_state_conv = jnp.stack(p_conv)
    s_state_ret = jnp.stack(s_ret)
    s_k_rows = jnp.stack(s_k)
    s_v_rows = jnp.stack(s_v)
    s_state_conv = jnp.stack(s_conv)
    return (y_prompt, y_sample, p_state_ret, p_k_rows, p_v_rows, p_state_conv,
            s_state_ret, s_k_rows, s_v_rows, s_state_conv)


_drawn_inputs = setup_inputs


def setup_inputs(seed=0):
    import zlib

    import numpy as np

    out = dict(_drawn_inputs(seed))
    spreads = {}
    factors = {'cache_k': 5.374,
     'cache_v': 4.475,
     'attn_sinks': 8.0,
     'conv_b': 32.133,
     'b_ada_f': 4.144,
     'state_conv': 3.164}
    for name, (base, spread) in spreads.items():
        noise = np.random.default_rng([zlib.crc32(name.encode()), seed]).standard_normal(out[name].shape)
        drawn = base * np.exp(spread * noise) if base else spread * noise
        out[name] = jnp.asarray(drawn.astype(out[name].dtype))
    for name, factor in factors.items():
        out[name] = (out[name] * factor).astype(out[name].dtype)
    return out
```

```python
from contextlib import ExitStack

import numpy as np

import concourse.bass as bass
from concourse import mybir

ALU = mybir.AluOpType
ACT = mybir.ActivationFunctionType
F32 = mybir.dt.float32
F32R = mybir.dt.float32r
BF16 = mybir.dt.bfloat16

P = 128
D = 1024
KT = D // P
S_PROMPT = 1024
S_SAMPLE = 64
T = S_PROMPT + S_SAMPLE
CHUNKS = [(0, 364), (364, 362), (726, 362)]
C2P = S_PROMPT - CHUNKS[2][0]
NB = 9
BLOCKS = [(P * b, P) for b in range(8)] + [(S_PROMPT, S_SAMPLE)]
HEADS = 4
D_FF = 2816
FT = D_FF // P
EPS = 1e-6
RET_SCALE = float(np.float32(128 ** -0.5))
ATT_SCALE = 64 ** -0.5
MASKED = -1e30

N_PRO, N_HEAD, N_OUT = 3, 5, 8
HEAD_SLOTS = [0, 1, 2, 0, 1]
UNIT_OUT = N_PRO + N_HEAD * HEADS - 1
UNIT_FFN = UNIT_OUT + N_OUT
GROUPS = FT // 2
N_UNITS = UNIT_FFN + 3 * FT
SLOTS = [2, 0, 1] + HEAD_SLOTS * 3 + HEAD_SLOTS[:4] + [1, 2] * 4 + [1, 2, 0, 1] + [2, 0, 1] * 20 + [2, 0]
assert len(SLOTS) == N_UNITS

RT_DECAY, RT_Q, RT_K, RT_COLS = 0, 128, 256, 260
N_MOD = 64


def unit_gap(units):
    gaps = []
    for n in units:
        before = [m for m in range(n) if SLOTS[m] == SLOTS[n]]
        if before:
            gaps.append(n - before[-1])
        else:
            return None
    return min(gaps)


def unit_loads(units, i):
    counts = [SLOTS[:n + 1].count(SLOTS[n]) for n in units]
    if len(counts) == 1:
        return counts[0]
    per = counts[1] - counts[0]
    assert counts == [counts[0] + per * k for k in range(len(counts))]
    return counts[0] + per * i


def hymba_step(nc, x_t, w_units, w_ada, b_ada, cond, gains, conv_wb, conv_st, sinks, ck_t, cv_in, st_in,
               ident_in, att_bias, ret_tab, y_t, p_state, pk_t, pv, p_conv, s_state, sk_t, sv):
    x_v = x_t.rearrange("(k p) t -> p k t", p=P)
    y_v = y_t.rearrange("(k p) t -> p k t", p=P)

    with ExitStack() as ctx:
        def sb(name, shape, dt=F32, at=ctx):
            return at.enter_context(nc.sbuf_tensor(name, shape, dt))

        def sem(name):
            return ctx.enter_context(nc.semaphore(name))

        act_hl = sb("act_hl", [P, 2, KT, T], F32R)
        w_hl = sb("w_hl", [P, 3, 2, KT, P], F32R)
        xm = sb("xm", [P, KT, T])
        w_raw = sb("w_raw", [P, 3, KT, P])
        ident = sb("ident", [P, P])
        ones = sb("ones", [P, P])
        sq = sb("sq", [P, 2, CHUNKS[0][1]])
        acc = sb("acc", [P, T])
        hf = sb("hf", [P, 2, CHUNKS[0][1]])
        std = sb("std", [P, 3, CHUNKS[0][1]])
        mod = sb("mod", [P, N_MOD, 2])
        mod_part = sb("mod_part", [P, 8, 2])
        scale_n = sb("scale_n", [P, 3, KT, 2])
        b_ada_sb = sb("b_ada_sb", [P, N_MOD])
        gains_sb = sb("gains_sb", [P, 3, KT])
        conv_wb_sb = sb("conv_wb_sb", [P, FT, 4])
        conv_st_sb = sb("conv_st_sb", [P, FT, 2])
        conv_out = sb("conv_out", [P, FT, 4])
        eps_sb = sb("eps_sb", [P, 1])

        ada_w = sb("ada_w", [P, 2, D])
        ada_out = sb("ada_out", [P, 2, D], BF16)
        silu_c = sb("silu_c", [P, 2, D])

        heads_phase = ExitStack()
        rq = sb("rq", [P, T], at=heads_phase)
        rk = sb("rk", [P, T], at=heads_phase)
        rv = sb("rv", [P, T], at=heads_phase)
        rg = sb("rg", [P, T], at=heads_phase)
        aq = sb("aq", [P, T], at=heads_phase)
        ak = sb("ak", [P, T + P], at=heads_phase)
        av_tok = sb("av_tok", [P, NB + 1, P], at=heads_phase)
        att_tab = sb("att_tab", [P, 2, 256], at=heads_phase)
        sink_sb = sb("sink_sb", [P, 2], at=heads_phase)
        rtab = sb("rtab", [P, RT_COLS], at=heads_phase)
        prob = sb("prob", [P, 2, 2, 256], at=heads_phase)
        prob_t = sb("prob_t", [P, 2, 2, 2, P], at=heads_phase)
        soft = sb("soft", [P, 2, 5, 2], at=heads_phase)
        rden = sb("rden", [P, 2, 2], at=heads_phase)
        k_tok = sb("k_tok", [P, 2, P], at=heads_phase)
        v_tok = sb("v_tok", [P, 2, P], at=heads_phase)
        s_dec = sb("s_dec", [P, 2, P], at=heads_phase)
        state = sb("state", [P, P], at=heads_phase)
        state_in = sb("state_in", [P, P], at=heads_phase)
        state_new = sb("state_new", [P, P], at=heads_phase)
        heads_phase.close()
        u_hl = sb("u_hl", [P, 2, 2, 2, T], F32R)
        gate_ext = sb("gate_ext", [P, T + 4])
        conv = sb("conv", [P, T + 2])

        bank = [ctx.enter_context(nc.psum_tensor(f"bank{i}", [P, 512], F32)) for i in range(8)]
        SUM_BANK = [7, 3, 6]

        const_loaded = sem("const_loaded")
        cond_loaded = sem("cond_loaded")
        x_loaded = [sem(f"x_loaded{c}") for c in range(3)]
        ada_loaded = [sem(f"ada_loaded{r}") for r in range(2)]
        w_loaded = [sem(f"w_loaded{slot}") for slot in range(3)]
        att_tab_loaded = sem("att_tab_loaded")
        ret_tab_loaded = sem("ret_tab_loaded")
        cache_loaded = sem("cache_loaded")
        stored = sem("stored")
        state_stored = sem("state_stored")
        silu_c_ready = sem("silu_c_ready")
        pool_const = sem("pool_const")
        dve_seq = sem("dve_seq")
        ada_used = sem("ada_used")
        mod_ready = sem("mod_ready")
        sq_ready = sem("sq_ready")
        sq_used = sem("sq_used")
        acc_ready = sem("acc_ready")
        sum_ready = sem("sum_ready")
        std_ready = sem("std_ready")
        norm_applied = sem("norm_applied")
        hf_ready = sem("hf_ready")
        hi_ready = sem("hi_ready")
        lo_ready = sem("lo_ready")
        wh_ready = sem("wh_ready")
        wl_ready = sem("wl_ready")
        unit_done = sem("unit_done")
        gemm_ready = sem("gemm_ready")
        act_evac = sem("act_evac")
        dve_evac = sem("dve_evac")
        av_t_ready = sem("av_t_ready")
        av_tok_ready = sem("av_tok_ready")
        qk_ready = sem("qk_ready")
        masked_ready = sem("masked_ready")
        exp_ready = sem("exp_ready")
        prob_ready = sem("prob_ready")
        pt_ready = sem("pt_ready")
        pt_copied = sem("pt_copied")
        pv_ready = sem("pv_ready")
        pv_copied = sem("pv_copied")
        qdec_ready = sem("qdec_ready")
        ret_a_ready = sem("ret_a_ready")
        ret_a_used = sem("ret_a_used")
        ret_b_ready = sem("ret_b_ready")
        ret_o_copied = sem("ret_o_copied")
        state_ready = sem("state_ready")
        ret_sq_ready = sem("ret_sq_ready")
        mix_hi_ready = sem("mix_hi_ready")
        mix_lo_ready = sem("mix_lo_ready")
        ext_ready = sem("ext_ready")
        conv_ready = sem("conv_ready")
        silu_ready = sem("silu_ready")
        uf_ready = sem("uf_ready")
        u_hi_ready = sem("u_hi_ready")
        u_lo_ready = sem("u_lo_ready")
        down_ready = sem("down_ready")
        down_free = sem("down_free")
        y_ready = sem("y_ready")
        waits_passed = sem("waits_passed")

        def head_unit(j, p):
            return N_PRO + N_HEAD * j + p

        def seal_waits(eng):
            eng.sem_inc(waits_passed, 1)

        def keys_of(b):
            if b == 0:
                return [(0, P, P, 0)]
            if b == NB - 1:
                return [(S_PROMPT, P, 0, 8), (S_PROMPT + P, S_SAMPLE, P, 9)]
            return [(P * (b - 1), P, 0, b - 1), (P * b, P, P, b)]

        def pieces(c):
            a, n = CHUNKS[c]
            if c < 2:
                return [(0, a, n, 0)]
            return [(0, a, C2P, 0), (C2P, S_PROMPT, S_SAMPLE, 1)]

        FFN_BODY = [("up", 0), ("up", 1), ("up", 2), ("up", 3), ("down", 0), ("down", 1)]

        block = ctx.enter_context(nc.Block())

        @block.sync
        def _(sp):
            def load_unit(n, like):
                gap = unit_gap(like)
                if gap is not None:
                    sp.wait_ge(wl_ready, n - gap + 1)
                slot = SLOTS[like[0]]
                sp.dma_start(w_raw[:, slot], w_units[n].rearrange("p (k m) -> p k m", k=KT)).then_inc(w_loaded[slot], 16)

            def load_ada(m, ring):
                sp.wait_ge(ada_used, 2 * (m - 2) + 2)
                sp.dma_start(ada_w[:, ring], w_ada[m]).then_inc(ada_loaded[ring], 16)

            def load_x(c):
                a, n = CHUNKS[c]
                sp.dma_start(xm[:, :, a:a + n], x_v[:, :, a:a + n]).then_inc(x_loaded[c], 16)

            def load_head_tables(j):
                if not isinstance(j, int) or j > 0:
                    sp.wait_ge(prob_ready, NB * j)
                sp.dma_start(att_tab[:, :, :], att_bias[j].rearrange("p (g k) -> p g k", g=2)).then_inc(att_tab_loaded, 16)
                sp.dma_start(sink_sb[:, :], sinks[j].partition_broadcast(P)).then_inc(att_tab_loaded, 16)

            def load_ret_tables(j):
                if not isinstance(j, int) or j > 0:
                    sp.wait_ge(state_ready, NB * j)
                sp.dma_start(rtab[:, :], ret_tab[j]).then_inc(ret_tab_loaded, 16)
                sp.dma_start(state_in[:, :], st_in[j]).then_inc(ret_tab_loaded, 16)

            sp.dma_start(silu_c[:, :, :], cond.partition_broadcast(P)).then_inc(cond_loaded, 16)
            for dst, src in ((ident, ident_in), (b_ada_sb, b_ada), (gains_sb, gains), (conv_wb_sb, conv_wb),
                             (conv_st_sb, conv_st)):
                sp.dma_start(dst[:], src).then_inc(const_loaded, 16)
            for m in range(2):
                sp.dma_start(ada_w[:, m], w_ada[m]).then_inc(ada_loaded[m], 16)
            load_x(0)
            load_unit(0, [0])
            load_x(1)
            load_x(2)
            load_unit(1, [1])
            sp.dma_start(ak[:, S_PROMPT:S_PROMPT + P], ck_t).then_inc(cache_loaded, 16)
            sp.dma_start(av_tok[:, 8, :], cv_in).then_inc(cache_loaded, 16)
            for m in range(2, 16):
                load_ada(m, m % 2)
            load_unit(2, [2])
            load_head_tables(0)
            load_ret_tables(0)
            load_unit(3, [3])
            load_unit(4, [4])

            def head_in_loop(j):
                for p in range(N_HEAD):
                    load_unit(head_unit(j, p) + 2, [head_unit(i, p) + 2 for i in range(HEADS - 1)])
                    for t in range(2) if p < 4 else ():
                        load_ada(16 + 8 * j + 2 * p + t, t)
                load_head_tables(j + 1)
                load_ret_tables(j + 1)

            with sp.Fori(0, HEADS - 1) as j:
                head_in_loop(j)
            j = HEADS - 1
            for p in range(N_HEAD - 1):
                load_unit(head_unit(j, p) + 2, [head_unit(j, p) + 2])
                for t in range(2):
                    load_ada(16 + 8 * j + 2 * p + t, t)

            sp.wait_ge(mix_lo_ready, 3 * KT)
            for c in range(3):
                load_x(c)
            with sp.Fori(0, N_OUT // 2 - 1) as i:
                for t in range(2):
                    load_unit(UNIT_OUT + 2 * i + t + 2, [UNIT_OUT + 2 * k + t + 2 for k in range(N_OUT // 2 - 1)])
                for t in range(4):
                    load_ada(48 + 4 * i + t, t % 2)
            for t in range(2):
                n = UNIT_FFN - 2 + t
                load_unit(n + 2, [n + 2])
            for t in range(4):
                load_ada(60 + t, t % 2)
            for p in range(4):
                load_unit(UNIT_FFN + p + 2, [UNIT_FFN + p + 2])
            with sp.Fori(0, (GROUPS - 1) // 2) as i:
                for p in range(12):
                    at = UNIT_FFN + 4 + p + 2
                    load_unit(at + 12 * i, [at + 12 * k for k in range((GROUPS - 1) // 2)])
            sp.wait_ge(ext_ready, 2 * FT)
            sp.dma_start(p_conv, conv_out[:, :, :]).then_inc(stored, 16)
            for c in range(3):
                a, n = CHUNKS[c]
                sp.wait_ge(y_ready, KT * (c + 1))
                sp.dma_start(y_v[:, :, a:a + n], xm[:, :, a:a + n]).then_inc(stored, 16)
            sp.wait_ge(stored, 16 * 8)
            sp.wait_ge(state_stored, 32 * HEADS + 32)

        @block.scalar
        def _(act):
            def split_weights(n, like, i=0):
                act.wait_ge(w_loaded[SLOTS[like[0]]], 16 * unit_loads(like, i))
                gap = unit_gap(like)
                if gap is not None:
                    act.wait_ge(unit_done, n - gap + 1)
                slot = SLOTS[like[0]]
                act.activation(w_hl[:, slot, 0], w_raw[:, slot], ACT.Copy).then_inc(wh_ready, 1)

            def square(src, item, ring):
                n = src.shape[-1]
                if not isinstance(item, int) or item >= 2:
                    act.wait_ge(sq_used, item - 1)
                act.activation(sq[:, ring, 0:n], src, ACT.Square).then_inc(sq_ready, 1)

            def root(q, c, width, at=None):
                n = CHUNKS[c][1]
                act.wait_ge(sum_ready, q + 1)
                if not isinstance(q, int) or q >= 3:
                    act.wait_ge(norm_applied, q - 2)
                act.activation(std[:, c, 0:n], bank[SUM_BANK[c] if at is None else at][:, 0:n], ACT.Sqrt, bias=eps_sb[:, 0:1],
                               scale=1.0 / width).then_inc(std_ready, 1)

            def split_hf(item, c, k):
                a, n = CHUNKS[c]
                act.wait_ge(hf_ready, item + 1)
                act.activation(act_hl[:, 0, k, a:a + n], hf[:, item % 2, 0:n], ACT.Copy).then_inc(hi_ready, 1)

            act.sem_inc(state_stored, 32)
            act.wait_ge(cond_loaded, 16)
            act.activation(silu_c[:, :, :], silu_c[:, :, :], ACT.Silu).then_inc(silu_c_ready, 1)
            for c in range(3):
                a, n = CHUNKS[c]
                act.wait_ge(x_loaded[c], 16)
                for k in range(KT):
                    square(xm[:, k, a:a + n], KT * c + k, k % 2)
            split_weights(0, [0])
            split_weights(1, [1])
            act.wait_ge(pool_const, 2)
            for c in range(3):
                root(c, c, D)
            for c in range(3):
                for k in range(KT):
                    split_hf(KT * c + k, c, k)

            def evac(n_chunk, c, dst, func=ACT.Copy, scale=1.0):
                a, n = CHUNKS[c]
                act.wait_ge(gemm_ready, n_chunk + 1)
                act.activation(dst[:, a:a + n], bank[c][:, 0:n], func, scale=scale).then_inc(act_evac, 1)

            for c in range(3):
                act.wait_ge(gemm_ready, c + 1)
                for o, t, n, part in pieces(c):
                    ins = act.activation(ak[:, t + P * part:t + P * part + n], bank[c][:, o:o + n], ACT.Copy)
                ins.then_inc(act_evac, 1)
            act.wait_ge(act_evac, 3)
            act.dma_start(pk_t, ak[:, S_PROMPT - P:S_PROMPT]).then_inc(stored, 16)
            act.dma_start(sk_t, ak[:, T + P - S_SAMPLE:T + P]).then_inc(stored, 16)
            split_weights(2, [2])
            for c in range(3):
                evac(3 + c, c, rv)
            split_weights(3, [3])
            for c in range(3):
                evac(6 + c, c, aq, scale=ATT_SCALE)
            split_weights(4, [4])
            act.wait_ge(av_tok_ready, NB)
            act.dma_start(pv, av_tok[:, 7, :]).then_inc(stored, 16)
            act.dma_start(sv, av_tok[0:S_SAMPLE, 9, :]).then_inc(stored, 16)

            def exps(j, b):
                qn, kn, r = BLOCKS[b][1], sum(k[1] for k in keys_of(b)), b % 2
                act.wait_ge(masked_ready, NB * j + b + 1)
                for g in range(2):
                    act.activation(prob[0:qn, r, g, 0:kn], prob[0:qn, r, g, 0:kn], ACT.Exp,
                                   bias=soft[0:qn, r, 1, g:g + 1], accum_out=soft[0:qn, r, 3, g:g + 1])
                act.activation(soft[0:qn, r, 4, :], soft[0:qn, r, 2, :], ACT.Exp).then_inc(exp_ready, 1)

            def copy_prob_t(j, b):
                qn, r, kb = BLOCKS[b][1], b % 2, keys_of(b)
                act.wait_ge(pt_ready, NB * j + b + 1)
                src = bank[5][:, :].rearrange("p (g k q) -> p g k q", g=2, k=2)
                if b < NB - 1:
                    ins = act.activation(prob_t[:, r, :, 0:len(kb), :], src[:, :, 0:len(kb), :], ACT.Copy)
                else:
                    for i, k in enumerate(kb):
                        ins = act.activation(prob_t[0:k[1], r, :, i, 0:qn], src[0:k[1], :, i, 0:qn], ACT.Copy)
                ins.then_inc(pt_copied, 1)

            def copy_att_out(j, b):
                t, n = BLOCKS[b]
                act.wait_ge(pv_ready, NB * j + b + 1)
                act.activation(xm[:, 4 + j, t:t + n], bank[6][:, 0:n], ACT.Copy).then_inc(pv_copied, 1)

            def copy_ret_out(j, b):
                t, n = BLOCKS[b]
                act.wait_ge(ret_b_ready, NB * j + b + 1)
                act.activation(xm[:, j, t:t + n], bank[6][:, 0:n], ACT.Copy).then_inc(ret_o_copied, 1)

            def head(j, last):
                n_units = N_HEAD - last
                dst = [(rq, ACT.Copy, 1.0), (rk, ACT.Copy, RET_SCALE), (rv, ACT.Copy, 1.0), (rg, ACT.Silu, 1.0),
                       (aq, ACT.Copy, ATT_SCALE)]
                for p in range(n_units):
                    for c in range(3):
                        s = 3 * p + c
                        if 2 <= s <= NB + 1:
                            copy_att_out(j, s - 2)
                        if s < NB:
                            exps(j, s)
                        if 1 <= s <= NB:
                            copy_prob_t(j, s - 1)
                        for b in range(NB):
                            if RET_PE_STEP[last][b + 1] in (3 * s, 3 * s + 1):
                                copy_ret_out(j, b)
                        evac(3 * head_unit(j, p) + c, c, *dst[p])
                        for b in range(NB):
                            if RET_PE_STEP[last][b + 1] == 3 * s + 2:
                                copy_ret_out(j, b)
                    like = [head_unit(j, p) + 2] if last else [head_unit(i, p) + 2 for i in range(HEADS - 1)]
                    split_weights(head_unit(j, p) + 2, like, j)
                for b in range(NB):
                    if RET_PE_STEP[last][b + 1] >= 9 * n_units:
                        copy_ret_out(j, b)
                act.wait_ge(ret_o_copied, NB * j + NB)
                seal_waits(act)
                for c in range(3):
                    a, n = CHUNKS[c]
                    if c == 2:
                        act.wait_ge(sum_ready, 3 + 3 * j + 1)
                    act.activation(sq[:, c % 2, 0:n], xm[:, j, a:a + n], ACT.Square).then_inc(ret_sq_ready, 1)
                for c in range(3):
                    root(3 + 3 * j + c, c, P)
                act.wait_ge(state_ready, NB * j + NB)
                act.dma_start(p_state[j], state[:, :]).then_inc(state_stored, 16)
                act.dma_start(s_state[j], state_new[:, :]).then_inc(state_stored, 16)

            with act.Fori(0, HEADS - 1) as j:
                head(j, 0)
            head(HEADS - 1, 1)

            act.wait_ge(pv_copied, NB * HEADS)
            act.wait_ge(ret_o_copied, NB * HEADS)
            for c in range(3):
                a, n = CHUNKS[c]
                act.wait_ge(norm_applied, 3 + 3 * (HEADS - 1) + c + 1)
                for k in MIX_ORDER:
                    act.activation(act_hl[:, 0, k, a:a + n], xm[:, k, a:a + n], ACT.Copy).then_inc(mix_hi_ready, 1)

            def out_unit(o, p, like, i=0):
                for c in range(3):
                    a, n = CHUNKS[c]
                    act.wait_ge(dve_evac, 3 * o + c + 1)
                    square(xm[:, o, a:a + n], 3 * KT + 3 * o + c, (3 * p + c) % 2)
                split_weights(UNIT_OUT + o + 2, like, i)

            with act.Fori(0, N_OUT // 2 - 1) as i:
                for p in range(2):
                    out_unit(2 * i + p, p, [UNIT_OUT + 2 * k + p + 2 for k in range(N_OUT // 2 - 1)], i)
            for p in range(2):
                out_unit(N_OUT - 2 + p, p, [UNIT_FFN + p])
            for c in range(3):
                root(15 + c, c, D)
            for c in range(3):
                for k in range(KT):
                    split_hf(3 * KT + KT * c + k, c, k)

            def up_pair(f, t, par, unit, like, i=0):
                if not isinstance(f, int) or f > 0:
                    act.wait_ge(conv_ready, f)
                for c in range(3):
                    act.wait_ge(gemm_ready, 90 + 6 * f + c + 1)
                    for o, tok, n, part in pieces(c):
                        ins = act.activation(gate_ext[:, 2 + tok + 2 * part:2 + tok + 2 * part + n],
                                             bank[c][:, o:o + n], ACT.Copy)
                    ins.then_inc(act_evac, 1)
                act.activation(gate_ext[:, S_PROMPT + 2:S_PROMPT + 4], conv_st_sb[:, f, :], ACT.Copy).then_inc(ext_ready, 1)
                act.wait_ge(act_evac, 66 + 3 * f + 3)
                seal_waits(act)
                last_rows = gate_ext[:, T + 4 - 2 * 66:T + 4].rearrange("p (s r) -> p s r", s=2)[:, :, 64:66]
                act.activation(conv_out[:, f, :].rearrange("p (s r) -> p s r", s=2), last_rows,
                               ACT.Copy).then_inc(ext_ready, 1)
                split_weights(unit + 2, like[0], i)
                act.wait_ge(conv_ready, f + 1)
                act.activation(conv[:, :], conv[:, :], ACT.Silu).then_inc(silu_ready, 1)
                for c in range(3):
                    a, n = CHUNKS[c]
                    act.wait_ge(uf_ready, 3 * f + c + 1)
                    act.activation(u_hl[:, par, t, 0, a:a + n], hf[:, (3 * t + c) % 2, 0:n], ACT.Copy).then_inc(u_hi_ready, 1)
                split_weights(unit + 3, like[1], i)

            for t in range(2):
                n = UNIT_FFN + 2 * t
                up_pair(t, t, 0, n, ([n + 2], [n + 3]))
            with act.Fori(0, (GROUPS - 1) // 2) as i:
                reps = range((GROUPS - 1) // 2)
                for h in range(2):
                    at = UNIT_FFN + 4 + 6 * h
                    for t in range(2):
                        likes = [[at + 2 * t + q + 12 * k for k in reps] for q in (2, 3)]
                        up_pair(2 + 4 * i + 2 * h + t, t, 1 - h, at + 2 * t + 12 * i, likes, i)
                    for q in (6, 7):
                        split_weights(at + q + 12 * i, [at + q + 12 * k for k in reps], i)
            for c in range(3):
                for k in range(KT):
                    a, n = CHUNKS[c]
                    act.wait_ge(down_free, 4 + 24 * (GROUPS - 1) + KT * c + k + 1)
                    square(xm[:, k, a:a + n], 6 * KT + KT * c + k, k % 2)
                root(18 + c, c, D, (7, 0, 1)[c])

        @block.gpsimd
        def _(pool):
            def split_weights(n, like):
                slot = SLOTS[like[0]]
                pool.wait_ge(wh_ready, n + 1)
                pool.tensor_tensor(w_hl[:, slot, 1], w_raw[:, slot], w_hl[:, slot, 0].bitcast(F32),
                                   ALU.subtract).then_inc(wl_ready, 1)

            def add_square(item, ring, first, dst, done):
                pool.wait_ge(sq_ready, item + 1)
                src = sq[:, ring, 0:dst.shape[-1]]
                if first:
                    ins = pool.tensor_copy(dst, src)
                else:
                    ins = pool.tensor_tensor(dst, dst, src, ALU.add)
                ins.then_inc(sq_used, 1)

            def split_hf(item, c, k):
                a, n = CHUNKS[c]
                pool.wait_ge(hi_ready, item + 1)
                pool.tensor_tensor(act_hl[:, 1, k, a:a + n], hf[:, item % 2, 0:n],
                                   act_hl[:, 0, k, a:a + n].bitcast(F32), ALU.subtract).then_inc(lo_ready, 1)

            pool.memset(ones[:, :], 1.0).then_inc(pool_const, 1)
            pool.memset(eps_sb[:, :], EPS).then_inc(pool_const, 1)
            for c in range(3):
                a, n = CHUNKS[c]
                for k in range(KT):
                    if k > 0:
                        pool.wait_ge(sq_used, KT * c + k)
                    add_square(KT * c + k, k % 2, k == 0, acc[:, a:a + n], None)
            split_weights(0, [0])
            split_weights(1, [1])
            for c in range(3):
                for k in range(KT):
                    split_hf(KT * c + k, c, k)
            for n in (2, 3, 4):
                split_weights(n, [n])

            def decay_q(j):
                pool.wait_ge(act_evac, 3 * head_unit(j, 0) + 3)
                pool.wait_ge(ret_tab_loaded, 32 * (j + 1))
                dec = rtab[:, RT_Q:RT_Q + P]
                pool.tensor_tensor(acc[:, 0:S_PROMPT].rearrange("p (b l) -> p b l", b=8),
                                   rq[:, 0:S_PROMPT].rearrange("p (b l) -> p b l", b=8),
                                   dec.unsqueeze(1).broadcast_to([P, 8, P]), ALU.mult).then_inc(qdec_ready, 1)
                pool.tensor_tensor(acc[:, S_PROMPT:T], rq[:, S_PROMPT:T], dec[:, 0:S_SAMPLE],
                                   ALU.mult).then_inc(qdec_ready, 1)

            with pool.Fori(0, HEADS - 1) as j:
                for p in range(N_HEAD):
                    split_weights(head_unit(j, p) + 2, [head_unit(0, p) + 2])
                    if p == 0:
                        decay_q(j)
            for p in range(N_HEAD - 1):
                split_weights(head_unit(HEADS - 1, p) + 2, [head_unit(HEADS - 1, p) + 2])
                if p == 0:
                    decay_q(HEADS - 1)

            def out_unit(o, p, first, like):
                for c in range(3):
                    a, n = CHUNKS[c]
                    if not first:
                        pool.wait_ge(sq_used, 3 * KT + 3 * (o - 1) + c + 1)
                    add_square(3 * KT + 3 * o + c, (3 * p + c) % 2, first, acc[:, a:a + n], None)
                split_weights(UNIT_OUT + o + 2, like)

            for p in range(2):
                out_unit(p, p, p == 0, [UNIT_OUT + p + 2])
            with pool.Fori(0, N_OUT // 2 - 2) as i:
                for p in range(2):
                    out_unit(2 * i + 2 + p, p, False, [UNIT_OUT + 2 + p + 2])
            for p in range(2):
                out_unit(N_OUT - 2 + p, p, False, [UNIT_FFN + p])
            for c in range(3):
                for k in range(KT):
                    split_hf(3 * KT + KT * c + k, c, k)
            pool.memset(gate_ext[:, 0:2], 0.0).then_inc(pool_const, 1)

            def up_pair(f, t, par, unit, like):
                split_weights(unit + 2, like[0])
                for c in range(3):
                    a, n = CHUNKS[c]
                    pool.wait_ge(u_hi_ready, 3 * f + c + 1)
                    pool.tensor_tensor(u_hl[:, par, t, 1, a:a + n], hf[:, (3 * t + c) % 2, 0:n],
                                       u_hl[:, par, t, 0, a:a + n].bitcast(F32), ALU.subtract).then_inc(u_lo_ready, 1)
                split_weights(unit + 3, like[1])

            for t in range(2):
                n = UNIT_FFN + 2 * t
                up_pair(t, t, 0, n, ([n + 2], [n + 3]))
            with pool.Fori(0, (GROUPS - 1) // 2) as i:
                for h in range(2):
                    at = UNIT_FFN + 4 + 6 * h
                    for t in range(2):
                        up_pair(2 + 4 * i + 2 * h + t, t, 1 - h, at + 2 * t + 12 * i,
                                ([at + 2 * t + 2], [at + 2 * t + 3]))
                    for q in (6, 7):
                        split_weights(at + q + 12 * i, [at + q])
            for c in range(3):
                a, n = CHUNKS[c]
                for k in range(KT):
                    if k > 0:
                        pool.wait_ge(sq_used, 6 * KT + KT * c + k)
                    add_square(6 * KT + KT * c + k, k % 2, k == 0, acc[:, a:a + n], None)

        @block.vector
        def _(dve):
            seq = [0]

            def then_wait(ins):
                seq[0] += 1
                ins.then_inc(dve_seq, 1)
                dve.wait_ge(dve_seq, seq[0])

            def in_loop_wait(ins, base, per, j, local):
                ins.then_inc(dve_seq, 1)
                dve.wait_ge(dve_seq, base + per * j + local)

            def ada_dots(m, pair, ring, dst0, dst1):
                dve.wait_ge(ada_loaded[ring], 16 * pair)
                for s, dst in enumerate((dst0, dst1)):
                    if not isinstance(m, int) or m > 0:
                        dve.wait_ge(ada_used, 2 * m + s - 1)
                    if not isinstance(m, int):
                        seal_waits(dve)
                    dve.tensor_tensor_reduce(ada_out[:, s], ada_w[:, ring], silu_c[:, s], 1.0, 0.0,
                                             ALU.mult, ALU.add, dst).then_inc(ada_used, 1)

            def add_ada_bias(m0, n, used):
                dve.wait_ge(ada_used, 2 * used)
                return dve.tensor_tensor(mod[:, bass.ds(m0, n), :], mod_part[:, 0:n, :],
                                         b_ada_sb[:, bass.ds(m0, n)].unsqueeze(2).broadcast_to([P, n, 2]), ALU.add)

            def norm_scale(which, m0):
                return dve.scalar_tensor_tensor(scale_n[:, which], mod[:, m0:m0 + 16:2, :], 1.0,
                                                gains_sb[:, which].unsqueeze(2).broadcast_to([P, KT, 2]),
                                                ALU.add, ALU.mult)

            def modulate(q, item0, which, m0, store):
                for c in range(3):
                    a, n = CHUNKS[c]
                    dve.wait_ge(std_ready, q + c + 1)
                    then_wait(dve.reciprocal(std[:, c, 0:n], std[:, c, 0:n]))
                    for k in range(KT):
                        item = item0 + KT * c + k
                        if store:
                            dst, ready = xm[:, k, a:a + n], y_ready
                        else:
                            dst, ready = hf[:, item % 2, 0:n], hf_ready
                            if item >= 2:
                                dve.wait_ge(lo_ready, item - 1)
                        then_wait(dve.tensor_tensor(dst, xm[:, k, a:a + n], std[:, c, 0:n], ALU.mult))
                        for o, tok, m, part in pieces(c):
                            ins = dve.tensor_scalar(dst[:, o:o + m], dst[:, o:o + m], scale_n[:, which, k, part:part + 1],
                                                    mod[:, m0 + 2 * k + 1, part:part + 1], ALU.mult, ALU.add)
                        ins.then_inc(ready, 1)
                    dve.wait_ge(ready, item0 + KT * (c + 1) if not store else KT * (c + 1))
                    dve.sem_inc(norm_applied, 1)

            dve.wait_ge(silu_c_ready, 1)
            dve.wait_ge(const_loaded, 16 * 5)
            for h in range(2):
                for m in range(8 * h, 8 * h + 8):
                    ada_dots(m, m // 2 + 1, m % 2, mod_part[:, m - 8 * h, 0:1], mod_part[:, m - 8 * h, 1:2])
                then_wait(add_ada_bias(8 * h, 8, 8 * h + 8))
            then_wait(norm_scale(0, 0))
            modulate(0, 0, 0, 0, False)

            for b in range(NB):
                t, n = BLOCKS[b]
                dve.wait_ge(av_t_ready, b + 1)
                dve.tensor_copy(av_tok[0:n, b + (b == NB - 1), :], bank[(3, 6)[b % 2]][0:n, 0:P]).then_inc(av_tok_ready, 1)

            def mask_and_max(j, b):
                qn, kb, r = BLOCKS[b][1], keys_of(b), b % 2
                kn = sum(k[1] for k in kb)
                if b == 0:
                    dve.wait_ge(att_tab_loaded, 32 * (j + 1))
                if b >= 2:
                    dve.wait_ge(pt_ready, NB * j + b - 1)
                dve.wait_ge(qk_ready, NB * j + b + 1)
                seal_waits(dve)
                for g in range(2):
                    ins = dve.tensor_tensor_reduce(prob[0:qn, r, g, 0:kn], bank[3 + g][0:qn, 0:kn],
                                                   att_tab[0:qn, g, kb[0][2]:kb[0][2] + kn], 1.0, sink_sb[0:qn, g:g + 1],
                                                   ALU.add, ALU.max, soft[0:qn, r, 0, g:g + 1])
                chain(ins, j)
                dve.tensor_scalar(soft[0:qn, r, 1, :], soft[0:qn, r, 0, :], -1.0, None, ALU.mult)
                dve.tensor_tensor(soft[0:qn, r, 2, :], sink_sb[0:qn, :], soft[0:qn, r, 0, :],
                                  ALU.subtract).then_inc(masked_ready, 1)

            def normalise(j, b):
                qn, r = BLOCKS[b][1], b % 2
                kn = sum(k[1] for k in keys_of(b))
                dve.wait_ge(exp_ready, NB * j + b + 1)
                chain(dve.tensor_tensor(rden[0:qn, r, :], soft[0:qn, r, 3, :], soft[0:qn, r, 4, :], ALU.add), j)
                chain(dve.reciprocal(rden[0:qn, r, :], rden[0:qn, r, :]), j)
                for g in range(2):
                    ins = dve.tensor_scalar(prob[0:qn, r, g, 0:kn], prob[0:qn, r, g, 0:kn], rden[0:qn, r, g:g + 1],
                                            None, ALU.mult)
                ins.then_inc(prob_ready, 1)

            def take_block(j, b):
                n, r = BLOCKS[b][1], b % 2
                A = bank[3 + r]
                if b == 0:
                    dve.wait_ge(ret_tab_loaded, 32 * (j + 1))
                if b >= 2:
                    dve.wait_ge(ret_b_ready, NB * j + b - 1)
                dve.wait_ge(ret_a_ready, NB * j + b + 1)
                kd = RT_K + (b == NB - 1)
                dve.tensor_scalar(k_tok[0:n, r, :], A[0:n, 0:P], rtab[0:n, kd:kd + 1], None, ALU.mult)
                dve.tensor_copy(v_tok[0:n, r, :], A[0:n, P:2 * P])
                dve.tensor_tensor(s_dec[0:n, r, 0:n], A[0:n, 2 * P:2 * P + n], rtab[0:n, 0:n],
                                  ALU.mult).then_inc(ret_a_used, 1)

            def next_state(j, b):
                if b == 0:
                    dve.wait_ge(state_stored, 32 * j + 32)
                dve.wait_ge(ret_b_ready, NB * j + b + 1)
                if b == 0:
                    ins = dve.tensor_copy(state[:, :], bank[5][:, 0:P])
                elif b < NB - 1:
                    dve.wait_ge(state_ready, NB * j + b)
                    ins = dve.scalar_tensor_tensor(state[:, :], state[:, :], rtab[:, RT_K + 2:RT_K + 3],
                                                   bank[5][:, 0:P], ALU.mult, ALU.add)
                else:
                    ins = dve.scalar_tensor_tensor(state_new[:, :], state_in[:, :], rtab[:, RT_K + 3:RT_K + 4],
                                                   bank[5][:, 0:P], ALU.mult, ALU.add)
                ins.then_inc(state_ready, 1)

            PER_HEAD = 3 * NB + 7
            base = seq[0]
            local = [0]

            def chain(ins, j):
                local[0] += 1
                in_loop_wait(ins, base, PER_HEAD, j, local[0])

            def head(j, last):
                local[0] = 0
                for s in range(3 * (N_HEAD - last)):
                    if 1 <= s <= NB:
                        normalise(j, s - 1)
                    if s < NB:
                        mask_and_max(j, s)
                    if 1 <= s <= 8:
                        ada_dots(16 + s - 1 + 8 * j, 8 + (s - 1) // 2 + 1 + 4 * j, (s - 1) % 2, mod_part[:, s - 1, 0:1], mod_part[:, s - 1, 1:2])
                    if s == NB:
                        chain(add_ada_bias(16 + 8 * j, 8, 16 + 8 * j + 8), j)
                    for b in range(NB + 1):
                        if s >= NB and RET_TAKE_SLOT[last][b] == s:
                            if b < NB:
                                take_block(j, b)
                            if b >= 1:
                                next_state(j, b - 1)
                for b in range(NB + 1):
                    if RET_TAKE_SLOT[last][b] >= 3 * (N_HEAD - last):
                        if b < NB:
                            take_block(j, b)
                        if b >= 1:
                            next_state(j, b - 1)
                dve.wait_ge(act_evac, 3 * head_unit(j, 3) + 3)
                for c in range(3):
                    a, n = CHUNKS[c]
                    dve.wait_ge(std_ready, 3 + 3 * j + c + 1)
                    chain(dve.reciprocal(std[:, c, 0:n], std[:, c, 0:n]), j)
                    out = xm[:, j, a:a + n]
                    chain(dve.tensor_tensor(out, out, std[:, c, 0:n], ALU.mult), j)
                    dve.tensor_tensor(out, out, rg[:, a:a + n], ALU.mult).then_inc(norm_applied, 1)
                assert local[0] == PER_HEAD, local[0]

            with dve.Fori(0, HEADS - 1) as j:
                head(j, 0)
            head(HEADS - 1, 1)
            seq[0] = base + PER_HEAD * HEADS

            then_wait(norm_scale(1, 24))
            for c in range(3):
                a, n = CHUNKS[c]
                for i, k in enumerate(MIX_ORDER):
                    dve.wait_ge(mix_hi_ready, KT * c + i + 1)
                    dve.tensor_tensor(act_hl[:, 1, k, a:a + n], xm[:, k, a:a + n], act_hl[:, 0, k, a:a + n].bitcast(F32),
                                      ALU.subtract).then_inc(mix_lo_ready, 1)

            def out_unit(o):
                for c in range(3):
                    a, n = CHUNKS[c]
                    dve.wait_ge(gemm_ready, 66 + 3 * o + c + 1)
                    for off, tok, m, part in pieces(c):
                        x = xm[:, o, tok:tok + m]
                        ins = dve.scalar_tensor_tensor(x, bank[c][:, off:off + m], mod[:, 16 + o, part:part + 1],
                                                       x, ALU.mult, ALU.add)
                    ins.then_inc(dve_evac, 1)

            for c in range(3):
                dve.wait_ge(x_loaded[c], 32)
            base_out = seq[0]
            with dve.Fori(0, N_OUT // 2) as i:
                for p in range(2):
                    out_unit(2 * i + p)
                    for t in range(2):
                        m = 2 * p + t
                        ada_dots(48 + m + 4 * i, 24 + p + 1 + 2 * i, t, mod_part[:, m, 0:1], mod_part[:, m, 1:2])
                in_loop_wait(add_ada_bias(48 + 4 * i, 4, 48 + 4 * i + 4), base_out, 1, i, 1)
            seq[0] = base_out + N_OUT // 2
            modulate(15, 3 * KT, 1, 24, False)
            then_wait(norm_scale(2, 48))

            def up_pair(f, t, n_ext, local0, i, base_seq, per):
                dve.wait_ge(ext_ready, 2 * n_ext + 2)
                w = conv_wb_sb[:, bass.ds(f, 1), :]
                ins = dve.tensor_scalar(conv[:, :], gate_ext[:, 0:T + 2], w[:, 0, 0:1], w[:, 0, 3:4], ALU.mult, ALU.add)
                in_loop_wait(ins, base_seq, per, i, local0 + 1)
                ins = dve.scalar_tensor_tensor(conv[:, :], gate_ext[:, 1:T + 3], w[:, 0, 1:2], conv[:, :], ALU.mult, ALU.add)
                in_loop_wait(ins, base_seq, per, i, local0 + 2)
                dve.scalar_tensor_tensor(conv[:, :], gate_ext[:, 2:T + 4], w[:, 0, 2:3], conv[:, :], ALU.mult,
                                         ALU.add).then_inc(conv_ready, 1)
                dve.wait_ge(silu_ready, f + 1)
                for c in range(3):
                    dve.wait_ge(gemm_ready, 90 + 6 * f + 3 + c + 1)
                    if c >= 2 or t > 0 or not isinstance(f, int) or f > 0:
                        dve.wait_ge(u_lo_ready, 3 * f + c - 1)
                    for off, tok, m, part in pieces(c):
                        ins = dve.tensor_tensor(hf[:, (3 * t + c) % 2, off:off + m], conv[:, tok + 2 * part:tok + 2 * part + m],
                                                bank[c][:, off:off + m], ALU.mult)
                    ins.then_inc(uf_ready, 1)

            def down_tile(g, r, o, c):
                dve.wait_ge(down_ready, 24 * g + r + 1)
                for off, tok, m, part in pieces(c):
                    x = xm[:, o, tok:tok + m]
                    ins = dve.scalar_tensor_tensor(x, bank[3 + r % 4][:, off:off + m], mod[:, 40 + o, part:part + 1],
                                                   x, ALU.mult, ALU.add)
                ins.then_inc(down_free, 1)

            dve.sem_inc(down_free, 4)
            dve.wait_ge(pool_const, 3)
            for t in range(2):
                up_pair(t, t, t, 2 * t, 0, seq[0], 0)
            seq[0] += 4
            base_ffn = seq[0]
            with dve.Fori(0, (GROUPS - 1) // 2) as i:
                for h in range(2):
                    for t in range(2):
                        f = 2 + 4 * i + 2 * h + t
                        up_pair(f, t, f, 4 * h + 2 * t, i, base_ffn, 8)
                    for o in range(KT):
                        for c in range(3):
                            down_tile(2 * i + h, 3 * o + c, o, c)
            seq[0] = base_ffn + 8 * ((GROUPS - 1) // 2)
            for c in range(3):
                for o in range(KT):
                    down_tile(GROUPS - 1, KT * c + o, o, c)
            modulate(18, 0, 2, 48, True)

        @block.tensor
        def _(pe):
            def sums(q, c, src, to=None):
                n = CHUNKS[c][1]
                pe.matmul(bank[SUM_BANK[c] if to is None else to][:, 0:n], ones[:, :], src[:, 0:n], start=True, stop=True).then_inc(sum_ready, 1)

            def unit(n, slot, wait_bank, between, order=range(KT), wait_input=None, after_unit=True):
                pe.wait_ge(wl_ready, n + 1)
                for c in range(3):
                    a, m = CHUNKS[c]
                    wait_bank(c)
                    for pas, (w, x) in enumerate(((0, 0), (0, 1), (1, 0))):
                        for i, k in enumerate(order):
                            if wait_input and pas == 0:
                                wait_input(c, i)
                            ins = pe.matmul(bank[c][:, 0:m], w_hl[:, slot, w, k, :], act_hl[:, x, k, a:a + m],
                                            start=(pas == 0 and i == 0), stop=(pas == 2 and i == KT - 1))
                            if after_unit and c == pas == i == 0:
                                ins.then_inc(unit_done, 1)
                        if pas == 2:
                            ins.then_inc(gemm_ready, 1)
                        between(3 * c + pas)

            def finish_unit(n):
                pe.wait_ge(gemm_ready, 3 * (n + 1))
                pe.sem_inc(unit_done, 1)

            pe.wait_ge(pool_const, 2)
            pe.wait_ge(const_loaded, 16 * 5)
            for c in range(3):
                a, n = CHUNKS[c]
                pe.wait_ge(sq_used, KT * (c + 1))
                sums(c, c, acc[:, a:a + n])

            def after(n):
                def wait(c):
                    pe.wait_ge(act_evac, 3 * (n - 1) + c + 1)
                return wait

            def nothing(s):
                pass

            def values_by_token(s):
                t, n = BLOCKS[s]
                if s == 0:
                    pe.wait_ge(act_evac, 6)
                    pe.wait_ge(std_ready, 3)
                if s >= 2:
                    pe.wait_ge(av_tok_ready, s - 1)
                pe.transpose(bank[(3, 6)[s % 2]][0:n, 0:P], rv[:, t:t + n], ident[:, :]).then_inc(av_t_ready, 1)

            unit(0, SLOTS[0], lambda c: None, nothing, wait_input=lambda c, i: pe.wait_ge(lo_ready, KT * c + i + 1),
                 after_unit=False)
            unit(1, SLOTS[1], after(1), nothing)
            unit(2, SLOTS[2], after(2), values_by_token)
            finish_unit(2)

            def scores(j, b):
                t, n = BLOCKS[b]
                kb = keys_of(b)
                kn = sum(k[1] for k in kb)
                if b == 0:
                    pe.wait_ge(act_evac, 9 + 15 * j)
                    pe.wait_ge(av_tok_ready, NB)
                    pe.wait_ge(cache_loaded, 32)
                    pe.wait_ge(std_ready, 3 + 3 * j)
                else:
                    pe.wait_ge(masked_ready, NB * j + b)
                    if b == NB - 1:
                        seal_waits(pe)
                for g in range(2):
                    h = slice(64 * g, 64 * g + 64)
                    ins = pe.matmul(bank[3 + g][0:n, 0:kn], aq[h, t:t + n], ak[h, kb[0][0]:kb[0][0] + kn],
                                    start=True, stop=True)
                ins.then_inc(qk_ready, 1)

            def transpose_prob(j, b):
                n, r, kb = BLOCKS[b][1], b % 2, keys_of(b)
                pe.wait_ge(prob_ready, NB * j + b + 1)
                if b > 0:
                    pe.wait_ge(pt_copied, NB * j + b)
                if b == NB - 1:
                    seal_waits(pe)
                for g in range(2):
                    at = 0
                    for i, k in enumerate(kb):
                        col = P * (2 * g + i)
                        ins = pe.transpose(bank[5][0:k[1], col:col + n], prob[0:n, r, g, at:at + k[1]], ident[0:n, 0:n])
                        at += k[1]
                ins.then_inc(pt_ready, 1)

            def weigh_values(j, b):
                n, r, kb = BLOCKS[b][1], b % 2, keys_of(b)
                pe.wait_ge(pt_copied, NB * j + b + 1)
                if b > 0:
                    pe.wait_ge(pv_copied, NB * j + b)
                for g in range(2):
                    h = slice(64 * g, 64 * g + 64)
                    for i, k in enumerate(kb):
                        ins = pe.matmul(bank[6][h, 0:n], av_tok[0:k[1], k[3], h], prob_t[0:k[1], r, g, i, 0:n],
                                        start=(i == 0), stop=(i == len(kb) - 1))
                ins.then_inc(pv_ready, 1)

            def block_scores(j, b):
                t, n = BLOCKS[b]
                if b == 0:
                    pe.wait_ge(act_evac, 3 * head_unit(j, 2) + 3)
                    pe.wait_ge(masked_ready, NB * j + NB)
                if b >= 2:
                    pe.wait_ge(ret_a_used, NB * j + b - 1)
                if b == NB - 1:
                    seal_waits(pe)
                A = bank[3 + b % 2]
                pe.transpose(A[0:n, 0:P], rk[:, t:t + n], ident[:, :])
                pe.transpose(A[0:n, P:2 * P], rv[:, t:t + n], ident[:, :])
                pe.matmul(A[0:n, 2 * P:2 * P + n], rk[:, t:t + n], rq[:, t:t + n], start=True,
                          stop=True).then_inc(ret_a_ready, 1)

            def block_output(j, b):
                t, n = BLOCKS[b]
                r = b % 2
                if b == 0:
                    pe.wait_ge(qdec_ready, 2 * j + 2)
                    pe.wait_ge(pv_copied, NB * j + NB)
                else:
                    pe.wait_ge(ret_o_copied, NB * j + b)
                    pe.wait_ge(state_ready, NB * j + b)
                pe.wait_ge(ret_a_used, NB * j + b + 1)
                carried = state if b < NB - 1 else state_in
                if b == NB - 1:
                    pe.wait_ge(ret_tab_loaded, 32 * (j + 1))
                pe.matmul(bank[6][:, 0:n], v_tok[0:n, r, :], s_dec[0:n, r, 0:n], start=True, stop=(b == 0))
                if b > 0:
                    pe.matmul(bank[6][:, 0:n], carried[:, :], acc[:, t:t + n], start=False, stop=True)
                pe.matmul(bank[5][:, 0:P], k_tok[0:n, r, :], v_tok[0:n, r, :], start=True, stop=True).then_inc(ret_b_ready, 1)

            def head(j, last):
                def between(p):
                    def steps(i):
                        s = 9 * p + i
                        b = s // 3
                        if s % 3 == 0 and b < NB:
                            scores(j, b)
                        if s % 3 == 1 and 1 <= b <= NB:
                            transpose_prob(j, b - 1)
                        if s % 3 == 0 and 2 <= b <= NB + 1:
                            weigh_values(j, b - 2)
                        for k in range(NB + 1):
                            if RET_PE_STEP[last][k] == s:
                                if k < NB:
                                    block_scores(j, k)
                                if k >= 1:
                                    block_output(j, k - 1)
                    return steps
                for p in range(N_HEAD - last):
                    unit(head_unit(j, p), HEAD_SLOTS[p], after(head_unit(j, p)), between(p), after_unit=p > 0)
                finish_unit(head_unit(j, N_HEAD - last - 1))
                for k in range(NB + 1):
                    if RET_PE_STEP[last][k] >= 9 * (N_HEAD - last):
                        if k < NB:
                            block_scores(j, k)
                        if k >= 1:
                            block_output(j, k - 1)
                for c in range(3):
                    pe.wait_ge(ret_sq_ready, 3 * j + c + 1)
                    sums(3 + 3 * j + c, c, sq[:, c % 2, :])

            with pe.Fori(0, HEADS - 1) as j:
                head(j, 0)
            head(HEADS - 1, 1)

            def after_out(o):
                def wait(c):
                    if isinstance(o, int) and o == -2:
                        pe.wait_ge(act_evac, 63 + c + 1)
                    else:
                        pe.wait_ge(dve_evac, 3 * o + 3 + c + 1)
                return wait

            def out_unit(o, first):
                unit(UNIT_OUT + o, SLOTS[UNIT_OUT + o], after_out(o - 2), nothing, MIX_ORDER,
                     (lambda c, i: pe.wait_ge(mix_lo_ready, KT * c + i + 1)) if first else None, not first)

            for p in range(2):
                out_unit(p, p == 0)
            with pe.Fori(0, N_OUT // 2 - 1) as i:
                for p in range(2):
                    unit(UNIT_OUT + 2 + p + 2 * i, SLOTS[UNIT_OUT + p], after_out(2 * i + p), nothing, MIX_ORDER)
            finish_unit(UNIT_FFN - 1)
            for c in range(3):
                a, n = CHUNKS[c]
                pe.wait_ge(sq_used, 3 * KT + 3 * (N_OUT - 1) + c + 1)
                sums(15 + c, c, acc[:, a:a + n])

            def ffn_unit(n, f, f_before, is_up, slot, units_before, wait_input=None):
                pe.wait_ge(wl_ready, n + 1)
                for c in range(3):
                    a, m = CHUNKS[c]
                    if is_up:
                        pe.wait_ge(act_evac, 66 + 3 * f + c + 1)
                    elif f_before is None:
                        pe.wait_ge(dve_evac, 21 + c + 1)
                    else:
                        pe.wait_ge(uf_ready, 3 * f_before + c + 1)
                    for pas, (w, x) in enumerate(((0, 0), (0, 1), (1, 0))):
                        for k in range(KT):
                            if wait_input and pas == 0:
                                wait_input(c, k)
                            ins = pe.matmul(bank[c][:, 0:m], w_hl[:, slot, w, k, :], act_hl[:, x, k, a:a + m],
                                            start=(pas == 0 and k == 0), stop=(pas == 2 and k == KT - 1))
                            if c == pas == 0 and k < units_before:
                                ins.then_inc(unit_done, 1)
                    ins.then_inc(gemm_ready, 1)

            def down(g, n, slots, par, order, after_unit=True):
                pe.wait_ge(wl_ready, n + 2)
                pe.wait_ge(u_lo_ready, 6 * g + 6)
                for r, (o, c) in enumerate(order):
                    a, m = CHUNKS[c]
                    pe.wait_ge(down_free, 24 * g + r + 1)
                    i = 0
                    for t in range(2):
                        for w, x in ((0, 0), (0, 1), (1, 0)):
                            ins = pe.matmul(bank[3 + r % 4][:, 0:m], w_hl[:, slots[t], w, o, :],
                                            u_hl[:, par, t, x, a:a + m], start=(i == 0), stop=(i == 5))
                            if r == i == 0 and after_unit:
                                ins.then_inc(unit_done, 1)
                            i += 1
                    ins.then_inc(down_ready, 1)

            tile_order = [(o, c) for o in range(KT) for c in range(3)]
            for t in range(2):
                for h in range(2):
                    n = UNIT_FFN + 2 * t + h
                    first = t == 0 and h == 0
                    ffn_unit(n, t, None if t == 0 else 0, h, SLOTS[n], [[0, 1], [1, 0]][t][h],
                             (lambda c, k: pe.wait_ge(lo_ready, 3 * KT + KT * c + k + 1)) if first else None)
            with pe.Fori(0, (GROUPS - 1) // 2) as i:
                for h in range(2):
                    at = UNIT_FFN + 4 + 6 * h
                    for t in range(2):
                        for b in range(2):
                            ffn_unit(at + 2 * t + b + 12 * i, 2 + 4 * i + 2 * h + t, 1 + 2 * h + t + 4 * i, b, SLOTS[at + 2 * t + b],
                                     2 if t == b == 0 else 1)
                    down(2 * i + h, at + 4 + 12 * i, SLOTS[at + 4:at + 6], h, tile_order)
            pe.wait_ge(down_ready, 24 * (GROUPS - 1))
            pe.sem_inc(unit_done, 2)
            n = N_UNITS - 2
            down(GROUPS - 1, n, SLOTS[n:n + 2], 0, [(o, c) for c in range(3) for o in range(KT)], False)
            for c in range(3):
                a, m = CHUNKS[c]
                pe.wait_ge(sq_used, 6 * KT + KT * (c + 1))
                sums(18 + c, c, acc[:, a:a + m], (7, 0, 1)[c])


MIX_ORDER = [4, 5, 6, 7, 0, 1, 2, 3]
RET_PE_STEP = [[28, 31, 32, 34, 35, 37, 38, 40, 41, 43], [28] + list(range(31, 40))]
RET_TAKE_SLOT = [[s // 3 for s in RET_PE_STEP[i]] for i in range(2)]


def constants():
    q = np.arange(P)[:, None]
    k = np.arange(2 * P)[None, :]
    dist = np.abs(P + q - k).astype(np.float64)
    valid = np.where(q < 64, k < 192, k >= 64)
    slopes = 2.0 ** -np.arange(1, 9)
    bias = np.where(valid[None], -slopes[:, None, None] * dist[None], MASKED).astype(np.float32)
    att_bias = np.stack([np.concatenate([bias[j], bias[j + 4]], axis=1) for j in range(HEADS)])
    lg = np.log1p(-2.0 ** (-5.0 - np.arange(HEADS)))
    tab = np.zeros((HEADS, P, RT_COLS))
    i = np.arange(P)
    for h in range(HEADS):
        diff = i[None, :] - i[:, None]
        tab[h, :, RT_DECAY:RT_DECAY + P] = np.where(diff >= 0, np.exp(lg[h] * np.maximum(diff, 0)), 0.0)
        tab[h, :, RT_Q:RT_Q + P] = np.exp(lg[h] * (i[None, :] + 1.0))
        tab[h, :, RT_K] = np.exp(lg[h] * (P - 1.0 - i))
        tab[h, :64, RT_K + 1] = np.exp(lg[h] * (63.0 - i[:64]))
        tab[h, :, RT_K + 2] = np.exp(lg[h] * P)
        tab[h, :, RT_K + 3] = np.exp(lg[h] * 64)
    return np.eye(P, dtype=np.float32), att_bias, tab.astype(np.float32)


def unit_of(w):
    return w.reshape(KT, P, P).transpose(1, 0, 2).reshape(P, D)


def kernel(**inputs):
    import numpy as _np
    import concourse.bacc as _bacc
    from concourse import mybir as _mybir
    from concourse.bass_utils import run_bass_kernel_spmd as _run

    x = {k: _np.asarray(v) for k, v in inputs.items()}
    w_in, w_out, w_up, w_down = x["w_in"][0], x["w_out"][0], x["w_up"][0], x["w_down"][0]
    aq0, ak0, av0 = 2048, 2560, 2688

    def aq_cols(j):
        return _np.concatenate([w_in[:, aq0 + 64 * h:aq0 + 64 * h + 64] for h in (j, j + 4)], axis=1)

    units = [w_in[:, ak0:ak0 + P], w_in[:, av0:av0 + P], aq_cols(0)]
    for j in range(HEADS):
        units += [w_in[:, 512 * g + P * j:512 * g + P * (j + 1)] for g in range(4)]
        if j < HEADS - 1:
            units.append(aq_cols(j + 1))
    rows = list(range(512)) + [512 + 64 * h + i for j in range(HEADS) for h in (j, j + 4) for i in range(64)]
    w_out = w_out[rows]
    units += [w_out[:, P * o:P * (o + 1)] for o in range(N_OUT)]
    units = [unit_of(u) for u in units]

    def up(g):
        out = []
        for f in (2 * g, 2 * g + 1):
            out += [unit_of(w_up[:, P * f:P * (f + 1)]), unit_of(w_up[:, D_FF + P * f:D_FF + P * (f + 1)])]
        return out

    def down(g):
        return [w_down[P * f:P * (f + 1)] for f in (2 * g, 2 * g + 1)]

    units += up(0)
    for g in range(GROUPS - 1):
        units += up(g + 1) + down(g)
    units += down(GROUPS - 1)

    w_all = _np.concatenate([x["w_ada"][0], x["w_ada_f"]], axis=1)
    b_all = _np.concatenate([x["b_ada"][0], x["b_ada_f"]])
    sh1, sc1, g1, sh2, sc2, g2, shf, scf = (D * i for i in range(8))
    cols = []
    for a, b in ((sc1, sh1), (g1, None), (sc2, sh2), (g2, None), (scf, shf)):
        for k in range(KT):
            cols += [a + P * k] + ([b + P * k] if b is not None else [])
    tiles = _np.stack([w_all[:, c:c + P].T for c in cols])
    biases = _np.stack([b_all[c:c + P] for c in cols], axis=1)

    def by_tile(a):
        return a.reshape(a.shape[0], -1, P).transpose(2, 1, 0)

    ident, att_bias, ret_tab = constants()
    arrays = {
        "x_t": _np.concatenate([x["x_prompt"][0], x["x_sample"][0]]).T,
        "w_units": _np.stack(units),
        "w_ada_t": tiles,
        "b_ada_t": biases,
        "cond_rows": _np.concatenate([x["c_prompt"], x["c_sample"]]),
        "gains": _np.stack([x["norm1_g"][0], x["norm2_g"][0], x["normf_g"]]).reshape(3, KT, P).transpose(2, 0, 1),
        "conv_wb": by_tile(_np.concatenate([x["conv_w"][0], x["conv_b"]])),
        "conv_st": by_tile(x["state_conv"][0, 0]),
        "sinks": x["attn_sinks"][0].reshape(2, HEADS).T,
        "ck_t": x["cache_k"].reshape(P, P).T,
        "cv": x["cache_v"].reshape(P, P),
        "st_in": x["state_ret"].reshape(HEADS, P, P),
        "identity": ident, "att_bias": att_bias, "ret_tab": ret_tab,
    }
    outs = {"y_t": (D, T), "p_state": (HEADS, P, P), "pk_t": (P, P), "pv": (P, P), "conv_out_t": (P, FT, 4),
            "s_state": (HEADS, P, P), "sk_t": (P, S_SAMPLE), "sv": (S_SAMPLE, P)}

    nc = _bacc.Bacc("TRN2", target_bir_lowering=False, num_devices=1, dynamic_dma_scratch_size=1024)
    arrays = {k: _np.ascontiguousarray(v) for k, v in arrays.items()}
    args = [nc.dram_tensor(f"in_{k}", v.shape, _mybir.dt.from_np(v.dtype), kind="ExternalInput").ap() for k, v in arrays.items()]
    args += [nc.dram_tensor(f"out_{k}", s, F32, kind="ExternalOutput").ap() for k, s in outs.items()]
    hymba_step(nc, *args)
    r = _run(nc, [{f"in_{k}": v for k, v in arrays.items()}], core_ids=[0]).results[0]
    r = {k: r[f"out_{k}"] for k in outs}

    y = r["y_t"].T
    conv_rows = r["conv_out_t"].transpose(2, 1, 0).reshape(2, 2, D_FF)
    return (y[None, :S_PROMPT], y[None, S_PROMPT:], r["p_state"][None, None],
            r["pk_t"].T.reshape(1, 1, P, 2, 64), r["pv"].reshape(1, 1, P, 2, 64), conv_rows[0][None, None],
            r["s_state"][None, None], r["sk_t"].T.reshape(1, 1, S_SAMPLE, 2, 64), r["sv"].reshape(1, 1, S_SAMPLE, 2, 64),
            conv_rows[1][None, None])
```

```python
from contextlib import ExitStack

import numpy as np

import concourse.bass as bass
from concourse import mybir

ALU = mybir.AluOpType
ACT = mybir.ActivationFunctionType
F32 = mybir.dt.float32
F32R = mybir.dt.float32r
BF16 = mybir.dt.bfloat16

P = 128
D = 1024
KT = D // P
S_PROMPT = 1024
S_SAMPLE = 64
T = S_PROMPT + S_SAMPLE
CHUNKS = [(0, 364), (364, 362), (726, 362)]
C2P = S_PROMPT - CHUNKS[2][0]
NB = 9
BLOCKS = [(P * b, P) for b in range(8)] + [(S_PROMPT, S_SAMPLE)]
HEADS = 4
D_FF = 2816
FT = D_FF // P
EPS = 1e-6
RET_SCALE = float(np.float32(128 ** -0.5))
ATT_SCALE = 64 ** -0.5
MASKED = -1e30

N_PRO, N_HEAD, N_OUT = 3, 5, 8
HEAD_SLOTS = [0, 1, 2, 0, 1]
UNIT_OUT = N_PRO + N_HEAD * HEADS - 1
UNIT_FFN = UNIT_OUT + N_OUT
GROUPS = FT // 2
N_UNITS = UNIT_FFN + 3 * FT
SLOTS = ([2, 0, 1] + HEAD_SLOTS * 3 + HEAD_SLOTS[:4] + [1] + [2, 0] * 2 + [1, 2, 0] + [1, 2, 0, 1] + [2, 0, 1] * 20
         + [2, 0])
assert len(SLOTS) == N_UNITS

RT_DECAY, RT_Q, RT_K, RT_COLS = 0, 128, 256, 260
N_MOD = 64


def unit_gap(units):
    gaps = []
    for n in units:
        before = [m for m in range(n) if SLOTS[m] == SLOTS[n]]
        if before:
            gaps.append(n - before[-1])
        else:
            return None
    return min(gaps)


def unit_loads(units, i):
    counts = [SLOTS[:n + 1].count(SLOTS[n]) for n in units]
    if len(counts) == 1:
        return counts[0]
    per = counts[1] - counts[0]
    assert counts == [counts[0] + per * k for k in range(len(counts))]
    return counts[0] + per * i


def hymba_step(nc, x_t, w_units, w_ada, b_ada, cond, gains, conv_wb, conv_st, sinks, ck_t, cv_in, st_in,
               ident_in, att_bias, ret_tab, y_t, p_state, pk_t, pv, p_conv, s_state, sk_t, sv):
    x_v = x_t.rearrange("(k p) t -> p k t", p=P)
    y_v = y_t.rearrange("(k p) t -> p k t", p=P)

    with ExitStack() as ctx:
        def sb(name, shape, dt=F32, at=ctx):
            return at.enter_context(nc.sbuf_tensor(name, shape, dt))

        def sem(name):
            return ctx.enter_context(nc.semaphore(name))

        act_hl = sb("act_hl", [P, 2, KT, T], F32R)
        w_hl = sb("w_hl", [P, 3, 2, KT, P], F32R)
        xm = sb("xm", [P, KT, T])
        w_raw = sb("w_raw", [P, 3, KT, P])
        ident = sb("ident", [P, P])
        ones = sb("ones", [P, P])
        sq = sb("sq", [P, 2, CHUNKS[0][1]])
        acc = sb("acc", [P, T])
        hf = sb("hf", [P, 3, CHUNKS[0][1]])
        std = sb("std", [P, 3, CHUNKS[0][1]])
        mod = sb("mod", [P, N_MOD, 2])
        mod_part = sb("mod_part", [P, 8, 2])
        scale_n = sb("scale_n", [P, 3, KT, 2])
        b_ada_sb = sb("b_ada_sb", [P, N_MOD])
        gains_sb = sb("gains_sb", [P, 3, KT])
        conv_wb_sb = sb("conv_wb_sb", [P, FT, 4])
        conv_st_sb = sb("conv_st_sb", [P, FT, 2])
        conv_out = sb("conv_out", [P, FT, 4])
        eps_sb = sb("eps_sb", [P, 1])

        ada_w = sb("ada_w", [P, 2, D])
        ada_out = sb("ada_out", [P, D], BF16)
        silu_c = sb("silu_c", [P, 2, D])

        heads_phase = ExitStack()
        rq = sb("rq", [P, T], at=heads_phase)
        rk = sb("rk", [P, T], at=heads_phase)
        rv = sb("rv", [P, T], at=heads_phase)
        rg = sb("rg", [P, T], at=heads_phase)
        aq = sb("aq", [P, T], at=heads_phase)
        ak = sb("ak", [P, T + P], at=heads_phase)
        av_tok = sb("av_tok", [P, NB + 1, P], at=heads_phase)
        att_tab = sb("att_tab", [P, 2, 256], at=heads_phase)
        sink_sb = sb("sink_sb", [P, 2], at=heads_phase)
        rtab = sb("rtab", [P, RT_COLS], at=heads_phase)
        prob = sb("prob", [P, 2, 2, 256], at=heads_phase)
        prob_t = sb("prob_t", [P, 2, 2, 2, P], at=heads_phase)
        soft = sb("soft", [P, 2, 5, 2], at=heads_phase)
        rden = sb("rden", [P, 2, 2], at=heads_phase)
        k_tok = sb("k_tok", [P, 2, P], at=heads_phase)
        v_tok = sb("v_tok", [P, 2, P], at=heads_phase)
        s_dec = sb("s_dec", [P, 2, P], at=heads_phase)
        state = sb("state", [P, P], at=heads_phase)
        state_in = sb("state_in", [P, P], at=heads_phase)
        state_new = sb("state_new", [P, P], at=heads_phase)
        heads_phase.close()
        u_hl = sb("u_hl", [P, 2, 2, 2, T], F32R)
        gate_ext = sb("gate_ext", [P, T + 4])
        conv = sb("conv", [P, T + 2])

        bank = [ctx.enter_context(nc.psum_tensor(f"bank{i}", [P, 512], F32)) for i in range(8)]
        SUM_BANK = [7, 6, 7]
        ada_place = [ada_w[:, 0], ada_w[:, 1]] + [t[:, 0:D] for t in (rk, rg, rq, rv, aq, ak)]

        const_loaded = sem("const_loaded")
        cond_loaded = sem("cond_loaded")
        x_loaded = [sem(f"x_loaded{c}") for c in range(3)]
        x_again = [sem(f"x_again{c}") for c in range(3)]
        x_tile_again = sem("x_tile_again")
        ada_loaded = [sem(f"ada_loaded{r}") for r in range(8)]
        w_loaded = [sem(f"w_loaded{slot}") for slot in range(3)]
        att_tab_loaded = sem("att_tab_loaded")
        ret_tab_loaded = sem("ret_tab_loaded")
        cache_loaded = sem("cache_loaded")
        stored = sem("stored")
        state_stored = sem("state_stored")
        silu_c_ready = sem("silu_c_ready")
        pool_const = sem("pool_const")
        dve_seq = sem("dve_seq")
        ada_used = sem("ada_used")
        mod_ready = sem("mod_ready")
        sq_ready = sem("sq_ready")
        sq_used = sem("sq_used")
        acc_ready = sem("acc_ready")
        sum_ready = sem("sum_ready")
        std_ready = sem("std_ready")
        norm_applied = sem("norm_applied")
        hf_ready = sem("hf_ready")
        hi_ready = sem("hi_ready")
        lo_ready = sem("lo_ready")
        wh_ready = sem("wh_ready")
        wl_ready = sem("wl_ready")
        unit_done = sem("unit_done")
        gemm_ready = sem("gemm_ready")
        act_evac = sem("act_evac")
        dve_evac = sem("dve_evac")
        av_t_ready = sem("av_t_ready")
        av_tok_ready = sem("av_tok_ready")
        qk_ready = sem("qk_ready")
        masked_ready = sem("masked_ready")
        exp_ready = sem("exp_ready")
        prob_ready = sem("prob_ready")
        pt_ready = sem("pt_ready")
        pt_copied = sem("pt_copied")
        pv_ready = sem("pv_ready")
        pv_copied = sem("pv_copied")
        qdec_ready = sem("qdec_ready")
        ret_a_ready = sem("ret_a_ready")
        ret_a_used = sem("ret_a_used")
        ret_b_ready = sem("ret_b_ready")
        ret_o_copied = sem("ret_o_copied")
        state_ready = sem("state_ready")
        ret_sq_ready = sem("ret_sq_ready")
        mix_hi_ready = sem("mix_hi_ready")
        mix_lo_ready = sem("mix_lo_ready")
        mix_lo_pool = sem("mix_lo_pool")
        ext_ready = sem("ext_ready")
        conv_ready = sem("conv_ready")
        silu_ready = sem("silu_ready")
        uf_ready = sem("uf_ready")
        u_hi_ready = sem("u_hi_ready")
        u_lo_ready = sem("u_lo_ready")
        down_ready = sem("down_ready")
        down_free = sem("down_free")
        normed_ready = sem("normed_ready")
        y_ready = sem("y_ready")
        waits_passed = sem("waits_passed")

        def head_unit(j, p):
            return N_PRO + N_HEAD * j + p

        def seal_waits(eng):
            eng.sem_inc(waits_passed, 1)

        def keys_of(b):
            if b == 0:
                return [(0, P, P, 0)]
            if b == NB - 1:
                return [(S_PROMPT, P, 0, 8), (S_PROMPT + P, S_SAMPLE, P, 9)]
            return [(P * (b - 1), P, 0, b - 1), (P * b, P, P, b)]

        def pieces(c):
            a, n = CHUNKS[c]
            if c < 2:
                return [(0, a, n, 0)]
            return [(0, a, C2P, 0), (C2P, S_PROMPT, S_SAMPLE, 1)]

        FFN_BODY = [("up", 0), ("up", 1), ("up", 2), ("up", 3), ("down", 0), ("down", 1)]

        def ffn_chunk(f, is_up, c):
            if isinstance(f, int) and f == 0:
                return 90 + ((1, 2, 5), (3, 4, 6))[is_up][c]
            return 90 + 6 * f + 3 * is_up + c + 1

        block = ctx.enter_context(nc.Block())

        @block.sync
        def _(sp):
            def load_unit(n, like):
                gap = unit_gap(like)
                if gap is not None:
                    sp.wait_ge(wl_ready, n - gap + 1)
                slot = SLOTS[like[0]]
                sp.dma_start(w_raw[:, slot], w_units[n].rearrange("p (k m) -> p k m", k=KT)).then_inc(w_loaded[slot], 16)

            def load_ada(m, ring):
                sp.wait_ge(ada_used, 2 * (m - 2) + 2)
                sp.dma_start(ada_w[:, ring], w_ada[m]).then_inc(ada_loaded[ring], 16)

            def load_first_ada(m):
                if m >= 8:
                    sp.wait_ge(ada_used, 2 * (m - 8) + 2)
                sp.dma_start(ada_place[m % 8], w_ada[m]).then_inc(ada_loaded[m % 8], 16)

            def load_x(c):
                a, n = CHUNKS[c]
                sp.dma_start(xm[:, :, a:a + n], x_v[:, :, a:a + n]).then_inc(x_loaded[c], 16)

            def load_head_tables(j):
                if not isinstance(j, int) or j > 0:
                    sp.wait_ge(prob_ready, NB * j)
                sp.dma_start(att_tab[:, :, :], att_bias[j].rearrange("p (g k) -> p g k", g=2)).then_inc(att_tab_loaded, 16)
                sp.dma_start(sink_sb[:, :], sinks[j].partition_broadcast(P)).then_inc(att_tab_loaded, 16)

            def load_ret_tables(j):
                if not isinstance(j, int) or j > 0:
                    sp.wait_ge(state_ready, NB * j)
                sp.dma_start(rtab[:, :], ret_tab[j]).then_inc(ret_tab_loaded, 16)
                sp.dma_start(state_in[:, :], st_in[j]).then_inc(ret_tab_loaded, 16)

            sp.dma_start(silu_c[:, :, :], cond.partition_broadcast(P)).then_inc(cond_loaded, 16)
            load_first_ada(0)
            load_first_ada(1)
            load_x(0)
            load_first_ada(2)
            load_x(1)
            load_first_ada(3)
            for dst, src in ((b_ada_sb, b_ada), (gains_sb, gains), (ident, ident_in), (conv_wb_sb, conv_wb),
                             (conv_st_sb, conv_st)):
                sp.dma_start(dst[:], src).then_inc(const_loaded, 16)
            load_unit(0, [0])
            load_x(2)
            load_first_ada(4)
            load_unit(1, [1])
            load_first_ada(5)
            load_unit(2, [2])
            for m in range(6, 16):
                load_first_ada(m)
            sp.dma_start(ak[:, S_PROMPT:S_PROMPT + P], ck_t).then_inc(cache_loaded, 16)
            sp.dma_start(av_tok[:, 8, :], cv_in).then_inc(cache_loaded, 16)
            load_head_tables(0)
            load_ret_tables(0)
            load_unit(3, [3])
            load_unit(4, [4])

            def head_in_loop(j):
                for p in range(N_HEAD):
                    load_unit(head_unit(j, p) + 2, [head_unit(i, p) + 2 for i in range(HEADS - 1)])
                    for t in range(2) if p < 4 else ():
                        load_ada(16 + 8 * j + 2 * p + t, t)
                load_head_tables(j + 1)
                load_ret_tables(j + 1)

            with sp.Fori(0, HEADS - 1) as j:
                head_in_loop(j)
            j = HEADS - 1
            for p in range(N_HEAD - 1):
                load_unit(head_unit(j, p) + 2, [head_unit(j, p) + 2])
                for t in range(2):
                    load_ada(16 + 8 * j + 2 * p + t, t)

            for c in range(3):
                a, n = CHUNKS[c]
                sp.wait_ge(mix_lo_ready, 5 * (c + 1))
                sp.wait_ge(mix_lo_pool, 2 * (c + 1))
                for k0, k1 in ((0, 3), (4, 8)):
                    sp.dma_start(xm[:, k0:k1, a:a + n], x_v[:, k0:k1, a:a + n]).then_inc(x_again[c], 16)
            sp.wait_ge(mix_lo_ready, 18)
            sp.dma_start(xm[:, 3, :], x_v[:, 3, :]).then_inc(x_tile_again, 16)
            for o in range(N_OUT):
                load_unit(UNIT_OUT + o + 2, [UNIT_OUT + o + 2])
                for t in range(2):
                    load_ada(48 + 2 * o + t, t)
            for p in range(4):
                load_unit(UNIT_FFN + p + 2, [UNIT_FFN + p + 2])
            with sp.Fori(0, (GROUPS - 1) // 2) as i:
                for p in range(12):
                    at = UNIT_FFN + 4 + p + 2
                    load_unit(at + 12 * i, [at + 12 * k for k in range((GROUPS - 1) // 2)])
            sp.wait_ge(ext_ready, 2 * FT)
            sp.dma_start(p_conv, conv_out[:, :, :]).then_inc(stored, 16)
            for c in range(3):
                a, n = CHUNKS[c]
                for k in (0, KT // 2):
                    sp.wait_ge(y_ready, KT * c + k + KT // 2)
                    sp.dma_start(y_v[:, k:k + KT // 2, a:a + n], xm[:, k:k + KT // 2, a:a + n]).then_inc(stored, 16)
            sp.wait_ge(stored, 16 * 11)
            sp.wait_ge(state_stored, 32 * HEADS + 32)

        @block.scalar
        def _(act):
            def split_weights(n, like, i=0):
                act.wait_ge(w_loaded[SLOTS[like[0]]], 16 * unit_loads(like, i))
                gap = unit_gap(like)
                if gap is not None:
                    act.wait_ge(unit_done, n - gap + 1)
                slot = SLOTS[like[0]]
                act.activation(w_hl[:, slot, 0], w_raw[:, slot], ACT.Copy).then_inc(wh_ready, 1)

            def square(src, item, ring):
                n = src.shape[-1]
                if not isinstance(item, int) or item >= 2:
                    act.wait_ge(sq_used, item - 1)
                act.activation(sq[:, ring, 0:n], src, ACT.Square).then_inc(sq_ready, 1)

            def root(q, c, width, at=None):
                n = CHUNKS[c][1]
                act.wait_ge(sum_ready, q + 1)
                if not isinstance(q, int) or q >= 3:
                    act.wait_ge(norm_applied, q - 2)
                act.activation(std[:, c, 0:n], bank[at or SUM_BANK[c]][:, 0:n], ACT.Sqrt, bias=eps_sb[:, 0:1],
                               scale=1.0 / width).then_inc(std_ready, 1)

            def shift_and_split(item, c, k, m0):
                act.wait_ge(hf_ready, item + 1)
                for dst in (act_hl[:, 0, k, :], None):
                    for o, tok, m, part in pieces(c):
                        h = hf[:, item % 3, o:o + m]
                        ins = act.activation(h if dst is None else dst[:, tok:tok + m], h, ACT.Identity,
                                             bias=mod[:, m0 + 2 * k + 1, part:part + 1])
                ins.then_inc(hi_ready, 1)

            act.sem_inc(state_stored, 32)
            act.wait_ge(cond_loaded, 16)
            act.activation(silu_c[:, :, :], silu_c[:, :, :], ACT.Silu).then_inc(silu_c_ready, 1)
            act.wait_ge(pool_const, 2)
            for c in range(3):
                a, n = CHUNKS[c]
                act.wait_ge(x_loaded[c], 16)
                for k in range(KT):
                    square(xm[:, k, a:a + n], KT * c + k, k % 2)
                root(c, c, D)
                split_weights(c, [c])
            for k in range(KT):
                for c in range(3):
                    shift_and_split(3 * k + c, c, k, 0)

            def evac(n_chunk, at, dst, func=ACT.Copy, scale=1.0):
                a, n = CHUNKS[(n_chunk if isinstance(n_chunk, int) else at) % 3]
                act.wait_ge(gemm_ready, n_chunk + 1)
                act.activation(dst[:, a:a + n], bank[at][:, 0:n], func, scale=scale).then_inc(act_evac, 1)

            for c in range(3):
                act.wait_ge(gemm_ready, c + 1)
                for o, t, n, part in pieces(c):
                    ins = act.activation(ak[:, t + P * part:t + P * part + n], bank[c][:, o:o + n], ACT.Copy)
                ins.then_inc(act_evac, 1)
            act.wait_ge(act_evac, 3)
            act.dma_start(pk_t, ak[:, S_PROMPT - P:S_PROMPT]).then_inc(stored, 16)
            act.dma_start(sk_t, ak[:, T + P - S_SAMPLE:T + P]).then_inc(stored, 16)
            for c in range(3):
                evac(3 + c, 3 + c, rv)
            split_weights(3, [3])
            for c in range(3):
                evac(6 + c, (6, 7, 0)[c], aq, scale=ATT_SCALE)
            split_weights(4, [4])
            act.wait_ge(av_tok_ready, NB)
            act.dma_start(pv, av_tok[:, 7, :]).then_inc(stored, 16)
            act.dma_start(sv, av_tok[0:S_SAMPLE, 9, :]).then_inc(stored, 16)

            def exps(j, b):
                qn, kn, r = BLOCKS[b][1], sum(k[1] for k in keys_of(b)), b % 2
                act.wait_ge(masked_ready, NB * j + b + 1)
                for g in range(2):
                    act.activation(prob[0:qn, r, g, 0:kn], prob[0:qn, r, g, 0:kn], ACT.Exp,
                                   bias=soft[0:qn, r, 1, g:g + 1], accum_out=soft[0:qn, r, 3, g:g + 1])
                act.activation(soft[0:qn, r, 4, :], soft[0:qn, r, 2, :], ACT.Exp).then_inc(exp_ready, 1)

            def copy_prob_t(j, b):
                qn, r, kb = BLOCKS[b][1], b % 2, keys_of(b)
                act.wait_ge(pt_ready, NB * j + b + 1)
                src = bank[5][:, :].rearrange("p (g k q) -> p g k q", g=2, k=2)
                if b < NB - 1:
                    ins = act.activation(prob_t[:, r, :, 0:len(kb), :], src[:, :, 0:len(kb), :], ACT.Copy)
                else:
                    for i, k in enumerate(kb):
                        ins = act.activation(prob_t[0:k[1], r, :, i, 0:qn], src[0:k[1], :, i, 0:qn], ACT.Copy)
                ins.then_inc(pt_copied, 1)

            def copy_att_out(j, b):
                t, n = BLOCKS[b]
                act.wait_ge(pv_ready, NB * j + b + 1)
                act.activation(xm[:, 4 + j, t:t + n], bank[6][:, 0:n], ACT.Copy).then_inc(pv_copied, 1)

            def copy_ret_out(j, b):
                t, n = BLOCKS[b]
                act.wait_ge(ret_b_ready, NB * j + b + 1)
                act.activation(xm[:, j, t:t + n], bank[6][:, 0:n], ACT.Copy).then_inc(ret_o_copied, 1)

            def ret_squares(j, chunks):
                act.wait_ge(ret_o_copied, NB * j + NB)
                for c in chunks:
                    a, n = CHUNKS[c]
                    if c == 2:
                        act.wait_ge(sum_ready, 3 + 3 * j + 1)
                    if c != 1:
                        seal_waits(act)
                    act.activation(sq[:, c % 2, 0:n], xm[:, j, a:a + n], ACT.Square).then_inc(ret_sq_ready, 1)

            def ret_roots(j, chunks):
                for c in chunks:
                    root(3 + 3 * j + c, c, P)

            def mix_hi(c, span):
                a, n = CHUNKS[c]
                if span[0] == 3:
                    act.wait_ge(pv_copied, NB * (HEADS - 1) + (3, 6, 9)[c])
                for k in MIX_ORDER[span[0]:span[1]]:
                    act.activation(act_hl[:, 0, k, a:a + n], xm[:, k, a:a + n], ACT.Copy).then_inc(mix_hi_ready, 1)

            def head(j, last):
                n_units = N_HEAD - last
                dst = [(rq, ACT.Copy, 1.0), (rk, ACT.Copy, RET_SCALE), (rv, ACT.Copy, 1.0), (rg, ACT.Silu, 1.0),
                       (aq, ACT.Copy, ATT_SCALE)]
                for p in range(n_units):
                    mixing = last and p == n_units - 1
                    for c in range(3):
                        s = 3 * p + c
                        if s == 13:
                            ret_squares(j, (0, 1))
                        if s == 14:
                            ret_squares(j, (2,))
                            ret_roots(j, (0, 1))
                        if 2 <= s <= NB + 1:
                            copy_att_out(j, s - 2)
                        if s < NB:
                            exps(j, s)
                        if 1 <= s <= NB:
                            copy_prob_t(j, s - 1)
                        if mixing and c == 0:
                            split_weights(UNIT_OUT + 1, [UNIT_OUT + 1])
                        for step in (3 * s, 3 * s + 1):
                            if step in RET_PE_STEP[1:]:
                                copy_ret_out(j, RET_PE_STEP[1:].index(step))
                                if mixing:
                                    mix_hi(c - 1, (3, 5) if step == 3 * s else (5, 7))
                        evac(3 * head_unit(j, p) + c, c, *dst[p])
                        if 3 * s + 2 in RET_PE_STEP[1:]:
                            copy_ret_out(j, RET_PE_STEP[1:].index(3 * s + 2))
                        if mixing:
                            mix_hi(c, (0, 3))
                    if not mixing:
                        like = [head_unit(j, p) + 2] if last else [head_unit(i, p) + 2 for i in range(HEADS - 1)]
                        split_weights(head_unit(j, p) + 2, like, j)
                if last:
                    copy_ret_out(j, NB - 3)
                    mix_hi(2, (3, 5))
                    copy_ret_out(j, NB - 2)
                    mix_hi(2, (5, 7))
                    copy_ret_out(j, NB - 1)
                    ret_squares(j, (0, 1, 2))
                    ret_roots(j, (0, 1, 2))
                    for c in range(3):
                        act.wait_ge(norm_applied, 3 + 3 * j + c + 1)
                        mix_hi(c, (7, 8))
                else:
                    ret_roots(j, (2,))
                act.wait_ge(state_ready, NB * j + NB)
                act.dma_start(p_state[j], state[:, :]).then_inc(state_stored, 16)
                act.dma_start(s_state[j], state_new[:, :]).then_inc(state_stored, 16)

            with act.Fori(0, HEADS - 1) as j:
                head(j, 0)
            head(HEADS - 1, 1)

            for r in range(3 * N_OUT):
                o, c = OUT_ORDER[r]
                a, n = CHUNKS[c]
                act.wait_ge(dve_evac, r + 1)
                square(xm[:, o, a:a + n], 3 * KT + r, r % 2)
                if r in (18, 21):
                    root(15 + (r - 18) // 3, (r - 18) // 3, D)
                if r in OUT_SPLITS:
                    split_weights(OUT_SPLITS[r], [OUT_SPLITS[r]])
                for item in NORM2_ITEMS.get(r, ()):
                    shift_and_split(3 * KT + item, item // KT, item % KT, 24)
                    if item == 2 * KT - 1:
                        root(17, 2, D)

            def up_pair(f, t, par, unit, like, i=0):
                if not isinstance(f, int) or f > 0:
                    act.wait_ge(conv_ready, f)
                for c in range(3):
                    act.wait_ge(gemm_ready, ffn_chunk(f, 0, c))
                    for o, tok, n, part in pieces(c):
                        ins = act.activation(gate_ext[:, 2 + tok + 2 * part:2 + tok + 2 * part + n],
                                             bank[c][:, o:o + n], ACT.Copy)
                    ins.then_inc(act_evac, 1)
                act.activation(gate_ext[:, S_PROMPT + 2:S_PROMPT + 4], conv_st_sb[:, f, :], ACT.Copy).then_inc(ext_ready, 1)
                act.wait_ge(act_evac, 66 + 3 * f + 3)
                seal_waits(act)
                last_rows = gate_ext[:, T + 4 - 2 * 66:T + 4].rearrange("p (s r) -> p s r", s=2)[:, :, 64:66]
                act.activation(conv_out[:, f, :].rearrange("p (s r) -> p s r", s=2), last_rows,
                               ACT.Copy).then_inc(ext_ready, 1)
                split_weights(unit + 2, like[0], i)
                act.wait_ge(conv_ready, f + 1)
                act.activation(conv[:, :], conv[:, :], ACT.Silu).then_inc(silu_ready, 1)
                split_weights(unit + 3, like[1], i)
                for c in range(3):
                    a, n = CHUNKS[c]
                    act.wait_ge(uf_ready, 3 * f + c + 1)
                    act.activation(u_hl[:, par, t, 0, a:a + n], hf[:, c, 0:n], ACT.Copy).then_inc(u_hi_ready, 1)

            for t in range(2):
                n = UNIT_FFN + 2 * t
                up_pair(t, t, 0, n, ([n + 2], [n + 3]))
            with act.Fori(0, (GROUPS - 1) // 2) as i:
                reps = range((GROUPS - 1) // 2)
                for h in range(2):
                    at = UNIT_FFN + 4 + 6 * h
                    for t in range(2):
                        likes = [[at + 2 * t + q + 12 * k for k in reps] for q in (2, 3)]
                        up_pair(2 + 4 * i + 2 * h + t, t, 1 - h, at + 2 * t + 12 * i, likes, i)
                    for q in (6, 7):
                        split_weights(at + q + 12 * i, [at + q + 12 * k for k in reps], i)
            def shift(item):
                c, k = divmod(item, KT)
                act.wait_ge(normed_ready, item + 1)
                for o, tok, m, part in pieces(c):
                    y = xm[:, k, tok:tok + m]
                    ins = act.activation(y, y, ACT.Identity, bias=mod[:, 48 + 2 * k + 1, part:part + 1])
                ins.then_inc(y_ready, 1)

            for r in range(3 * KT):
                c, k = divmod(r, KT)
                a, n = CHUNKS[c]
                act.wait_ge(down_free, 4 + 24 * (GROUPS - 1) + r + 1)
                square(xm[:, k, a:a + n], 6 * KT + r, k % 2)
                if r % KT == FINAL_SUM_AT and r > KT:
                    root(18 + c - 1, c - 1, D, 7)
                if r >= FINAL_LAG:
                    shift(r - FINAL_LAG)
            root(20, 2, D, 7)
            for item in range(3 * KT - FINAL_LAG, 3 * KT):
                shift(item)

        @block.gpsimd
        def _(pool):
            def split_weights(n, like):
                slot = SLOTS[like[0]]
                pool.wait_ge(wh_ready, n + 1)
                pool.tensor_tensor(w_hl[:, slot, 1], w_raw[:, slot], w_hl[:, slot, 0].bitcast(F32),
                                   ALU.subtract).then_inc(wl_ready, 1)

            def add_square(item, ring, first, dst):
                pool.wait_ge(sq_ready, item + 1)
                src = sq[:, ring, 0:dst.shape[-1]]
                if first:
                    ins = pool.tensor_copy(dst, src)
                else:
                    ins = pool.tensor_tensor(dst, dst, src, ALU.add)
                ins.then_inc(sq_used, 1)

            def split_hf(item, c, k):
                a, n = CHUNKS[c]
                pool.wait_ge(hi_ready, item + 1)
                pool.tensor_tensor(act_hl[:, 1, k, a:a + n], hf[:, item % 3, 0:n],
                                   act_hl[:, 0, k, a:a + n].bitcast(F32), ALU.subtract).then_inc(lo_ready, 1)

            pool.memset(ones[:, :], 1.0).then_inc(pool_const, 1)
            pool.memset(eps_sb[:, :], EPS).then_inc(pool_const, 1)
            for n in range(3):
                split_weights(n, [n])
            for k in range(KT):
                for c in range(3):
                    split_hf(3 * k + c, c, k)
            for n in (3, 4):
                split_weights(n, [n])

            def decay_q(j):
                pool.wait_ge(act_evac, 3 * head_unit(j, 0) + 3)
                pool.wait_ge(ret_tab_loaded, 32 * (j + 1))
                dec = rtab[:, RT_Q:RT_Q + P]
                pool.tensor_tensor(acc[:, 0:S_PROMPT].rearrange("p (b l) -> p b l", b=8),
                                   rq[:, 0:S_PROMPT].rearrange("p (b l) -> p b l", b=8),
                                   dec.unsqueeze(1).broadcast_to([P, 8, P]), ALU.mult).then_inc(qdec_ready, 1)
                pool.tensor_tensor(acc[:, S_PROMPT:T], rq[:, S_PROMPT:T], dec[:, 0:S_SAMPLE],
                                   ALU.mult).then_inc(qdec_ready, 1)

            with pool.Fori(0, HEADS - 1) as j:
                for p in range(N_HEAD):
                    split_weights(head_unit(j, p) + 2, [head_unit(0, p) + 2])
                    if p == 0:
                        decay_q(j)
            for p in range(N_HEAD - 1):
                split_weights(head_unit(HEADS - 1, p) + 2, [head_unit(HEADS - 1, p) + 2])
                if p == 0:
                    decay_q(HEADS - 1)
            for c in range(3):
                a, n = CHUNKS[c]
                for i, k in enumerate(MIX_ORDER[:2]):
                    pool.wait_ge(mix_hi_ready, 7 * c + i + 1)
                    pool.tensor_tensor(act_hl[:, 1, k, a:a + n], xm[:, k, a:a + n], act_hl[:, 0, k, a:a + n].bitcast(F32),
                                       ALU.subtract).then_inc(mix_lo_pool, 1)

            for r in range(3 * N_OUT):
                o, c = OUT_ORDER[r]
                a, n = CHUNKS[c]
                if o > 0:
                    pool.wait_ge(sq_used, 3 * KT + r)
                add_square(3 * KT + r, r % 2, o == 0, acc[:, a:a + n])
                if r in OUT_SPLITS:
                    split_weights(OUT_SPLITS[r], [OUT_SPLITS[r]])
                for item in NORM2_ITEMS.get(r, ()):
                    split_hf(3 * KT + item, item // KT, item % KT)
            pool.memset(gate_ext[:, 0:2], 0.0).then_inc(pool_const, 1)

            def up_pair(f, t, par, unit, like):
                split_weights(unit + 2, like[0])
                split_weights(unit + 3, like[1])
                for c in range(3):
                    a, n = CHUNKS[c]
                    pool.wait_ge(u_hi_ready, 3 * f + c + 1)
                    pool.tensor_tensor(u_hl[:, par, t, 1, a:a + n], hf[:, c, 0:n],
                                       u_hl[:, par, t, 0, a:a + n].bitcast(F32), ALU.subtract).then_inc(u_lo_ready, 1)

            for t in range(2):
                n = UNIT_FFN + 2 * t
                up_pair(t, t, 0, n, ([n + 2], [n + 3]))
            with pool.Fori(0, (GROUPS - 1) // 2) as i:
                for h in range(2):
                    at = UNIT_FFN + 4 + 6 * h
                    for t in range(2):
                        up_pair(2 + 4 * i + 2 * h + t, t, 1 - h, at + 2 * t + 12 * i,
                                ([at + 2 * t + 2], [at + 2 * t + 3]))
                    for q in (6, 7):
                        split_weights(at + q + 12 * i, [at + q])
            for c in range(3):
                a, n = CHUNKS[c]
                for k in range(KT - (c == 2)):
                    if k > 0:
                        pool.wait_ge(sq_used, 6 * KT + KT * c + k)
                    add_square(6 * KT + KT * c + k, k % 2, k == 0, acc[:, a:a + n])

        @block.vector
        def _(dve):
            seq = [0]

            def then_wait(ins):
                seq[0] += 1
                ins.then_inc(dve_seq, 1)
                dve.wait_ge(dve_seq, seq[0])

            def in_loop_wait(ins, base, per, j, local):
                ins.then_inc(dve_seq, 1)
                dve.wait_ge(dve_seq, base + per * j + local)

            def ada_dots(m, load, place, part):
                dve.wait_ge(ada_loaded[place], 16 * load)
                for s in range(2):
                    if not isinstance(m, int) or m > 0 or s > 0:
                        dve.wait_ge(ada_used, 2 * m + s)
                    if not isinstance(m, int):
                        seal_waits(dve)
                    out = ada_place[place] if s else ada_out[:, :]
                    dve.tensor_tensor_reduce(out, ada_place[place], silu_c[:, s], 1.0, 0.0, ALU.mult, ALU.add,
                                             mod_part[:, part, s:s + 1]).then_inc(ada_used, 1)

            def add_ada_bias(m0, n, used, part=0):
                dve.wait_ge(ada_used, 2 * used)
                return dve.tensor_tensor(mod[:, bass.ds(m0, n), :], mod_part[:, part:part + n, :],
                                         b_ada_sb[:, bass.ds(m0, n)].unsqueeze(2).broadcast_to([P, n, 2]), ALU.add)

            def norm_scale(which, m0):
                return dve.scalar_tensor_tensor(scale_n[:, which], mod[:, m0:m0 + 16:2, :], 1.0,
                                                gains_sb[:, which].unsqueeze(2).broadcast_to([P, KT, 2]),
                                                ALU.add, ALU.mult)

            def invert(q, c):
                n = CHUNKS[c][1]
                dve.wait_ge(std_ready, q + 1)
                then_wait(dve.reciprocal(std[:, c, 0:n], std[:, c, 0:n]))

            def norm_tile(which, c, k, dst, ready):
                for o, tok, m, part in pieces(c):
                    ins = dve.scalar_tensor_tensor(dst[:, o:o + m], xm[:, k, tok:tok + m], scale_n[:, which, k, part:part + 1],
                                                   std[:, c, o:o + m], ALU.mult, ALU.mult)
                ins.then_inc(ready, 1)

            dve.wait_ge(silu_c_ready, 1)
            for m in range(6):
                ada_dots(m, 1, m, m)
                if m >= 3:
                    invert(m - 3, m - 3)
            dve.wait_ge(const_loaded, 16 * 5)
            for k in range(KT):
                if k >= 3:
                    for m in (2 * k, 2 * k + 1):
                        ada_dots(m, m // 8 + 1, m % 8, m % 8)
                then_wait(add_ada_bias(2 * k, 2, 2 * k + 2, 2 * k % 8))
                then_wait(dve.tensor_scalar(scale_n[:, 0, k, :], mod[:, 2 * k, :], 1.0, gains_sb[:, 0, k:k + 1],
                                            ALU.add, ALU.mult))
                for c in range(3):
                    if k > 0:
                        dve.wait_ge(lo_ready, 3 * k + c - 2)
                    norm_tile(0, c, k, hf[:, c], hf_ready)
            dve.wait_ge(hf_ready, 3 * KT)
            dve.sem_inc(norm_applied, 3)

            for b in range(NB):
                t, n = BLOCKS[b]
                dve.wait_ge(av_t_ready, b + 1)
                dve.tensor_copy(av_tok[0:n, b + (b == NB - 1), :], bank[(3, 6)[b % 2]][0:n, 0:P]).then_inc(av_tok_ready, 1)

            def mask_and_max(j, b):
                qn, kb, r = BLOCKS[b][1], keys_of(b), b % 2
                kn = sum(k[1] for k in kb)
                if b == 0:
                    dve.wait_ge(att_tab_loaded, 32 * (j + 1))
                if b >= 2:
                    dve.wait_ge(pt_ready, NB * j + b - 1)
                dve.wait_ge(qk_ready, NB * j + b + 1)
                seal_waits(dve)
                for g in range(2):
                    ins = dve.tensor_tensor_reduce(prob[0:qn, r, g, 0:kn], bank[3 + g][0:qn, 0:kn],
                                                   att_tab[0:qn, g, kb[0][2]:kb[0][2] + kn], 1.0, sink_sb[0:qn, g:g + 1],
                                                   ALU.add, ALU.max, soft[0:qn, r, 0, g:g + 1])
                chain(ins, j)
                dve.tensor_scalar(soft[0:qn, r, 1, :], soft[0:qn, r, 0, :], -1.0, None, ALU.mult)
                dve.tensor_tensor(soft[0:qn, r, 2, :], sink_sb[0:qn, :], soft[0:qn, r, 0, :],
                                  ALU.subtract).then_inc(masked_ready, 1)

            def normalise(j, b):
                qn, r = BLOCKS[b][1], b % 2
                kn = sum(k[1] for k in keys_of(b))
                dve.wait_ge(exp_ready, NB * j + b + 1)
                chain(dve.tensor_tensor(rden[0:qn, r, :], soft[0:qn, r, 3, :], soft[0:qn, r, 4, :], ALU.add), j)
                chain(dve.reciprocal(rden[0:qn, r, :], rden[0:qn, r, :]), j)
                for g in range(2):
                    ins = dve.tensor_scalar(prob[0:qn, r, g, 0:kn], prob[0:qn, r, g, 0:kn], rden[0:qn, r, g:g + 1],
                                            None, ALU.mult)
                ins.then_inc(prob_ready, 1)

            def take_block(j, b):
                n, r = BLOCKS[b][1], b % 2
                A = bank[3 + r]
                if b == 0:
                    dve.wait_ge(ret_tab_loaded, 32 * (j + 1))
                if b >= 2:
                    dve.wait_ge(ret_b_ready, NB * j + b - 1)
                dve.wait_ge(ret_a_ready, NB * j + b + 1)
                kd = RT_K + (b == NB - 1)
                dve.tensor_scalar(k_tok[0:n, r, :], A[0:n, 0:P], rtab[0:n, kd:kd + 1], None, ALU.mult)
                dve.tensor_copy(v_tok[0:n, r, :], A[0:n, P:2 * P])
                dve.tensor_tensor(s_dec[0:n, r, 0:n], A[0:n, 2 * P:2 * P + n], rtab[0:n, 0:n],
                                  ALU.mult).then_inc(ret_a_used, 1)

            def next_state(j, b):
                if b == 0:
                    dve.wait_ge(state_stored, 32 * j + 32)
                dve.wait_ge(ret_b_ready, NB * j + b + 1)
                if b == 0:
                    ins = dve.tensor_copy(state[:, :], bank[5][:, 0:P])
                elif b < NB - 1:
                    dve.wait_ge(state_ready, NB * j + b)
                    ins = dve.scalar_tensor_tensor(state[:, :], state[:, :], rtab[:, RT_K + 2:RT_K + 3],
                                                   bank[5][:, 0:P], ALU.mult, ALU.add)
                else:
                    ins = dve.scalar_tensor_tensor(state_new[:, :], state_in[:, :], rtab[:, RT_K + 3:RT_K + 4],
                                                   bank[5][:, 0:P], ALU.mult, ALU.add)
                ins.then_inc(state_ready, 1)

            def mix_lo(c, span):
                a, n = CHUNKS[c]
                for i in range(*span):
                    k = MIX_ORDER[i]
                    dve.wait_ge(mix_hi_ready, 7 * c + i + 1 if i < 7 else 21 + c + 1)
                    dve.tensor_tensor(act_hl[:, 1, k, a:a + n], xm[:, k, a:a + n], act_hl[:, 0, k, a:a + n].bitcast(F32),
                                      ALU.subtract).then_inc(mix_lo_ready, 1)

            PER_HEAD = 3 * NB + 7
            base = seq[0]
            local = [0]

            def chain(ins, j):
                local[0] += 1
                in_loop_wait(ins, base, PER_HEAD, j, local[0])

            def head(j, last):
                local[0] = 0
                def retention(k):
                    if k < NB:
                        take_block(j, k)
                    if k >= 1:
                        next_state(j, k - 1)

                for s in range(3 * (N_HEAD - last)):
                    if 1 <= s <= NB:
                        normalise(j, s - 1)
                    if s < NB:
                        mask_and_max(j, s)
                    if 1 <= s <= 8:
                        ada_dots(16 + s - 1 + 8 * j, 2 + (s - 1) // 2 + 1 + 4 * j, (s - 1) % 2, s - 1)
                    if s == NB:
                        chain(add_ada_bias(16 + 8 * j, 8, 16 + 8 * j + 8), j)
                    for k in range(NB + 1):
                        if RET_PE_STEP[k] // 3 == s:
                            retention(k)
                            if last and k in MIX_LO_AFTER:
                                mix_lo(*MIX_LO_AFTER[k])
                for k in range(7, NB + 1) if last else ():
                    retention(k)
                    mix_lo(*MIX_LO_AFTER[k])
                dve.wait_ge(act_evac, 3 * head_unit(j, 3) + 3)
                for c in range(3):
                    a, n = CHUNKS[c]
                    dve.wait_ge(std_ready, 3 + 3 * j + c + 1)
                    chain(dve.reciprocal(std[:, c, 0:n], std[:, c, 0:n]), j)
                    if last and c > 0:
                        mix_lo(c - 1, (7, 8))
                    out = xm[:, j, a:a + n]
                    chain(dve.tensor_tensor(out, out, std[:, c, 0:n], ALU.mult), j)
                    dve.tensor_tensor(out, out, rg[:, a:a + n], ALU.mult).then_inc(norm_applied, 1)
                if last:
                    mix_lo(2, (7, 8))
                assert local[0] == PER_HEAD, local[0]

            with dve.Fori(0, HEADS - 1) as j:
                head(j, 0)
            head(HEADS - 1, 1)
            seq[0] = base + PER_HEAD * HEADS

            then_wait(norm_scale(1, 24))

            for r in range(3 * N_OUT):
                o, c = OUT_ORDER[r]
                if r < 3:
                    dve.wait_ge(x_again[c], 32)
                if r == 9:
                    dve.wait_ge(x_tile_again, 16)
                dve.wait_ge(gemm_ready, 66 + r + 1)
                for off, tok, m, part in pieces(c):
                    x = xm[:, o, tok:tok + m]
                    ins = dve.scalar_tensor_tensor(x, bank[r % 3][:, off:off + m], mod[:, 16 + o, part:part + 1],
                                                   x, ALU.mult, ALU.add)
                ins.then_inc(dve_evac, 1)
                if r < 16:
                    ada_dots(48 + r, 18 + r // 2 + 1, r % 2, r % 8)
                    if r % 8 == 7:
                        then_wait(add_ada_bias(48 + r - 7, 8, 48 + r + 1))
                for item in NORM2_ITEMS.get(r, ()):
                    c, k = divmod(item, KT)
                    if k == 0:
                        invert(15 + c, c)
                    dve.wait_ge(lo_ready, 3 * KT + item - 2)
                    norm_tile(1, c, k, hf[:, item % 3], hf_ready)
                    if k == KT - 1:
                        dve.wait_ge(hf_ready, 3 * KT + item + 1)
                        dve.sem_inc(norm_applied, 1)
            then_wait(norm_scale(2, 48))

            def up_pair(f, t, n_ext, local0, i, base_seq, per):
                dve.wait_ge(ext_ready, 2 * n_ext + 2)
                w = conv_wb_sb[:, bass.ds(f, 1), :]
                ins = dve.tensor_scalar(conv[:, :], gate_ext[:, 0:T + 2], w[:, 0, 0:1], w[:, 0, 3:4], ALU.mult, ALU.add)
                in_loop_wait(ins, base_seq, per, i, local0 + 1)
                ins = dve.scalar_tensor_tensor(conv[:, :], gate_ext[:, 1:T + 3], w[:, 0, 1:2], conv[:, :], ALU.mult, ALU.add)
                in_loop_wait(ins, base_seq, per, i, local0 + 2)
                dve.scalar_tensor_tensor(conv[:, :], gate_ext[:, 2:T + 4], w[:, 0, 2:3], conv[:, :], ALU.mult,
                                         ALU.add).then_inc(conv_ready, 1)
                dve.wait_ge(silu_ready, f + 1)
                for c in range(3):
                    dve.wait_ge(gemm_ready, ffn_chunk(f, 1, c))
                    src = bank[3 + c if isinstance(f, int) and f == 0 else c]
                    if not isinstance(f, int) or f > 0:
                        dve.wait_ge(u_lo_ready, 3 * f + c - 2)
                    for off, tok, m, part in pieces(c):
                        ins = dve.tensor_tensor(hf[:, c, off:off + m], conv[:, tok + 2 * part:tok + 2 * part + m],
                                                src[:, off:off + m], ALU.mult)
                    ins.then_inc(uf_ready, 1)

            def down_tile(g, r, o, c):
                dve.wait_ge(down_ready, 24 * g + r + 1)
                for off, tok, m, part in pieces(c):
                    x = xm[:, o, tok:tok + m]
                    ins = dve.scalar_tensor_tensor(x, bank[3 + r % 4][:, off:off + m], mod[:, 40 + o, part:part + 1],
                                                   x, ALU.mult, ALU.add)
                ins.then_inc(down_free, 1)

            dve.sem_inc(down_free, 4)
            dve.wait_ge(pool_const, 3)
            for t in range(2):
                up_pair(t, t, t, 2 * t, 0, seq[0], 0)
            seq[0] += 4
            base_ffn = seq[0]
            with dve.Fori(0, (GROUPS - 1) // 2) as i:
                for h in range(2):
                    for t in range(2):
                        f = 2 + 4 * i + 2 * h + t
                        up_pair(f, t, f, 4 * h + 2 * t, i, base_ffn, 8)
                    for o in range(KT):
                        for c in range(3):
                            down_tile(2 * i + h, 3 * o + c, o, c)
            seq[0] = base_ffn + 8 * ((GROUPS - 1) // 2)
            def final_tile(item):
                c, k = divmod(item, KT)
                if k == 0:
                    invert(18 + c, c)
                a, n = CHUNKS[c]
                dve.wait_ge(sq_ready, 6 * KT + item + 1)
                norm_tile(2, c, k, xm[:, k, a:a + n], normed_ready)

            for r in range(3 * KT):
                c, o = divmod(r, KT)
                down_tile(GROUPS - 1, r, o, c)
                if r >= FINAL_LAG:
                    final_tile(r - FINAL_LAG)
            for item in range(3 * KT - FINAL_LAG, 3 * KT):
                final_tile(item)

        @block.tensor
        def _(pe):
            def sums(q, c, src):
                n = CHUNKS[c][1]
                if c == 2:
                    pe.wait_ge(std_ready, q - 1)
                    seal_waits(pe)
                pe.matmul(bank[SUM_BANK[c]][:, 0:n], ones[:, :], src[:, 0:n], start=True, stop=True).then_inc(sum_ready, 1)

            def unit(n, slot, wait_bank, between, order=range(KT), after_unit=True):
                pe.wait_ge(wl_ready, n + 1)
                for c in range(3):
                    a, m = CHUNKS[c]
                    wait_bank(c)
                    for pas, (w, x) in enumerate(((0, 0), (0, 1), (1, 0))):
                        for i, k in enumerate(order):
                            ins = pe.matmul(bank[c][:, 0:m], w_hl[:, slot, w, k, :], act_hl[:, x, k, a:a + m],
                                            start=(pas == 0 and i == 0), stop=(pas == 2 and i == KT - 1))
                            if after_unit and c == pas == i == 0:
                                ins.then_inc(unit_done, 1)
                        if pas == 2:
                            ins.then_inc(gemm_ready, 1)
                        between(3 * c + pas)

            def finish_unit(n):
                pe.wait_ge(gemm_ready, 3 * (n + 1))
                pe.sem_inc(unit_done, 1)

            pe.wait_ge(pool_const, 2)
            for c in range(3):
                a, n = CHUNKS[c]
                if c == 2:
                    pe.wait_ge(std_ready, 1)
                for k in range(KT):
                    pe.wait_ge(sq_ready, KT * c + k + 1)
                    ins = pe.matmul(bank[SUM_BANK[c]][:, 0:n], ones[:, :], sq[:, k % 2, 0:n], start=(k == 0),
                                    stop=(k == KT - 1))
                    ins.then_inc(sq_used, 1)
                pe.wait_ge(sq_used, KT * (c + 1))
                pe.sem_inc(sum_ready, 1)

            def after(n):
                def wait(c):
                    pe.wait_ge(act_evac, 3 * (n - 1) + c + 1)
                return wait

            def nothing(s):
                pass

            def values_by_token(s):
                t, n = BLOCKS[s]
                if s >= 2:
                    pe.wait_ge(av_tok_ready, s - 1)
                pe.transpose(bank[(3, 6)[s % 2]][0:n, 0:P], rv[:, t:t + n], ident[:, :]).then_inc(av_t_ready, 1)

            pe.wait_ge(wl_ready, 3)
            pe.wait_ge(std_ready, 3)
            for k in range(KT):
                jobs = [(u, c) for c in range(3) for u in range(3) if (u, c) != (2, 2)]
                for u, c in sorted(jobs) if k == KT - 1 else jobs:
                    a, m = CHUNKS[c]
                    pe.wait_ge(lo_ready, 3 * k + c + 1)
                    for pas, (w, x) in enumerate(((0, 0), (0, 1), (1, 0))):
                        ins = pe.matmul(bank[3 * u + c][:, 0:m], w_hl[:, SLOTS[u], w, k, :], act_hl[:, x, k, a:a + m],
                                        start=(k == pas == 0), stop=(k == KT - 1 and pas == 2))
                    if k == KT - 1:
                        ins.then_inc(gemm_ready, 1)
            pe.wait_ge(gemm_ready, 6)
            pe.sem_inc(unit_done, 2)
            pe.wait_ge(act_evac, 7)
            pe.wait_ge(const_loaded, 16 * 5)
            a, m = CHUNKS[2]
            for pas, (w, x) in enumerate(((0, 0), (0, 1), (1, 0))):
                for k in range(KT):
                    ins = pe.matmul(bank[0][:, 0:m], w_hl[:, SLOTS[2], w, k, :], act_hl[:, x, k, a:a + m],
                                    start=(k == pas == 0), stop=(k == KT - 1 and pas == 2))
                if pas == 2:
                    ins.then_inc(gemm_ready, 1)
                for b in range(3):
                    values_by_token(3 * pas + b)
            pe.wait_ge(act_evac, 9)
            finish_unit(2)

            def scores(j, b):
                t, n = BLOCKS[b]
                kb = keys_of(b)
                kn = sum(k[1] for k in kb)
                if b in (0, 2, 5):
                    pe.wait_ge(act_evac, 7 + (0, 2, 5).index(b) + 15 * j)
                if b == 0:
                    pe.wait_ge(av_tok_ready, NB)
                    pe.wait_ge(cache_loaded, 32)
                else:
                    pe.wait_ge(masked_ready, NB * j + b)
                    if b == NB - 1:
                        seal_waits(pe)
                for g in range(2):
                    h = slice(64 * g, 64 * g + 64)
                    ins = pe.matmul(bank[3 + g][0:n, 0:kn], aq[h, t:t + n], ak[h, kb[0][0]:kb[0][0] + kn],
                                    start=True, stop=True)
                ins.then_inc(qk_ready, 1)

            def transpose_prob(j, b):
                n, r, kb = BLOCKS[b][1], b % 2, keys_of(b)
                pe.wait_ge(prob_ready, NB * j + b + 1)
                if b > 0:
                    pe.wait_ge(pt_copied, NB * j + b)
                if b == NB - 1:
                    seal_waits(pe)
                for g in range(2):
                    at = 0
                    for i, k in enumerate(kb):
                        col = P * (2 * g + i)
                        ins = pe.transpose(bank[5][0:k[1], col:col + n], prob[0:n, r, g, at:at + k[1]], ident[0:n, 0:n])
                        at += k[1]
                ins.then_inc(pt_ready, 1)

            def weigh_values(j, b):
                n, r, kb = BLOCKS[b][1], b % 2, keys_of(b)
                pe.wait_ge(pt_copied, NB * j + b + 1)
                if b > 0:
                    pe.wait_ge(pv_copied, NB * j + b)
                else:
                    pe.wait_ge(std_ready, 3 + 3 * j)
                for g in range(2):
                    h = slice(64 * g, 64 * g + 64)
                    for i, k in enumerate(kb):
                        ins = pe.matmul(bank[6][h, 0:n], av_tok[0:k[1], k[3], h], prob_t[0:k[1], r, g, i, 0:n],
                                        start=(i == 0), stop=(i == len(kb) - 1))
                ins.then_inc(pv_ready, 1)

            def block_scores(j, b):
                t, n = BLOCKS[b]
                if b == 0:
                    pe.wait_ge(act_evac, 3 * head_unit(j, 2) + 3)
                    pe.wait_ge(masked_ready, NB * j + NB)
                if b >= 2:
                    pe.wait_ge(ret_a_used, NB * j + b - 1)
                if b == NB - 1:
                    seal_waits(pe)
                A = bank[3 + b % 2]
                pe.transpose(A[0:n, 0:P], rk[:, t:t + n], ident[:, :])
                pe.transpose(A[0:n, P:2 * P], rv[:, t:t + n], ident[:, :])
                pe.matmul(A[0:n, 2 * P:2 * P + n], rk[:, t:t + n], rq[:, t:t + n], start=True,
                          stop=True).then_inc(ret_a_ready, 1)

            def block_output(j, b):
                t, n = BLOCKS[b]
                r = b % 2
                if b == 0:
                    pe.wait_ge(qdec_ready, 2 * j + 2)
                    pe.wait_ge(pv_copied, NB * j + NB)
                else:
                    pe.wait_ge(ret_o_copied, NB * j + b)
                    pe.wait_ge(state_ready, NB * j + b)
                pe.wait_ge(ret_a_used, NB * j + b + 1)
                carried = state if b < NB - 1 else state_in
                if b == NB - 1:
                    pe.wait_ge(ret_tab_loaded, 32 * (j + 1))
                pe.matmul(bank[6][:, 0:n], v_tok[0:n, r, :], s_dec[0:n, r, 0:n], start=True, stop=(b == 0))
                if b > 0:
                    pe.matmul(bank[6][:, 0:n], carried[:, :], acc[:, t:t + n], start=False, stop=True)
                pe.matmul(bank[5][:, 0:P], k_tok[0:n, r, :], v_tok[0:n, r, :], start=True, stop=True).then_inc(ret_b_ready, 1)

            def ret_sums(j, c):
                pe.wait_ge(ret_sq_ready, 3 * j + c + 1)
                sums(3 + 3 * j + c, c, sq[:, c % 2, :])

            def head(j, last):
                def between(p):
                    def steps(i):
                        s = 9 * p + i
                        b = s // 3
                        if s % 3 == 0 and b < NB:
                            scores(j, b)
                        if s % 3 == 1 and 1 <= b <= NB:
                            transpose_prob(j, b - 1)
                        if s % 3 == 0 and 2 <= b <= NB + 1:
                            weigh_values(j, b - 2)
                        if s in RET_PE_STEP:
                            k = RET_PE_STEP.index(s)
                            if k < NB:
                                block_scores(j, k)
                            if k >= 1:
                                block_output(j, k - 1)
                        for c in RET_SUM_STEP.get(s, ()):
                            ret_sums(j, c)
                    return steps
                for p in range(N_HEAD - last):
                    unit(head_unit(j, p), HEAD_SLOTS[p], after(head_unit(j, p)), between(p), after_unit=p > 0)
                if last:
                    first_out_unit(between(N_HEAD - 1))
                else:
                    finish_unit(head_unit(j, N_HEAD - 1))

            def wait_mix(c, i):
                if i < 2:
                    pe.wait_ge(mix_lo_pool, 2 * c + i + 1)
                elif i < 7:
                    pe.wait_ge(mix_lo_ready, 5 * c + i - 1)
                else:
                    pe.wait_ge(mix_lo_ready, 15 + c + 1)

            def first_out_unit(between):
                pe.wait_ge(wl_ready, UNIT_OUT + 1)

                def tile(c, i):
                    a, m = CHUNKS[c]
                    wait_mix(c, i)
                    k = MIX_ORDER[i]
                    for pas, (w, x) in enumerate(((0, 0), (0, 1), (1, 0))):
                        ins = pe.matmul(bank[c][:, 0:m], w_hl[:, SLOTS[UNIT_OUT], w, k, :], act_hl[:, x, k, a:a + m],
                                        start=(i == pas == 0), stop=(i == KT - 1 and pas == 2))
                        if c == i == pas == 0:
                            ins.then_inc(unit_done, 1)
                    if i == KT - 1:
                        ins.then_inc(gemm_ready, 1)

                for c in range(3):
                    pe.wait_ge(act_evac, 63 + c + 1)
                    for t, tiles in enumerate(((0, 1), (2, 3), (4, 5, 6))):
                        for i in tiles:
                            tile(c, i)
                        between(3 * c + t)
                for c in range(3):
                    tile(c, KT - 1)

            with pe.Fori(0, HEADS - 1) as j:
                head(j, 0)
            head(HEADS - 1, 1)

            def after_out(o):
                def wait(c):
                    pe.wait_ge(dve_evac, 3 * o - 3 + c + 1)
                return wait

            with pe.Fori(0, 2) as i:
                for p in range(2):
                    unit(UNIT_OUT + 1 + p + 2 * i, SLOTS[UNIT_OUT + 1 + p], after_out(2 * i + 1 + p), nothing, MIX_ORDER)
            for r in range(15, 3 * N_OUT):
                o, c = OUT_ORDER[r]
                a, m = CHUNKS[c]
                if r in (19, 22):
                    pe.wait_ge(sq_used, 3 * KT + r - 1)
                    sums(15 + (r - 19) // 3, (r - 19) // 3, acc[:, CHUNKS[(r - 19) // 3][0]:])
                if c == 0:
                    pe.wait_ge(wl_ready, UNIT_OUT + o + 1)
                pe.wait_ge(dve_evac, r - 2)
                for pas, (w, x) in enumerate(((0, 0), (0, 1), (1, 0))):
                    for i, k in enumerate(MIX_ORDER):
                        ins = pe.matmul(bank[r % 3][:, 0:m], w_hl[:, SLOTS[UNIT_OUT + o], w, k, :],
                                        act_hl[:, x, k, a:a + m], start=(pas == i == 0), stop=(pas == 2 and i == KT - 1))
                        if pas == i == 0 and r in (15, 22, 23):
                            ins.then_inc(unit_done, 1)
                ins.then_inc(gemm_ready, 1)

            for r, (h, c, at) in enumerate(((0, 0, 0), (0, 1, 1), (1, 0, 3), (1, 1, 4), (0, 2, 2), (1, 2, 5))):
                a, m = CHUNKS[c]
                n = UNIT_FFN + h
                pe.wait_ge(wl_ready, n + 1)
                if h == 0:
                    pe.wait_ge(dve_evac, 3 * N_OUT - 2 + c)
                if r == 1:
                    pe.wait_ge(sq_used, 3 * KT + 3 * N_OUT)
                    sums(17, 2, acc[:, CHUNKS[2][0]:])
                for i, k in enumerate(range(KT)):
                    pe.wait_ge(lo_ready, 3 * KT + KT * c + k + 1)
                    for pas, (w, x) in enumerate(((0, 0), (0, 1), (1, 0))):
                        ins = pe.matmul(bank[at][:, 0:m], w_hl[:, SLOTS[n], w, k, :], act_hl[:, x, k, a:a + m],
                                        start=(k == pas == 0), stop=(k == KT - 1 and pas == 2))
                        if k == pas == 0 and r in (0, 5):
                            ins.then_inc(unit_done, 1)
                ins.then_inc(gemm_ready, 1)

            def ffn_unit(n, f, f_before, is_up, slot, units_before):
                pe.wait_ge(wl_ready, n + 1)
                for c in range(3):
                    a, m = CHUNKS[c]
                    if is_up:
                        pe.wait_ge(act_evac, 66 + 3 * f + c + 1)
                    elif f_before is None:
                        pe.wait_ge(act_evac, 66 + c + 1)
                    else:
                        pe.wait_ge(uf_ready, 3 * f_before + c + 1)
                    for pas, (w, x) in enumerate(((0, 0), (0, 1), (1, 0))):
                        for k in range(KT):
                            ins = pe.matmul(bank[c][:, 0:m], w_hl[:, slot, w, k, :], act_hl[:, x, k, a:a + m],
                                            start=(pas == 0 and k == 0), stop=(pas == 2 and k == KT - 1))
                            if c == pas == 0 and k < units_before:
                                ins.then_inc(unit_done, 1)
                    ins.then_inc(gemm_ready, 1)

            def final_sums(c):
                a, m = CHUNKS[c]
                last = c == 2
                if c > 0:
                    pe.wait_ge(std_ready, 18 + c)
                pe.wait_ge(sq_used, 6 * KT + KT * (c + 1) - last)
                ins = pe.matmul(bank[7][:, 0:m], ones[:, :], acc[:, a:a + m], start=True, stop=not last)
                if last:
                    pe.wait_ge(sq_ready, 9 * KT)
                    ins = pe.matmul(bank[7][:, 0:m], ones[:, :], sq[:, (KT - 1) % 2, 0:m], start=False, stop=True)
                ins.then_inc(sum_ready, 1)

            def down(g, n, slots, par, order, final=False):
                pe.wait_ge(wl_ready, n + 2)
                pe.wait_ge(u_lo_ready, 6 * g + 6)
                for r, (o, c) in enumerate(order):
                    a, m = CHUNKS[c]
                    if final and o == FINAL_SUM_AT and c > 0:
                        final_sums(c - 1)
                    pe.wait_ge(down_free, 24 * g + r + 1)
                    i = 0
                    for t in range(2):
                        for w, x in ((0, 0), (0, 1), (1, 0)):
                            ins = pe.matmul(bank[3 + r % 4][:, 0:m], w_hl[:, slots[t], w, o, :],
                                            u_hl[:, par, t, x, a:a + m], start=(i == 0), stop=(i == 5))
                            if r == i == 0 and not final:
                                ins.then_inc(unit_done, 1)
                            i += 1
                    ins.then_inc(down_ready, 1)

            tile_order = [(o, c) for o in range(KT) for c in range(3)]
            ffn_unit(UNIT_FFN + 2, 1, None, 0, SLOTS[UNIT_FFN + 2], 1)
            ffn_unit(UNIT_FFN + 3, 1, None, 1, SLOTS[UNIT_FFN + 3], 0)
            with pe.Fori(0, (GROUPS - 1) // 2) as i:
                for h in range(2):
                    at = UNIT_FFN + 4 + 6 * h
                    for t in range(2):
                        for b in range(2):
                            ffn_unit(at + 2 * t + b + 12 * i, 2 + 4 * i + 2 * h + t, 1 + 2 * h + t + 4 * i, b, SLOTS[at + 2 * t + b],
                                     2 if t == b == 0 else 1)
                    down(2 * i + h, at + 4 + 12 * i, SLOTS[at + 4:at + 6], h, tile_order)
            pe.wait_ge(down_ready, 24 * (GROUPS - 1))
            pe.sem_inc(unit_done, 2)
            n = N_UNITS - 2
            down(GROUPS - 1, n, SLOTS[n:n + 2], 0, [(o, c) for c in range(3) for o in range(KT)], True)
            final_sums(2)


MIX_ORDER = [4, 5, 6, 7, 0, 1, 2, 3]
RET_PE_STEP = [28] + list(range(30, 39))
RET_SUM_STEP = {41: (0, 1), 43: (2,)}
MIX_LO_AFTER = {2: (0, (2, 4)), 3: (0, (4, 7)), 4: (1, (2, 4)), 5: (1, (4, 5)), 6: (1, (5, 7)), 7: (2, (2, 3)),
                8: (2, (3, 5)), 9: (2, (5, 7))}
OUT_ORDER = [(o, c) for o in range(5) for c in range(3)] + [(o, c) for c in range(3) for o in range(5, N_OUT)]
OUT_SPLITS = {2: UNIT_OUT + 2, 5: UNIT_OUT + 3, 8: UNIT_OUT + 4, 9: UNIT_OUT + 5, 11: UNIT_OUT + 6, 14: UNIT_OUT + 7,
              21: UNIT_FFN, 22: UNIT_FFN + 1}
NORM2_ITEMS = {19: (0, 1), 20: (2, 3, 4), 21: (5, 6, 7), 22: (8, 9), 23: tuple(range(10, 3 * KT))}
FINAL_SUM_AT = 4
FINAL_LAG = KT + FINAL_SUM_AT + 2


def constants():
    q = np.arange(P)[:, None]
    k = np.arange(2 * P)[None, :]
    dist = np.abs(P + q - k).astype(np.float64)
    valid = np.where(q < 64, k < 192, k >= 64)
    slopes = 2.0 ** -np.arange(1, 9)
    bias = np.where(valid[None], -slopes[:, None, None] * dist[None], MASKED).astype(np.float32)
    att_bias = np.stack([np.concatenate([bias[j], bias[j + 4]], axis=1) for j in range(HEADS)])
    lg = np.log1p(-2.0 ** (-5.0 - np.arange(HEADS)))
    tab = np.zeros((HEADS, P, RT_COLS))
    i = np.arange(P)
    for h in range(HEADS):
        diff = i[None, :] - i[:, None]
        tab[h, :, RT_DECAY:RT_DECAY + P] = np.where(diff >= 0, np.exp(lg[h] * np.maximum(diff, 0)), 0.0)
        tab[h, :, RT_Q:RT_Q + P] = np.exp(lg[h] * (i[None, :] + 1.0))
        tab[h, :, RT_K] = np.exp(lg[h] * (P - 1.0 - i))
        tab[h, :64, RT_K + 1] = np.exp(lg[h] * (63.0 - i[:64]))
        tab[h, :, RT_K + 2] = np.exp(lg[h] * P)
        tab[h, :, RT_K + 3] = np.exp(lg[h] * 64)
    return np.eye(P, dtype=np.float32), att_bias, tab.astype(np.float32)


def unit_of(w):
    return w.reshape(KT, P, P).transpose(1, 0, 2).reshape(P, D)


def kernel(**inputs):
    import numpy as _np
    import concourse.bacc as _bacc
    from concourse import mybir as _mybir
    from concourse.bass_utils import run_bass_kernel_spmd as _run

    x = {k: _np.asarray(v) for k, v in inputs.items()}
    w_in, w_out, w_up, w_down = x["w_in"][0], x["w_out"][0], x["w_up"][0], x["w_down"][0]
    aq0, ak0, av0 = 2048, 2560, 2688

    def aq_cols(j):
        return _np.concatenate([w_in[:, aq0 + 64 * h:aq0 + 64 * h + 64] for h in (j, j + 4)], axis=1)

    units = [w_in[:, ak0:ak0 + P], w_in[:, av0:av0 + P], aq_cols(0)]
    for j in range(HEADS):
        units += [w_in[:, 512 * g + P * j:512 * g + P * (j + 1)] for g in range(4)]
        if j < HEADS - 1:
            units.append(aq_cols(j + 1))
    rows = list(range(512)) + [512 + 64 * h + i for j in range(HEADS) for h in (j, j + 4) for i in range(64)]
    w_out = w_out[rows]
    units += [w_out[:, P * o:P * (o + 1)] for o in range(N_OUT)]
    units = [unit_of(u) for u in units]

    def up(g):
        out = []
        for f in (2 * g, 2 * g + 1):
            out += [unit_of(w_up[:, P * f:P * (f + 1)]), unit_of(w_up[:, D_FF + P * f:D_FF + P * (f + 1)])]
        return out

    def down(g):
        return [w_down[P * f:P * (f + 1)] for f in (2 * g, 2 * g + 1)]

    units += up(0)
    for g in range(GROUPS - 1):
        units += up(g + 1) + down(g)
    units += down(GROUPS - 1)

    w_all = _np.concatenate([x["w_ada"][0], x["w_ada_f"]], axis=1)
    b_all = _np.concatenate([x["b_ada"][0], x["b_ada_f"]])
    sh1, sc1, g1, sh2, sc2, g2, shf, scf = (D * i for i in range(8))
    cols = []
    for a, b in ((sc1, sh1), (g1, None), (sc2, sh2), (g2, None), (scf, shf)):
        for k in range(KT):
            cols += [a + P * k] + ([b + P * k] if b is not None else [])
    tiles = _np.stack([w_all[:, c:c + P].T for c in cols])
    biases = _np.stack([b_all[c:c + P] for c in cols], axis=1)

    def by_tile(a):
        return a.reshape(a.shape[0], -1, P).transpose(2, 1, 0)

    ident, att_bias, ret_tab = constants()
    arrays = {
        "x_t": _np.concatenate([x["x_prompt"][0], x["x_sample"][0]]).T,
        "w_units": _np.stack(units),
        "w_ada_t": tiles,
        "b_ada_t": biases,
        "cond_rows": _np.concatenate([x["c_prompt"], x["c_sample"]]),
        "gains": _np.stack([x["norm1_g"][0], x["norm2_g"][0], x["normf_g"]]).reshape(3, KT, P).transpose(2, 0, 1),
        "conv_wb": by_tile(_np.concatenate([x["conv_w"][0], x["conv_b"]])),
        "conv_st": by_tile(x["state_conv"][0, 0]),
        "sinks": x["attn_sinks"][0].reshape(2, HEADS).T,
        "ck_t": x["cache_k"].reshape(P, P).T,
        "cv": x["cache_v"].reshape(P, P),
        "st_in": x["state_ret"].reshape(HEADS, P, P),
        "identity": ident, "att_bias": att_bias, "ret_tab": ret_tab,
    }
    outs = {"y_t": (D, T), "p_state": (HEADS, P, P), "pk_t": (P, P), "pv": (P, P), "conv_out_t": (P, FT, 4),
            "s_state": (HEADS, P, P), "sk_t": (P, S_SAMPLE), "sv": (S_SAMPLE, P)}

    nc = _bacc.Bacc("TRN2", target_bir_lowering=False, num_devices=1, dynamic_dma_scratch_size=1024)
    arrays = {k: _np.ascontiguousarray(v) for k, v in arrays.items()}
    args = [nc.dram_tensor(f"in_{k}", v.shape, _mybir.dt.from_np(v.dtype), kind="ExternalInput").ap() for k, v in arrays.items()]
    args += [nc.dram_tensor(f"out_{k}", s, F32, kind="ExternalOutput").ap() for k, s in outs.items()]
    hymba_step(nc, *args)
    r = _run(nc, [{f"in_{k}": v for k, v in arrays.items()}], core_ids=[0]).results[0]
    r = {k: r[f"out_{k}"] for k in outs}

    y = r["y_t"].T
    conv_rows = r["conv_out_t"].transpose(2, 1, 0).reshape(2, 2, D_FF)
    return (y[None, :S_PROMPT], y[None, S_PROMPT:], r["p_state"][None, None],
            r["pk_t"].T.reshape(1, 1, P, 2, 64), r["pv"].reshape(1, 1, P, 2, 64), conv_rows[0][None, None],
            r["s_state"][None, None], r["sk_t"].T.reshape(1, 1, S_SAMPLE, 2, 64), r["sv"].reshape(1, 1, S_SAMPLE, 2, 64),
            conv_rows[1][None, None])
```

```python
from contextlib import ExitStack

import numpy as np

import concourse.bass as bass
from concourse import mybir

ALU = mybir.AluOpType
ACT = mybir.ActivationFunctionType
F32 = mybir.dt.float32
F32R = mybir.dt.float32r
BF16 = mybir.dt.bfloat16

P = 128
D = 1024
KT = D // P
S_PROMPT = 1024
S_SAMPLE = 64
T = S_PROMPT + S_SAMPLE
CHUNKS = [(0, 364), (364, 362), (726, 362)]
C2P = S_PROMPT - CHUNKS[2][0]
NB = 9
BLOCKS = [(P * b, P) for b in range(8)] + [(S_PROMPT, S_SAMPLE)]
HEADS = 4
D_FF = 2816
FT = D_FF // P
EPS = 1e-6
RET_SCALE = float(np.float32(128 ** -0.5))
ATT_SCALE = 64 ** -0.5
MASKED = -1e30

N_PRO, N_HEAD, N_OUT = 3, 5, 8
HEAD_SLOTS = [0, 1, 2, 0, 1]
UNIT_OUT = N_PRO + N_HEAD * HEADS - 1
UNIT_FFN = UNIT_OUT + N_OUT
GEMM_OUT, GEMM_FFN = 3 * UNIT_OUT, 3 * UNIT_FFN
GROUPS = FT // 2
N_UNITS = UNIT_FFN + 3 * FT
SLOTS = ([2, 0, 1] + HEAD_SLOTS * 3 + HEAD_SLOTS[:4] + [1] + [2, 0] * 2 + [1, 2, 0] + [1, 2, 0, 1] + [2, 0, 1] * 20
         + [2, 0])
assert len(SLOTS) == N_UNITS

RT_DECAY, RT_Q, RT_K, RT_COLS = 0, 128, 256, 260
N_MOD = 64


def unit_gap(units):
    gaps = []
    for n in units:
        before = [m for m in range(n) if SLOTS[m] == SLOTS[n]]
        if before:
            gaps.append(n - before[-1])
        else:
            return None
    return min(gaps)


def unit_loads(units, i):
    counts = [SLOTS[:n + 1].count(SLOTS[n]) for n in units]
    if len(counts) == 1:
        return counts[0]
    per = counts[1] - counts[0]
    assert counts == [counts[0] + per * k for k in range(len(counts))]
    return counts[0] + per * i


def hymba_step(nc, x_t, w_units, w_ada, b_ada, cond, gains, conv_wb, conv_st, sinks, ck_t, cv_in, st_in,
               ident_in, att_bias, ret_tab, y_t, p_state, pk_t, pv, p_conv, s_state, sk_t, sv):
    x_v = x_t.rearrange("(k p) t -> p k t", p=P)
    y_v = y_t.rearrange("(k p) t -> p k t", p=P)

    with ExitStack() as ctx:
        def sb(name, shape, dt=F32, at=ctx):
            return at.enter_context(nc.sbuf_tensor(name, shape, dt))

        def sem(name):
            return ctx.enter_context(nc.semaphore(name))

        act_hl = sb("act_hl", [P, 2, KT, T], F32R)
        w_hl = sb("w_hl", [P, 3, 2, KT, P], F32R)
        xm = sb("xm", [P, KT, T])
        w_raw = sb("w_raw", [P, 3, KT, P])
        ident = sb("ident", [P, P])
        ones = sb("ones", [P, P])
        sq = sb("sq", [P, 2, CHUNKS[0][1]])
        acc = sb("acc", [P, T])
        hf = sb("hf", [P, 3, CHUNKS[0][1]])
        std = sb("std", [P, 3, CHUNKS[0][1]])
        mod = sb("mod", [P, N_MOD, 2])
        mod_part = sb("mod_part", [P, 12, 2])
        scale_n = sb("scale_n", [P, 3, KT, 2])
        b_ada_sb = sb("b_ada_sb", [P, N_MOD])
        gains_sb = sb("gains_sb", [P, 3, KT])
        conv_wb_sb = sb("conv_wb_sb", [P, FT, 4])
        conv_st_sb = sb("conv_st_sb", [P, FT, 2])
        conv_out = sb("conv_out", [P, FT, 4])
        eps_sb = sb("eps_sb", [P, 1])
        sqrt_eps = sb("sqrt_eps", [P, 1])

        ada_w = sb("ada_w", [P, 2, D])
        ada_out = sb("ada_out", [P, D], BF16)
        silu_c = sb("silu_c", [P, 2, D])

        heads_phase = ExitStack()
        rq = sb("rq", [P, T], at=heads_phase)
        rk = sb("rk", [P, T], at=heads_phase)
        rv = sb("rv", [P, T], at=heads_phase)
        rg = sb("rg", [P, T], at=heads_phase)
        aq = sb("aq", [P, T], at=heads_phase)
        ak = sb("ak", [P, T + P], at=heads_phase)
        av_tok = sb("av_tok", [P, NB + 1, P], at=heads_phase)
        att_tab = sb("att_tab", [P, 2, 256], at=heads_phase)
        sink_sb = sb("sink_sb", [P, 2], at=heads_phase)
        rtab = sb("rtab", [P, RT_COLS], at=heads_phase)
        prob = sb("prob", [P, 2, 2, 256], at=heads_phase)
        prob_t = sb("prob_t", [P, 2, 2, 2, P], at=heads_phase)
        soft = sb("soft", [P, 2, 5, 2], at=heads_phase)
        rden = sb("rden", [P, 2, 2], at=heads_phase)
        k_tok = sb("k_tok", [P, 2, P], at=heads_phase)
        v_tok = sb("v_tok", [P, 2, P], at=heads_phase)
        s_dec = sb("s_dec", [P, 2, P], at=heads_phase)
        state = sb("state", [P, P], at=heads_phase)
        state_in = sb("state_in", [P, P], at=heads_phase)
        state_new = sb("state_new", [P, P], at=heads_phase)
        heads_phase.close()
        u_hl = sb("u_hl", [P, 2, 2, 2, T], F32R)
        gate_ext = sb("gate_ext", [P, T + 4])
        conv = sb("conv", [P, T + 2])

        bank = [ctx.enter_context(nc.psum_tensor(f"bank{i}", [P, 512], F32)) for i in range(8)]
        SUM_BANK = [7, 6, 7]
        X_SQ = [sq[:, 0], sq[:, 1], hf[:, 0], hf[:, 1]]
        X_SUM_BANK = [0, 1, 2]
        ada_place = [ada_w[:, 0], ada_w[:, 1]] + [t[:, 0:D] for t in (rk, rg, rq, rv, aq)]
        ada_pool_place = [ak[:, 0:D], prob[:].rearrange("p a b c -> p (a b c)")]
        H_RING = [hf[:, 0], hf[:, 1], hf[:, 2], sq[:, 0], sq[:, 1]]

        const_loaded = sem("const_loaded")
        cond_loaded = sem("cond_loaded")
        x_loaded = [sem(f"x_loaded{c}") for c in range(3)]
        x_again = [sem(f"x_again{c}") for c in range(3)]
        x_tile_again = sem("x_tile_again")
        ada_loaded = [sem(f"ada_loaded{r}") for r in range(7)]
        ada_pool_loaded = [sem(f"ada_pool_loaded{r}") for r in range(2)]
        w_loaded = [sem(f"w_loaded{slot}") for slot in range(3)]
        att_tab_loaded = sem("att_tab_loaded")
        ret_tab_loaded = sem("ret_tab_loaded")
        cache_loaded = sem("cache_loaded")
        stored = sem("stored")
        state_stored = sem("state_stored")
        silu_c_ready = sem("silu_c_ready")
        pool_const = sem("pool_const")
        dve_seq = sem("dve_seq")
        ada_used = sem("ada_used")
        ada_product = sem("ada_product")
        ada_summed = sem("ada_summed")
        sq_ready = sem("sq_ready")
        sq_used = sem("sq_used")
        sum_ready = sem("sum_ready")
        std_ready = sem("std_ready")
        norm_applied = sem("norm_applied")
        inv_ready = sem("inv_ready")
        x_inv_ready = sem("x_inv_ready")
        x_normed = sem("x_normed")
        x_scaled = sem("x_scaled")
        vec_ready = sem("vec_ready")
        normed_by_pool = sem("normed_by_pool")
        ret_scaled = sem("ret_scaled")
        hf_ready = sem("hf_ready")
        hi_ready = sem("hi_ready")
        lo_ready = sem("lo_ready")
        wh_ready = sem("wh_ready")
        wl_ready = sem("wl_ready")
        unit_done = sem("unit_done")
        gemm_ready = sem("gemm_ready")
        act_evac = sem("act_evac")
        dve_evac = sem("dve_evac")
        av_t_ready = sem("av_t_ready")
        av_tok_ready = sem("av_tok_ready")
        qk_ready = sem("qk_ready")
        masked_ready = sem("masked_ready")
        exp_ready = sem("exp_ready")
        prob_ready = sem("prob_ready")
        pt_ready = sem("pt_ready")
        pt_copied = sem("pt_copied")
        pv_ready = sem("pv_ready")
        pv_copied = sem("pv_copied")
        qdec_ready = sem("qdec_ready")
        ret_a_ready = sem("ret_a_ready")
        ret_a_used = sem("ret_a_used")
        ret_b_ready = sem("ret_b_ready")
        ret_o_copied = sem("ret_o_copied")
        state_ready = sem("state_ready")
        ret_sq_ready = sem("ret_sq_ready")
        mix_hi_ready = sem("mix_hi_ready")
        mix_lo_ready = sem("mix_lo_ready")
        mix_lo_pool = sem("mix_lo_pool")
        ext_ready = sem("ext_ready")
        conv_ready = sem("conv_ready")
        silu_ready = sem("silu_ready")
        uf_ready = sem("uf_ready")
        u_hi_ready = sem("u_hi_ready")
        u_lo_ready = sem("u_lo_ready")
        down_ready = sem("down_ready")
        down_free = sem("down_free")
        normed_ready = sem("normed_ready")
        y_ready = sem("y_ready")
        y_by_dve = sem("y_by_dve")
        waits_passed = sem("waits_passed")

        def head_unit(j, p):
            return N_PRO + N_HEAD * j + p

        def seal_waits(eng):
            eng.sem_inc(waits_passed, 1)

        def keys_of(b):
            if b == 0:
                return [(0, P, P, 0)]
            if b == NB - 1:
                return [(S_PROMPT, P, 0, 8), (S_PROMPT + P, S_SAMPLE, P, 9)]
            return [(P * (b - 1), P, 0, b - 1), (P * b, P, P, b)]

        def pieces(c):
            a, n = CHUNKS[c]
            if c < 2:
                return [(0, a, n, 0)]
            return [(0, a, C2P, 0), (C2P, S_PROMPT, S_SAMPLE, 1)]

        def ffn_chunk(f, is_up, c):
            if isinstance(f, int) and f == 0:
                return GEMM_FFN + ((1, 2, 5), (3, 4, 6))[is_up][c]
            return GEMM_FFN + 6 * f + 3 * is_up + c + 1

        block = ctx.enter_context(nc.Block())

        @block.sync
        def _(sp):
            def load_unit(n, like):
                gap = unit_gap(like)
                if gap is not None:
                    sp.wait_ge(wl_ready, n - gap + 1)
                slot = SLOTS[like[0]]
                sp.dma_start(w_raw[:, slot], w_units[n].rearrange("p (k m) -> p k m", k=KT)).then_inc(w_loaded[slot], 16)

            def load_ada(m, ring):
                sp.wait_ge(ada_used, 2 * (m - 2) + 2)
                sp.dma_start(ada_w[:, ring], w_ada[m]).then_inc(ada_loaded[ring], 16)

            def load_first_ada(m):
                if 12 <= m < 14:
                    sp.dma_start(ada_pool_place[m - 12], w_ada[m]).then_inc(ada_pool_loaded[m - 12], 16)
                    return
                nth = ADA_DVE.index(m)
                if nth >= 7:
                    sp.wait_ge(ada_used, 2 * (nth - 7) + 2)
                sp.dma_start(ada_place[nth % 7], w_ada[m]).then_inc(ada_loaded[nth % 7], 16)

            def load_x(c):
                a, n = CHUNKS[c]
                sp.dma_start(xm[:, :, a:a + n], x_v[:, :, a:a + n]).then_inc(x_loaded[c], 16)

            def load_head_tables(j):
                if not isinstance(j, int) or j > 0:
                    sp.wait_ge(prob_ready, NB * j)
                sp.dma_start(att_tab[:, :, :], att_bias[j].rearrange("p (g k) -> p g k", g=2)).then_inc(att_tab_loaded, 16)
                sp.dma_start(sink_sb[:, :], sinks[j].partition_broadcast(P)).then_inc(att_tab_loaded, 16)

            def load_ret_tables(j):
                if not isinstance(j, int) or j > 0:
                    sp.wait_ge(state_ready, NB * j)
                sp.dma_start(rtab[:, :], ret_tab[j]).then_inc(ret_tab_loaded, 16)
                sp.dma_start(state_in[:, :], st_in[j]).then_inc(ret_tab_loaded, 16)

            sp.dma_start(silu_c[:, :, :], cond.partition_broadcast(P)).then_inc(cond_loaded, 16)
            load_first_ada(0)
            load_first_ada(1)
            load_x(0)
            load_first_ada(2)
            load_first_ada(3)
            load_x(1)
            load_first_ada(12)
            load_first_ada(4)
            load_first_ada(5)
            load_x(2)
            load_unit(0, [0])
            load_first_ada(6)
            load_unit(1, [1])
            load_unit(2, [2])
            for dst, src in ((b_ada_sb, b_ada), (gains_sb, gains), (ident, ident_in), (conv_wb_sb, conv_wb),
                             (conv_st_sb, conv_st)):
                sp.dma_start(dst[:], src).then_inc(const_loaded, 16)
            for m in (7, 8, 13, 9, 10, 11, 14, 15):
                load_first_ada(m)
            sp.dma_start(ak[:, S_PROMPT:S_PROMPT + P], ck_t).then_inc(cache_loaded, 16)
            sp.dma_start(av_tok[:, 8, :], cv_in).then_inc(cache_loaded, 16)
            load_head_tables(0)
            load_ret_tables(0)
            load_unit(3, [3])
            load_unit(4, [4])

            def head_in_loop(j):
                for p in range(N_HEAD):
                    load_unit(head_unit(j, p) + 2, [head_unit(i, p) + 2 for i in range(HEADS - 1)])
                    for t in range(2) if p < 4 else ():
                        load_ada(16 + 8 * j + 2 * p + t, t)
                load_head_tables(j + 1)
                load_ret_tables(j + 1)

            with sp.Fori(0, HEADS - 1) as j:
                head_in_loop(j)
            j = HEADS - 1
            for p in range(N_HEAD - 1):
                load_unit(head_unit(j, p) + 2, [head_unit(j, p) + 2])
                for t in range(2):
                    load_ada(16 + 8 * j + 2 * p + t, t)

            load_unit(UNIT_OUT + 2, [UNIT_OUT + 2])
            for t in range(2):
                load_ada(48 + t, t)
            for c in range(3):
                a, n = CHUNKS[c]
                sp.wait_ge(mix_lo_ready, 5 * (c + 1))
                sp.wait_ge(mix_lo_pool, 2 * (c + 1))
                for k0, k1 in ((0, 3), (4, 8)):
                    sp.dma_start(xm[:, k0:k1, a:a + n], x_v[:, k0:k1, a:a + n]).then_inc(x_again[c], 16)
            sp.wait_ge(mix_lo_ready, 18)
            sp.dma_start(xm[:, 3, :], x_v[:, 3, :]).then_inc(x_tile_again, 16)
            for o in range(1, N_OUT):
                load_unit(UNIT_OUT + o + 2, [UNIT_OUT + o + 2])
                for t in range(2):
                    load_ada(48 + 2 * o + t, t)
            for p in range(4):
                load_unit(UNIT_FFN + p + 2, [UNIT_FFN + p + 2])
            with sp.Fori(0, (GROUPS - 1) // 2) as i:
                for p in range(12):
                    at = UNIT_FFN + 4 + p + 2
                    load_unit(at + 12 * i, [at + 12 * k for k in range((GROUPS - 1) // 2)])
            sp.wait_ge(ext_ready, 2 * FT)
            sp.dma_start(p_conv, conv_out[:, :, :]).then_inc(stored, 16)
            for c, k0, k1, by_act, by_dve in ((0, 0, 4, 4, 0), (0, 4, 8, 8, 0), (1, 4, 8, 12, 0), (1, 0, 4, 16, 0), (2, 0, 3, 16, 3),
                                              (2, 3, 5, 16, 5), (2, 5, 8, 19, 5)):
                a, n = CHUNKS[c]
                sp.wait_ge(y_ready, by_act)
                if by_dve:
                    sp.wait_ge(y_by_dve, by_dve)
                sp.dma_start(y_v[:, k0:k1, a:a + n], xm[:, k0:k1, a:a + n]).then_inc(stored, 16)
            sp.wait_ge(stored, 16 * 12)
            sp.wait_ge(state_stored, 32 * HEADS + 32)

        @block.scalar
        def _(act):
            def split_weights(n, like, i=0):
                act.wait_ge(w_loaded[SLOTS[like[0]]], 16 * unit_loads(like, i))
                gap = unit_gap(like)
                if gap is not None:
                    act.wait_ge(unit_done, n - gap + 1)
                slot = SLOTS[like[0]]
                act.activation(w_hl[:, slot, 0], w_raw[:, slot], ACT.Copy).then_inc(wh_ready, 1)

            def square(src, item, ring):
                n = src.shape[-1]
                if not isinstance(item, int) or item >= 2:
                    act.wait_ge(sq_used, item - 1)
                act.activation(sq[:, ring, 0:n], src, ACT.Square).then_inc(sq_ready, 1)

            def root(q, c, width, at=None):
                n = CHUNKS[c][1]
                act.wait_ge(sum_ready, q + 1)
                if not isinstance(q, int) or q >= 3:
                    act.wait_ge(norm_applied, q - 2)
                act.activation(std[:, c, 0:n], bank[at or SUM_BANK[c]][:, 0:n], ACT.Sqrt, bias=eps_sb[:, 0:1],
                               scale=1.0 / width).then_inc(std_ready, 1)

            def shift_and_split(item, c, k, m0):
                act.wait_ge(hf_ready, item - 3 * KT + 1)
                for dst in (act_hl[:, 0, k, :], None):
                    for o, tok, m, part in pieces(c):
                        h = hf[:, item % 3, o:o + m]
                        ins = act.activation(h if dst is None else dst[:, tok:tok + m], h, ACT.Identity,
                                             bias=mod[:, m0 + 2 * k + 1, part:part + 1])
                ins.then_inc(hi_ready, 1)

            def modulate_x(k, c):
                item = 3 * k + c
                if c == 0:
                    act.wait_ge(vec_ready, k + 1)
                    act.wait_ge(x_normed, k + 1)
                    if item >= 5:
                        act.wait_ge(lo_ready, item - 4)
                else:
                    act.wait_ge(x_scaled, 2 * k + c)
                for ring in (False, True):
                    for o, tok, m, part in pieces(c):
                        slot = H_RING[item % 5][:, o:o + m]
                        src = xm[:, k, tok:tok + m] if c == 0 else slot
                        ins = act.activation(slot if ring else act_hl[:, 0, k, tok:tok + m], src, ACT.Identity,
                                             bias=mod[:, 2 * k + 1, part:part + 1],
                                             scale=1.0 if c else scale_n[:, 0, k, part:part + 1])
                ins.then_inc(hi_ready, 1)

            act.sem_inc(state_stored, 32)
            act.wait_ge(pool_const, 2)

            def x_squares(c):
                a, n = CHUNKS[c]
                act.wait_ge(x_loaded[c], 16)
                for k in range(KT):
                    item = KT * c + k
                    if item >= 4:
                        act.wait_ge(sq_used, item - 3)
                    act.activation(X_SQ[item % 4][:, 0:n], xm[:, k, a:a + n], ACT.Square).then_inc(sq_ready, 1)

            def x_root(c):
                n = CHUNKS[c][1]
                act.wait_ge(sum_ready, c + 1)
                act.activation(std[:, c, 0:n], bank[X_SUM_BANK[c]][:, 0:n], ACT.Sqrt, bias=eps_sb[:, 0:1],
                               scale=1.0 / D).then_inc(std_ready, 1)

            def sum_ada(m):
                for s in range(2):
                    act.wait_ge(ada_product, 2 * (m - 12) + s + 1)
                    src = ada_pool_place[m - 12] if s else acc[:, 0:D]
                    act.activation(src, src, ACT.Copy, accum_out=mod_part[:, m - 4, s:s + 1]).then_inc(ada_summed, 1)

            act.wait_ge(cond_loaded, 16)
            act.activation(silu_c[:, :, :], silu_c[:, :, :], ACT.Silu).then_inc(silu_c_ready, 1)
            x_squares(0)
            x_root(0)
            x_squares(1)
            x_root(1)
            x_squares(2)
            split_weights(0, [0])
            x_root(2)
            split_weights(1, [1])
            split_weights(2, [2])
            sum_ada(12)
            act.wait_ge(sq_used, 3 * KT)
            for k in range(KT):
                for c in range(3):
                    modulate_x(k, c)
                if k == 4:
                    sum_ada(13)

            def evac(n_chunk, at, dst, func=ACT.Copy, scale=1.0):
                a, n = CHUNKS[(n_chunk if isinstance(n_chunk, int) else at) % 3]
                act.wait_ge(gemm_ready, n_chunk + 1)
                act.activation(dst[:, a:a + n], bank[at][:, 0:n], func, scale=scale).then_inc(act_evac, 1)

            for c in range(3):
                act.wait_ge(gemm_ready, c + 1)
                for o, t, n, part in pieces(c):
                    ins = act.activation(ak[:, t + P * part:t + P * part + n], bank[c][:, o:o + n], ACT.Copy)
                ins.then_inc(act_evac, 1)
            act.wait_ge(act_evac, 3)
            act.dma_start(pk_t, ak[:, S_PROMPT - P:S_PROMPT]).then_inc(stored, 16)
            act.dma_start(sk_t, ak[:, T + P - S_SAMPLE:T + P]).then_inc(stored, 16)
            for c in range(3):
                evac(3 + c, 3 + c, rv)
            split_weights(3, [3])
            for c in range(3):
                evac(6 + c, (6, 7, 0)[c], aq, scale=ATT_SCALE)
            split_weights(4, [4])
            act.wait_ge(av_tok_ready, NB)
            act.dma_start(pv, av_tok[:, 7, :]).then_inc(stored, 16)
            act.dma_start(sv, av_tok[0:S_SAMPLE, 9, :]).then_inc(stored, 16)

            def exps(j, b):
                qn, kn, r = BLOCKS[b][1], sum(k[1] for k in keys_of(b)), b % 2
                act.wait_ge(masked_ready, NB * j + b + 1)
                for g in range(2):
                    act.activation(prob[0:qn, r, g, 0:kn], prob[0:qn, r, g, 0:kn], ACT.Exp,
                                   bias=soft[0:qn, r, 1, g:g + 1], accum_out=soft[0:qn, r, 3, g:g + 1])
                act.activation(soft[0:qn, r, 4, :], soft[0:qn, r, 2, :], ACT.Exp).then_inc(exp_ready, 1)

            def copy_prob_t(j, b):
                qn, r, kb = BLOCKS[b][1], b % 2, keys_of(b)
                act.wait_ge(pt_ready, NB * j + b + 1)
                src = bank[5][:, :].rearrange("p (g k q) -> p g k q", g=2, k=2)
                if b < NB - 1:
                    ins = act.activation(prob_t[:, r, :, 0:len(kb), :], src[:, :, 0:len(kb), :], ACT.Copy)
                else:
                    for i, k in enumerate(kb):
                        ins = act.activation(prob_t[0:k[1], r, :, i, 0:qn], src[0:k[1], :, i, 0:qn], ACT.Copy)
                ins.then_inc(pt_copied, 1)

            def copy_att_out(j, b):
                t, n = BLOCKS[b]
                act.wait_ge(pv_ready, NB * j + b + 1)
                act.activation(xm[:, 4 + j, t:t + n], bank[6][:, 0:n], ACT.Copy).then_inc(pv_copied, 1)

            def copy_ret_out(j, b):
                t, n = BLOCKS[b]
                act.wait_ge(ret_b_ready, NB * j + b + 1)
                act.activation(xm[:, j, t:t + n], bank[6][:, 0:n], ACT.Copy).then_inc(ret_o_copied, 1)

            def ret_squares(j, chunks):
                act.wait_ge(ret_o_copied, NB * j + NB)
                for c in chunks:
                    a, n = CHUNKS[c]
                    if c == 2:
                        act.wait_ge(sum_ready, 3 + 3 * j + 1)
                    if c != 1:
                        seal_waits(act)
                    act.activation(sq[:, c % 2, 0:n], xm[:, j, a:a + n], ACT.Square).then_inc(ret_sq_ready, 1)

            def ret_roots(j, chunks):
                for c in chunks:
                    root(3 + 3 * j + c, c, P)

            def mix_hi(c, span):
                a, n = CHUNKS[c]
                if span[0] == 3:
                    act.wait_ge(pv_copied, NB * (HEADS - 1) + (3, 6, 9)[c])
                for k in MIX_ORDER[span[0]:span[1]]:
                    act.activation(act_hl[:, 0, k, a:a + n], xm[:, k, a:a + n], ACT.Copy).then_inc(mix_hi_ready, 1)

            def head(j, last):
                n_units = N_HEAD - last
                dst = [(rq, ACT.Copy, 1.0), (rk, ACT.Copy, RET_SCALE), (rv, ACT.Copy, 1.0), (rg, ACT.Silu, 1.0),
                       (aq, ACT.Copy, ATT_SCALE)]
                for p in range(n_units):
                    mixing = last and p == n_units - 1
                    for c in range(3):
                        s = 3 * p + c
                        if s == 13:
                            ret_squares(j, (0, 1))
                        if s == 14:
                            ret_squares(j, (2,))
                            ret_roots(j, (0, 1))
                        if 2 <= s <= NB + 1:
                            copy_att_out(j, s - 2)
                        if s < NB:
                            exps(j, s)
                        if 1 <= s <= NB:
                            copy_prob_t(j, s - 1)
                        if mixing and c == 0:
                            split_weights(UNIT_OUT + 1, [UNIT_OUT + 1])
                        for step in (3 * s, 3 * s + 1):
                            if step in RET_PE_STEP[1:]:
                                copy_ret_out(j, RET_PE_STEP[1:].index(step))
                                if mixing:
                                    mix_hi(c - 1, (3, 5) if step == 3 * s else (5, 7))
                        evac(3 * head_unit(j, p) + c, c, *dst[p])
                        if 3 * s + 2 in RET_PE_STEP[1:]:
                            copy_ret_out(j, RET_PE_STEP[1:].index(3 * s + 2))
                        if mixing:
                            mix_hi(c, (0, 3))
                    if not mixing:
                        like = [head_unit(j, p) + 2] if last else [head_unit(i, p) + 2 for i in range(HEADS - 1)]
                        split_weights(head_unit(j, p) + 2, like, j)
                if last:
                    act.activation(sqrt_eps[:, :], eps_sb[:, :], ACT.Sqrt)
                    copy_ret_out(j, NB - 3)
                    mix_hi(2, (3, 5))
                    copy_ret_out(j, NB - 2)
                    mix_hi(2, (5, 7))
                    copy_ret_out(j, NB - 1)
                    ret_squares(j, (0, 1, 2))
                    ret_roots(j, (0, 1, 2))
                    for c in range(3):
                        act.wait_ge(norm_applied, 3 + 3 * j + c + 1)
                        mix_hi(c, (7, 8))
                else:
                    ret_roots(j, (2,))
                act.wait_ge(state_ready, NB * j + NB)
                act.dma_start(p_state[j], state[:, :]).then_inc(state_stored, 16)
                act.dma_start(s_state[j], state_new[:, :]).then_inc(state_stored, 16)

            with act.Fori(0, HEADS - 1) as j:
                head(j, 0)
            head(HEADS - 1, 1)

            for r in range(3 * N_OUT):
                o, c = OUT_ORDER[r]
                a, n = CHUNKS[c]
                act.wait_ge(dve_evac, r + 1)
                square(xm[:, o, a:a + n], 3 * KT + r, r % 2)
                if r in (18, 21):
                    root(15 + (r - 18) // 3, (r - 18) // 3, D)
                if r in OUT_SPLITS:
                    split_weights(OUT_SPLITS[r], [OUT_SPLITS[r]])
                for item in NORM2_ITEMS.get(r, ()):
                    shift_and_split(3 * KT + item, item // KT, item % KT, 24)
                    if item == 2 * KT - 1:
                        root(17, 2, D)

            def up_pair(f, t, par, unit, like, i=0):
                if not isinstance(f, int) or f > 0:
                    act.wait_ge(conv_ready, f)
                for c in range(3):
                    act.wait_ge(gemm_ready, ffn_chunk(f, 0, c))
                    for o, tok, n, part in pieces(c):
                        ins = act.activation(gate_ext[:, 2 + tok + 2 * part:2 + tok + 2 * part + n],
                                             bank[c][:, o:o + n], ACT.Copy)
                    ins.then_inc(act_evac, 1)
                act.activation(gate_ext[:, S_PROMPT + 2:S_PROMPT + 4], conv_st_sb[:, f, :], ACT.Copy).then_inc(ext_ready, 1)
                act.wait_ge(act_evac, GEMM_OUT + 3 * f + 3)
                seal_waits(act)
                last_rows = gate_ext[:, T + 4 - 2 * 66:T + 4].rearrange("p (s r) -> p s r", s=2)[:, :, 64:66]
                act.activation(conv_out[:, f, :].rearrange("p (s r) -> p s r", s=2), last_rows,
                               ACT.Copy).then_inc(ext_ready, 1)
                split_weights(unit + 2, like[0], i)
                act.wait_ge(conv_ready, f + 1)
                act.activation(conv[:, :], conv[:, :], ACT.Silu).then_inc(silu_ready, 1)
                split_weights(unit + 3, like[1], i)
                for c in range(3):
                    a, n = CHUNKS[c]
                    act.wait_ge(uf_ready, 3 * f + c + 1)
                    act.activation(u_hl[:, par, t, 0, a:a + n], hf[:, c, 0:n], ACT.Copy).then_inc(u_hi_ready, 1)

            for t in range(2):
                n = UNIT_FFN + 2 * t
                up_pair(t, t, 0, n, ([n + 2], [n + 3]))
            with act.Fori(0, (GROUPS - 1) // 2) as i:
                reps = range((GROUPS - 1) // 2)
                for h in range(2):
                    at = UNIT_FFN + 4 + 6 * h
                    for t in range(2):
                        likes = [[at + 2 * t + q + 12 * k for k in reps] for q in (2, 3)]
                        up_pair(2 + 4 * i + 2 * h + t, t, 1 - h, at + 2 * t + 12 * i, likes, i)
                    for q in (6, 7):
                        split_weights(at + q + 12 * i, [at + q + 12 * k for k in reps], i)
            def final_modulate(item):
                c, k = divmod(item, KT)
                if item in FINAL_POOL:
                    act.wait_ge(normed_by_pool, FINAL_POOL.index(item) + 1)
                else:
                    act.wait_ge(normed_ready, sum(i not in FINAL_POOL for i in range(item)) + 1)
                for o, tok, m, part in pieces(c):
                    y = xm[:, k, tok:tok + m]
                    ins = act.activation(y, y, ACT.Identity, bias=mod[:, 48 + 2 * k + 1, part:part + 1],
                                         scale=scale_n[:, 2, k, part:part + 1])
                ins.then_inc(y_ready, 1)

            for r in range(3 * KT):
                c, k = divmod(r, KT)
                a, n = CHUNKS[c]
                act.wait_ge(down_free, 4 + 24 * (GROUPS - 1) + r + 1)
                square(xm[:, k, a:a + n], 6 * KT + r, k % 2)
                if r % KT == FINAL_SUM_AT and r > KT:
                    root(18 + c - 1, c - 1, D, 7)
                if FINAL_LAG < r <= FINAL_LAG + KT:
                    final_modulate(r - FINAL_LAG - 1)
            root(20, 2, D, 7)
            for k in (4, 5, 6, 7, 0, 1, 2, 3):
                final_modulate(KT + k)
            for k in (5, 6, 7):
                final_modulate(2 * KT + k)

        @block.gpsimd
        def _(pool):
            def split_weights(n, like):
                slot = SLOTS[like[0]]
                pool.wait_ge(wh_ready, n + 1)
                pool.tensor_tensor(w_hl[:, slot, 1], w_raw[:, slot], w_hl[:, slot, 0].bitcast(F32),
                                   ALU.subtract).then_inc(wl_ready, 1)

            def add_square(item, ring, first, dst):
                pool.wait_ge(sq_ready, item + 1)
                src = sq[:, ring, 0:dst.shape[-1]]
                if first:
                    ins = pool.tensor_copy(dst, src)
                else:
                    ins = pool.tensor_tensor(dst, dst, src, ALU.add)
                ins.then_inc(sq_used, 1)

            def split_hf(item, c, k, ring=None):
                a, n = CHUNKS[c]
                pool.wait_ge(hi_ready, item + 1)
                h = hf[:, item % 3] if ring is None else ring[item % 5]
                pool.tensor_tensor(act_hl[:, 1, k, a:a + n], h[:, 0:n],
                                   act_hl[:, 0, k, a:a + n].bitcast(F32), ALU.subtract).then_inc(lo_ready, 1)

            pool.memset(ones[:, :], 1.0).then_inc(pool_const, 1)
            pool.memset(eps_sb[:, :], EPS).then_inc(pool_const, 1)

            def multiply_ada(m, s):
                if s == 0 and m > 12:
                    pool.wait_ge(ada_summed, 2 * (m - 12) - 1)
                pool.wait_ge(ada_pool_loaded[m - 12], 16)
                dst = ada_pool_place[m - 12] if s else acc[:, 0:D]
                pool.tensor_tensor(dst, ada_pool_place[m - 12], silu_c[:, s], ALU.mult).then_inc(ada_product, 1)

            pool.wait_ge(silu_c_ready, 1)
            for s in range(2):
                multiply_ada(12, s)
            pool.wait_ge(x_inv_ready, 1)
            for k in range(KT):
                x = xm[:, k, 0:CHUNKS[0][1]]
                pool.tensor_tensor(x, x, std[:, 0], ALU.mult).then_inc(x_normed, 1)
            for n in range(3):
                split_weights(n, [n])
            for k in range(KT):
                for c in range(3):
                    split_hf(3 * k + c, c, k, H_RING)
                if k in (1, 3):
                    multiply_ada(13, k // 2)
            for n in (3, 4):
                split_weights(n, [n])

            def decay_q(j):
                pool.wait_ge(act_evac, 3 * head_unit(j, 0) + 3)
                pool.wait_ge(ret_tab_loaded, 32 * (j + 1))
                dec = rtab[:, RT_Q:RT_Q + P]
                pool.tensor_tensor(acc[:, 0:S_PROMPT].rearrange("p (b l) -> p b l", b=8),
                                   rq[:, 0:S_PROMPT].rearrange("p (b l) -> p b l", b=8),
                                   dec.unsqueeze(1).broadcast_to([P, 8, P]), ALU.mult).then_inc(qdec_ready, 1)
                pool.tensor_tensor(acc[:, S_PROMPT:T], rq[:, S_PROMPT:T], dec[:, 0:S_SAMPLE],
                                   ALU.mult).then_inc(qdec_ready, 1)

            def gate_ret(j):
                pool.wait_ge(act_evac, 3 * head_unit(j, 3) + 3)
                for c in range(3):
                    a, n = CHUNKS[c]
                    out = xm[:, j, a:a + n]
                    pool.wait_ge(inv_ready, 3 * j + c + 1)
                    seal_waits(pool)
                    pool.tensor_tensor(out, out, std[:, c, 0:n], ALU.mult).then_inc(ret_scaled, 1)
                    pool.wait_ge(ret_scaled, 3 * j + c + 1)
                    seal_waits(pool)
                    pool.tensor_tensor(out, out, rg[:, a:a + n], ALU.mult).then_inc(norm_applied, 1)

            with pool.Fori(0, HEADS - 1) as j:
                for p in range(N_HEAD):
                    split_weights(head_unit(j, p) + 2, [head_unit(0, p) + 2])
                    if p == 0:
                        decay_q(j)
                gate_ret(j)
            for p in range(N_HEAD - 1):
                split_weights(head_unit(HEADS - 1, p) + 2, [head_unit(HEADS - 1, p) + 2])
                if p == 0:
                    decay_q(HEADS - 1)
            for c in range(3):
                a, n = CHUNKS[c]
                for i, k in enumerate(MIX_ORDER[:2]):
                    pool.wait_ge(mix_hi_ready, 7 * c + i + 1)
                    pool.tensor_tensor(act_hl[:, 1, k, a:a + n], xm[:, k, a:a + n], act_hl[:, 0, k, a:a + n].bitcast(F32),
                                       ALU.subtract).then_inc(mix_lo_pool, 1)
            gate_ret(HEADS - 1)

            for r in range(3 * N_OUT):
                o, c = OUT_ORDER[r]
                a, n = CHUNKS[c]
                if o > 0:
                    pool.wait_ge(sq_used, 3 * KT + r)
                add_square(3 * KT + r, r % 2, o == 0, acc[:, a:a + n])
                if r in OUT_SPLITS:
                    split_weights(OUT_SPLITS[r], [OUT_SPLITS[r]])
                for item in NORM2_ITEMS.get(r, ()):
                    split_hf(3 * KT + item, item // KT, item % KT)
            pool.memset(gate_ext[:, 0:2], 0.0).then_inc(pool_const, 1)

            def up_pair(f, t, par, unit, like):
                split_weights(unit + 2, like[0])
                split_weights(unit + 3, like[1])
                for c in range(3):
                    a, n = CHUNKS[c]
                    pool.wait_ge(u_hi_ready, 3 * f + c + 1)
                    pool.tensor_tensor(u_hl[:, par, t, 1, a:a + n], hf[:, c, 0:n],
                                       u_hl[:, par, t, 0, a:a + n].bitcast(F32), ALU.subtract).then_inc(u_lo_ready, 1)

            for t in range(2):
                n = UNIT_FFN + 2 * t
                up_pair(t, t, 0, n, ([n + 2], [n + 3]))
            with pool.Fori(0, (GROUPS - 1) // 2) as i:
                for h in range(2):
                    at = UNIT_FFN + 4 + 6 * h
                    for t in range(2):
                        up_pair(2 + 4 * i + 2 * h + t, t, 1 - h, at + 2 * t + 12 * i,
                                ([at + 2 * t + 2], [at + 2 * t + 3]))
                    for q in (6, 7):
                        split_weights(at + q + 12 * i, [at + q])
            for c in range(3):
                a, n = CHUNKS[c]
                for k in range(KT - (c == 2)):
                    if k > 0:
                        pool.wait_ge(sq_used, 6 * KT + KT * c + k)
                    add_square(6 * KT + KT * c + k, k % 2, k == 0, acc[:, a:a + n])
            for item in FINAL_POOL:
                c, k = divmod(item, KT)
                a, n = CHUNKS[c]
                pool.wait_ge(inv_ready, 3 * HEADS + c + 1)
                pool.tensor_tensor(xm[:, k, a:a + n], xm[:, k, a:a + n], std[:, c, 0:n],
                                   ALU.mult).then_inc(normed_by_pool, 1)

        @block.vector
        def _(dve):
            seq = [0]

            def then_wait(ins):
                seq[0] += 1
                ins.then_inc(dve_seq, 1)
                dve.wait_ge(dve_seq, seq[0])

            def in_loop_wait(ins, base, per, j, local):
                ins.then_inc(dve_seq, 1)
                dve.wait_ge(dve_seq, base + per * j + local)

            def ada_dots(m, load, place, part):
                dve.wait_ge(ada_loaded[place], 16 * load)
                for s in range(2):
                    if not isinstance(m, int) or m > 0 or s > 0:
                        dve.wait_ge(ada_used, 2 * m + s)
                    if not isinstance(m, int):
                        seal_waits(dve)
                    out = ada_place[place] if s else ada_out[:, :]
                    dve.tensor_tensor_reduce(out, ada_place[place], silu_c[:, s], 1.0, 0.0, ALU.mult, ALU.add,
                                             mod_part[:, part, s:s + 1]).then_inc(ada_used, 1)

            def add_ada_bias(m0, n, used, part=0):
                dve.wait_ge(ada_used, 2 * used)
                return dve.tensor_tensor(mod[:, bass.ds(m0, n), :], mod_part[:, part:part + n, :],
                                         b_ada_sb[:, bass.ds(m0, n)].unsqueeze(2).broadcast_to([P, n, 2]), ALU.add)

            def norm_scale(which, m0):
                return dve.scalar_tensor_tensor(scale_n[:, which], mod[:, m0:m0 + 16:2, :], 1.0,
                                                gains_sb[:, which].unsqueeze(2).broadcast_to([P, KT, 2]),
                                                ALU.add, ALU.mult)

            def invert(q, c):
                n = CHUNKS[c][1]
                dve.wait_ge(std_ready, q + 1)
                then_wait(dve.reciprocal(std[:, c, 0:n], std[:, c, 0:n]))

            def first_ada_dots(m):
                nth = ADA_DVE.index(m)
                ada_dots(nth, nth // 7 + 1, nth % 7, m % 8 if m < 12 else m - 4)

            def first_vectors(k):
                m = 2 * k
                if k < 6:
                    then_wait(add_ada_bias(m, 2, m + 2, m % 8))
                else:
                    dve.wait_ge(ada_summed, 4)
                    then_wait(add_ada_bias(m, 2, 12 if k == 6 else len(ADA_DVE), m - 4))
                dve.tensor_scalar(scale_n[:, 0, k, :], mod[:, 2 * k, :], 1.0, gains_sb[:, 0, k:k + 1],
                                  ALU.add, ALU.mult).then_inc(vec_ready, 1)
                dve.wait_ge(vec_ready, k + 1)

            dve.wait_ge(silu_c_ready, 1)
            for m in range(7):
                first_ada_dots(m)
                if m in (3, 5):
                    invert(m // 2 - 1, m // 2 - 1)
                if m == 3:
                    dve.sem_inc(x_inv_ready, 1)
            invert(2, 2)
            dve.wait_ge(const_loaded, 16 * 5)
            dve.wait_ge(sq_used, 3 * KT)
            for k in range(KT):
                first_vectors(k)
                for c in (1, 2):
                    item = 3 * k + c
                    if item >= 5:
                        dve.wait_ge(lo_ready, item - 4)
                    for o, tok, m, part in pieces(c):
                        ins = dve.scalar_tensor_tensor(H_RING[item % 5][:, o:o + m], xm[:, k, tok:tok + m],
                                                       scale_n[:, 0, k, part:part + 1], std[:, c, o:o + m],
                                                       ALU.mult, ALU.mult)
                    ins.then_inc(x_scaled, 1)
                    for tile in ADA_DOTS_IN.get(k, ())[c - 1:c]:
                        first_ada_dots(tile)
            dve.sem_inc(ada_used, 4)
            dve.wait_ge(x_scaled, 2 * KT)
            dve.wait_ge(x_normed, KT)
            dve.sem_inc(norm_applied, 3)

            for b in range(NB):
                t, n = BLOCKS[b]
                dve.wait_ge(av_t_ready, b + 1)
                dve.tensor_copy(av_tok[0:n, b + (b == NB - 1), :], bank[(3, 6)[b % 2]][0:n, 0:P]).then_inc(av_tok_ready, 1)

            def mask_and_max(j, b):
                qn, kb, r = BLOCKS[b][1], keys_of(b), b % 2
                kn = sum(k[1] for k in kb)
                if b == 0:
                    dve.wait_ge(att_tab_loaded, 32 * (j + 1))
                if b >= 2:
                    dve.wait_ge(pt_ready, NB * j + b - 1)
                dve.wait_ge(qk_ready, NB * j + b + 1)
                seal_waits(dve)
                for g in range(2):
                    ins = dve.tensor_tensor_reduce(prob[0:qn, r, g, 0:kn], bank[3 + g][0:qn, 0:kn],
                                                   att_tab[0:qn, g, kb[0][2]:kb[0][2] + kn], 1.0, sink_sb[0:qn, g:g + 1],
                                                   ALU.add, ALU.max, soft[0:qn, r, 0, g:g + 1])
                chain(ins, j)
                dve.tensor_scalar(soft[0:qn, r, 1, :], soft[0:qn, r, 0, :], -1.0, None, ALU.mult)
                dve.tensor_tensor(soft[0:qn, r, 2, :], sink_sb[0:qn, :], soft[0:qn, r, 0, :],
                                  ALU.subtract).then_inc(masked_ready, 1)

            def normalise(j, b):
                qn, r = BLOCKS[b][1], b % 2
                kn = sum(k[1] for k in keys_of(b))
                dve.wait_ge(exp_ready, NB * j + b + 1)
                chain(dve.tensor_tensor(rden[0:qn, r, :], soft[0:qn, r, 3, :], soft[0:qn, r, 4, :], ALU.add), j)
                chain(dve.reciprocal(rden[0:qn, r, :], rden[0:qn, r, :]), j)
                for g in range(2):
                    ins = dve.tensor_scalar(prob[0:qn, r, g, 0:kn], prob[0:qn, r, g, 0:kn], rden[0:qn, r, g:g + 1],
                                            None, ALU.mult)
                ins.then_inc(prob_ready, 1)

            def take_block(j, b):
                n, r = BLOCKS[b][1], b % 2
                A = bank[3 + r]
                if b == 0:
                    dve.wait_ge(ret_tab_loaded, 32 * (j + 1))
                if b >= 2:
                    dve.wait_ge(ret_b_ready, NB * j + b - 1)
                dve.wait_ge(ret_a_ready, NB * j + b + 1)
                kd = RT_K + (b == NB - 1)
                dve.tensor_scalar(k_tok[0:n, r, :], A[0:n, 0:P], rtab[0:n, kd:kd + 1], None, ALU.mult)
                dve.tensor_copy(v_tok[0:n, r, :], A[0:n, P:2 * P])
                dve.tensor_tensor(s_dec[0:n, r, 0:n], A[0:n, 2 * P:2 * P + n], rtab[0:n, 0:n],
                                  ALU.mult).then_inc(ret_a_used, 1)

            def next_state(j, b):
                if b == 0:
                    dve.wait_ge(state_stored, 32 * j + 32)
                dve.wait_ge(ret_b_ready, NB * j + b + 1)
                if b == 0:
                    ins = dve.tensor_copy(state[:, :], bank[5][:, 0:P])
                elif b < NB - 1:
                    dve.wait_ge(state_ready, NB * j + b)
                    ins = dve.scalar_tensor_tensor(state[:, :], state[:, :], rtab[:, RT_K + 2:RT_K + 3],
                                                   bank[5][:, 0:P], ALU.mult, ALU.add)
                else:
                    ins = dve.scalar_tensor_tensor(state_new[:, :], state_in[:, :], rtab[:, RT_K + 3:RT_K + 4],
                                                   bank[5][:, 0:P], ALU.mult, ALU.add)
                ins.then_inc(state_ready, 1)

            def mix_lo(c, span):
                a, n = CHUNKS[c]
                for i in range(*span):
                    k = MIX_ORDER[i]
                    dve.wait_ge(mix_hi_ready, 7 * c + i + 1 if i < 7 else 21 + c + 1)
                    dve.tensor_tensor(act_hl[:, 1, k, a:a + n], xm[:, k, a:a + n], act_hl[:, 0, k, a:a + n].bitcast(F32),
                                      ALU.subtract).then_inc(mix_lo_ready, 1)

            PER_HEAD = 3 * NB + 1
            base = seq[0]
            local = [0]

            def chain(ins, j):
                local[0] += 1
                in_loop_wait(ins, base, PER_HEAD, j, local[0])

            def head(j, last):
                local[0] = 0
                def retention(k):
                    if k < NB:
                        take_block(j, k)
                    if k >= 1:
                        next_state(j, k - 1)

                for s in range(3 * (N_HEAD - last)):
                    if 1 <= s <= NB:
                        normalise(j, s - 1)
                    if s < NB:
                        mask_and_max(j, s)
                    if 1 <= s <= 8:
                        ada_dots(16 + s - 1 + 8 * j, 2 + (s - 1) // 2 + 1 + 4 * j, (s - 1) % 2, s - 1)
                    if s == NB:
                        chain(add_ada_bias(16 + 8 * j, 8, 16 + 8 * j + 8), j)
                    for k in range(NB + 1):
                        if RET_PE_STEP[k] // 3 == s:
                            retention(k)
                            if last and k in MIX_LO_AFTER:
                                mix_lo(*MIX_LO_AFTER[k])
                for k in range(7, NB + 1) if last else ():
                    retention(k)
                    mix_lo(*MIX_LO_AFTER[k])
                for c in range(3):
                    n = CHUNKS[c][1]
                    dve.wait_ge(std_ready, 3 + 3 * j + c + 1)
                    dve.reciprocal(std[:, c, 0:n], std[:, c, 0:n]).then_inc(inv_ready, 1)
                for c in range(3) if last else ():
                    mix_lo(c, (7, 8))
                assert local[0] == PER_HEAD, local[0]

            with dve.Fori(0, HEADS - 1) as j:
                head(j, 0)
            head(HEADS - 1, 1)
            seq[0] = base + PER_HEAD * HEADS

            then_wait(norm_scale(1, 24))

            for r in range(3 * N_OUT):
                o, c = OUT_ORDER[r]
                if r < 3:
                    dve.wait_ge(x_again[c], 32)
                if r == 9:
                    dve.wait_ge(x_tile_again, 16)
                dve.wait_ge(gemm_ready, GEMM_OUT + r + 1)
                for off, tok, m, part in pieces(c):
                    x = xm[:, o, tok:tok + m]
                    ins = dve.scalar_tensor_tensor(x, bank[r % 3][:, off:off + m], mod[:, 16 + o, part:part + 1],
                                                   x, ALU.mult, ALU.add)
                ins.then_inc(dve_evac, 1)
                t = r - 2
                if 0 <= t < 16:
                    ada_dots(48 + t, 18 + t // 2 + 1, t % 2, t % 8)
                    if t % 8 == 7:
                        then_wait(add_ada_bias(48 + t - 7, 8, 48 + t + 1))
                for item in NORM2_ITEMS.get(r, ()):
                    c, k = divmod(item, KT)
                    if k == 0:
                        invert(15 + c, c)
                    dve.wait_ge(lo_ready, 3 * KT + item - 2)
                    for off, tok, m, part in pieces(c):
                        ins = dve.scalar_tensor_tensor(hf[:, item % 3, off:off + m], xm[:, k, tok:tok + m],
                                                       scale_n[:, 1, k, part:part + 1], std[:, c, off:off + m],
                                                       ALU.mult, ALU.mult)
                    ins.then_inc(hf_ready, 1)
                    if k == KT - 1:
                        dve.wait_ge(hf_ready, item + 1)
                        dve.sem_inc(norm_applied, 1)
            then_wait(norm_scale(2, 48))

            def up_pair(f, t, n_ext, local0, i, base_seq, per):
                dve.wait_ge(ext_ready, 2 * n_ext + 2)
                w = conv_wb_sb[:, bass.ds(f, 1), :]
                ins = dve.tensor_scalar(conv[:, :], gate_ext[:, 0:T + 2], w[:, 0, 0:1], w[:, 0, 3:4], ALU.mult, ALU.add)
                in_loop_wait(ins, base_seq, per, i, local0 + 1)
                ins = dve.scalar_tensor_tensor(conv[:, :], gate_ext[:, 1:T + 3], w[:, 0, 1:2], conv[:, :], ALU.mult, ALU.add)
                in_loop_wait(ins, base_seq, per, i, local0 + 2)
                dve.scalar_tensor_tensor(conv[:, :], gate_ext[:, 2:T + 4], w[:, 0, 2:3], conv[:, :], ALU.mult,
                                         ALU.add).then_inc(conv_ready, 1)
                dve.wait_ge(silu_ready, f + 1)
                for c in range(3):
                    dve.wait_ge(gemm_ready, ffn_chunk(f, 1, c))
                    src = bank[3 + c if isinstance(f, int) and f == 0 else c]
                    if not isinstance(f, int) or f > 0:
                        dve.wait_ge(u_lo_ready, 3 * f + c - 2)
                    for off, tok, m, part in pieces(c):
                        ins = dve.tensor_tensor(hf[:, c, off:off + m], conv[:, tok + 2 * part:tok + 2 * part + m],
                                                src[:, off:off + m], ALU.mult)
                    ins.then_inc(uf_ready, 1)

            def down_tile(g, r, o, c):
                dve.wait_ge(down_ready, 24 * g + r + 1)
                for off, tok, m, part in pieces(c):
                    x = xm[:, o, tok:tok + m]
                    ins = dve.scalar_tensor_tensor(x, bank[3 + r % 4][:, off:off + m], mod[:, 40 + o, part:part + 1],
                                                   x, ALU.mult, ALU.add)
                ins.then_inc(down_free, 1)

            dve.sem_inc(down_free, 4)
            dve.wait_ge(pool_const, 3)
            for t in range(2):
                up_pair(t, t, t, 2 * t, 0, seq[0], 0)
            seq[0] += 4
            base_ffn = seq[0]
            with dve.Fori(0, (GROUPS - 1) // 2) as i:
                for h in range(2):
                    for t in range(2):
                        f = 2 + 4 * i + 2 * h + t
                        up_pair(f, t, f, 4 * h + 2 * t, i, base_ffn, 8)
                    for o in range(KT):
                        for c in range(3):
                            down_tile(2 * i + h, 3 * o + c, o, c)
            seq[0] = base_ffn + 8 * ((GROUPS - 1) // 2)
            def final_invert(c):
                n = CHUNKS[c][1]
                dve.wait_ge(std_ready, 18 + c + 1)
                dve.reciprocal(std[:, c, 0:n], std[:, c, 0:n]).then_inc(inv_ready, 1)

            def final_tile(item):
                c, k = divmod(item, KT)
                a, n = CHUNKS[c]
                dve.wait_ge(inv_ready, 3 * HEADS + c + 1)
                dve.wait_ge(sq_ready, 6 * KT + item + 1)
                if c == 2:
                    for o, tok, m, part in pieces(c):
                        x = xm[:, k, tok:tok + m]
                        ins = dve.scalar_tensor_tensor(x, x, scale_n[:, 2, k, part:part + 1], std[:, c, o:o + m],
                                                       ALU.mult, ALU.mult)
                    then_wait(ins)
                    for o, tok, m, part in pieces(c):
                        x = xm[:, k, tok:tok + m]
                        ins = dve.tensor_scalar(x, x, mod[:, 48 + 2 * k + 1, part:part + 1], None, ALU.add)
                    ins.then_inc(y_by_dve, 1)
                else:
                    dve.tensor_tensor(xm[:, k, a:a + n], xm[:, k, a:a + n], std[:, c, 0:n],
                                      ALU.mult).then_inc(normed_ready, 1)

            for r in range(3 * KT):
                c, o = divmod(r, KT)
                down_tile(GROUPS - 1, r, o, c)
                if r == FINAL_LAG - 1:
                    final_invert(0)
                if FINAL_LAG <= r < FINAL_LAG + KT:
                    final_tile(r - FINAL_LAG)
            final_invert(1)
            final_invert(2)
            for item in range(KT, 3 * KT):
                if item not in FINAL_POOL:
                    final_tile(item)

        @block.tensor
        def _(pe):
            def sums(q, c, src):
                n = CHUNKS[c][1]
                if c == 2:
                    pe.wait_ge(std_ready, q - 1)
                    seal_waits(pe)
                pe.matmul(bank[SUM_BANK[c]][:, 0:n], ones[:, :], src[:, 0:n], start=True, stop=True).then_inc(sum_ready, 1)

            def unit(n, slot, wait_bank, between, order=range(KT)):
                pe.wait_ge(wl_ready, n + 1)
                for c in range(3):
                    a, m = CHUNKS[c]
                    wait_bank(c)
                    for pas, (w, x) in enumerate(((0, 0), (0, 1), (1, 0))):
                        for i, k in enumerate(order):
                            ins = pe.matmul(bank[c][:, 0:m], w_hl[:, slot, w, k, :], act_hl[:, x, k, a:a + m],
                                            start=(pas == 0 and i == 0), stop=(pas == 2 and i == KT - 1))
                            if c == pas == i == 0:
                                ins.then_inc(unit_done, 1)
                        if pas == 2:
                            ins.then_inc(gemm_ready, 1)
                        between(3 * c + pas)

            pe.wait_ge(pool_const, 2)
            for c in range(3):
                a, n = CHUNKS[c]
                for k in range(KT):
                    item = KT * c + k
                    pe.wait_ge(sq_ready, item + 1)
                    ins = pe.matmul(bank[X_SUM_BANK[c]][:, 0:n], ones[:, :], X_SQ[item % 4][:, 0:n], start=(k == 0),
                                    stop=(k == KT - 1))
                    ins.then_inc(sq_used, 1)
                pe.wait_ge(sq_used, KT * (c + 1))
                pe.sem_inc(sum_ready, 1)

            def after(n):
                def wait(c):
                    pe.wait_ge(act_evac, 3 * (n - 1) + c + 1)
                return wait

            def nothing(s):
                pass

            def values_by_token(s):
                t, n = BLOCKS[s]
                if s >= 2:
                    pe.wait_ge(av_tok_ready, s - 1)
                pe.transpose(bank[(3, 6)[s % 2]][0:n, 0:P], rv[:, t:t + n], ident[:, :]).then_inc(av_t_ready, 1)

            pe.wait_ge(wl_ready, 3)
            pe.wait_ge(std_ready, 3)
            for k in range(KT):
                jobs = [(u, c) for c in range(3) for u in range(3) if (u, c) != (2, 2)]
                for u, c in sorted(jobs) if k == KT - 1 else jobs:
                    a, m = CHUNKS[c]
                    pe.wait_ge(lo_ready, 3 * k + c + 1)
                    for pas, (w, x) in enumerate(((0, 0), (0, 1), (1, 0))):
                        ins = pe.matmul(bank[3 * u + c][:, 0:m], w_hl[:, SLOTS[u], w, k, :], act_hl[:, x, k, a:a + m],
                                        start=(k == pas == 0), stop=(k == KT - 1 and pas == 2))
                    if k == KT - 1:
                        ins.then_inc(gemm_ready, 1)
            pe.wait_ge(gemm_ready, 6)
            pe.sem_inc(unit_done, 2)
            pe.wait_ge(act_evac, 7)
            pe.wait_ge(const_loaded, 16 * 5)
            a, m = CHUNKS[2]
            for pas, (w, x) in enumerate(((0, 0), (0, 1), (1, 0))):
                for k in range(KT):
                    ins = pe.matmul(bank[0][:, 0:m], w_hl[:, SLOTS[2], w, k, :], act_hl[:, x, k, a:a + m],
                                    start=(k == pas == 0), stop=(k == KT - 1 and pas == 2))
                if pas == 2:
                    ins.then_inc(gemm_ready, 1)
                for b in range(3):
                    values_by_token(3 * pas + b)
            pe.wait_ge(act_evac, 9)

            def scores(j, b):
                t, n = BLOCKS[b]
                kb = keys_of(b)
                kn = sum(k[1] for k in kb)
                if b in (0, 2, 5):
                    pe.wait_ge(act_evac, 7 + (0, 2, 5).index(b) + 15 * j)
                if b == 0:
                    pe.wait_ge(av_tok_ready, NB)
                    pe.wait_ge(cache_loaded, 32)
                else:
                    pe.wait_ge(masked_ready, NB * j + b)
                    if b == NB - 1:
                        seal_waits(pe)
                for g in range(2):
                    h = slice(64 * g, 64 * g + 64)
                    ins = pe.matmul(bank[3 + g][0:n, 0:kn], aq[h, t:t + n], ak[h, kb[0][0]:kb[0][0] + kn],
                                    start=True, stop=True)
                ins.then_inc(qk_ready, 1)

            def transpose_prob(j, b):
                n, r, kb = BLOCKS[b][1], b % 2, keys_of(b)
                pe.wait_ge(prob_ready, NB * j + b + 1)
                if b > 0:
                    pe.wait_ge(pt_copied, NB * j + b)
                if b == NB - 1:
                    seal_waits(pe)
                for g in range(2):
                    at = 0
                    for i, k in enumerate(kb):
                        col = P * (2 * g + i)
                        ins = pe.transpose(bank[5][0:k[1], col:col + n], prob[0:n, r, g, at:at + k[1]], ident[0:n, 0:n])
                        at += k[1]
                ins.then_inc(pt_ready, 1)

            def weigh_values(j, b):
                n, r, kb = BLOCKS[b][1], b % 2, keys_of(b)
                pe.wait_ge(pt_copied, NB * j + b + 1)
                if b > 0:
                    pe.wait_ge(pv_copied, NB * j + b)
                else:
                    pe.wait_ge(std_ready, 3 + 3 * j)
                for g in range(2):
                    h = slice(64 * g, 64 * g + 64)
                    for i, k in enumerate(kb):
                        ins = pe.matmul(bank[6][h, 0:n], av_tok[0:k[1], k[3], h], prob_t[0:k[1], r, g, i, 0:n],
                                        start=(i == 0), stop=(i == len(kb) - 1))
                ins.then_inc(pv_ready, 1)

            def block_scores(j, b):
                t, n = BLOCKS[b]
                if b == 0:
                    pe.wait_ge(act_evac, 3 * head_unit(j, 2) + 3)
                    pe.wait_ge(masked_ready, NB * j + NB)
                if b >= 2:
                    pe.wait_ge(ret_a_used, NB * j + b - 1)
                if b == NB - 1:
                    seal_waits(pe)
                A = bank[3 + b % 2]
                pe.transpose(A[0:n, 0:P], rk[:, t:t + n], ident[:, :])
                pe.transpose(A[0:n, P:2 * P], rv[:, t:t + n], ident[:, :])
                pe.matmul(A[0:n, 2 * P:2 * P + n], rk[:, t:t + n], rq[:, t:t + n], start=True,
                          stop=True).then_inc(ret_a_ready, 1)

            def block_output(j, b):
                t, n = BLOCKS[b]
                r = b % 2
                if b == 0:
                    pe.wait_ge(qdec_ready, 2 * j + 2)
                    pe.wait_ge(pv_copied, NB * j + NB)
                else:
                    pe.wait_ge(ret_o_copied, NB * j + b)
                    pe.wait_ge(state_ready, NB * j + b)
                pe.wait_ge(ret_a_used, NB * j + b + 1)
                carried = state if b < NB - 1 else state_in
                if b == NB - 1:
                    pe.wait_ge(ret_tab_loaded, 32 * (j + 1))
                pe.matmul(bank[6][:, 0:n], v_tok[0:n, r, :], s_dec[0:n, r, 0:n], start=True, stop=(b == 0))
                if b > 0:
                    pe.matmul(bank[6][:, 0:n], carried[:, :], acc[:, t:t + n], start=False, stop=True)
                pe.matmul(bank[5][:, 0:P], k_tok[0:n, r, :], v_tok[0:n, r, :], start=True, stop=True).then_inc(ret_b_ready, 1)

            def ret_sums(j, c):
                pe.wait_ge(ret_sq_ready, 3 * j + c + 1)
                sums(3 + 3 * j + c, c, sq[:, c % 2, :])

            def head(j, last):
                def between(p):
                    def steps(i):
                        s = 9 * p + i
                        b = s // 3
                        if s % 3 == 0 and b < NB:
                            scores(j, b)
                        if s % 3 == 1 and 1 <= b <= NB:
                            transpose_prob(j, b - 1)
                        if s % 3 == 0 and 2 <= b <= NB + 1:
                            weigh_values(j, b - 2)
                        if s in RET_PE_STEP:
                            k = RET_PE_STEP.index(s)
                            if k < NB:
                                block_scores(j, k)
                            if k >= 1:
                                block_output(j, k - 1)
                        for c in RET_SUM_STEP[last].get(s, ()):
                            ret_sums(j, c)
                    return steps
                for p in range(N_HEAD - last):
                    unit(head_unit(j, p), HEAD_SLOTS[p], after(head_unit(j, p)), between(p))
                if last:
                    first_out_unit(between(N_HEAD - 1))

            def wait_mix(c, i):
                if i < 2:
                    pe.wait_ge(mix_lo_pool, 2 * c + i + 1)
                elif i < 7:
                    pe.wait_ge(mix_lo_ready, 5 * c + i - 1)
                else:
                    pe.wait_ge(mix_lo_ready, 15 + c + 1)

            def first_out_unit(between):
                pe.wait_ge(wl_ready, UNIT_OUT + 1)

                def tile(c, i):
                    a, m = CHUNKS[c]
                    wait_mix(c, i)
                    k = MIX_ORDER[i]
                    for pas, (w, x) in enumerate(((0, 0), (0, 1), (1, 0))):
                        ins = pe.matmul(bank[c][:, 0:m], w_hl[:, SLOTS[UNIT_OUT], w, k, :], act_hl[:, x, k, a:a + m],
                                        start=(i == pas == 0), stop=(i == KT - 1 and pas == 2))
                        if c == i == pas == 0:
                            ins.then_inc(unit_done, 1)
                    if i == KT - 1:
                        ins.then_inc(gemm_ready, 1)

                for c in range(3):
                    pe.wait_ge(act_evac, GEMM_OUT - 3 + c + 1)
                    for t, tiles in enumerate(((0, 1), (2, 3), (4, 5, 6))):
                        for i in tiles:
                            tile(c, i)
                        between(3 * c + t)
                for c in range(3):
                    tile(c, KT - 1)

            with pe.Fori(0, HEADS - 1) as j:
                head(j, 0)
            head(HEADS - 1, 1)

            def after_out(o):
                def wait(c):
                    pe.wait_ge(dve_evac, 3 * o - 3 + c + 1)
                return wait

            with pe.Fori(0, 2) as i:
                for p in range(2):
                    unit(UNIT_OUT + 1 + p + 2 * i, SLOTS[UNIT_OUT + 1 + p], after_out(2 * i + 1 + p), nothing, MIX_ORDER)
            for r in range(15, 3 * N_OUT):
                o, c = OUT_ORDER[r]
                a, m = CHUNKS[c]
                if r in (19, 22):
                    pe.wait_ge(sq_used, 3 * KT + r - 1)
                    sums(15 + (r - 19) // 3, (r - 19) // 3, acc[:, CHUNKS[(r - 19) // 3][0]:])
                if c == 0:
                    pe.wait_ge(wl_ready, UNIT_OUT + o + 1)
                pe.wait_ge(dve_evac, r - 2)
                for pas, (w, x) in enumerate(((0, 0), (0, 1), (1, 0))):
                    for i, k in enumerate(MIX_ORDER):
                        ins = pe.matmul(bank[r % 3][:, 0:m], w_hl[:, SLOTS[UNIT_OUT + o], w, k, :],
                                        act_hl[:, x, k, a:a + m], start=(pas == i == 0), stop=(pas == 2 and i == KT - 1))
                        if pas == i == 0 and r in (15, 22, 23):
                            ins.then_inc(unit_done, 1)
                ins.then_inc(gemm_ready, 1)

            for r, (h, c, at) in enumerate(((0, 0, 0), (0, 1, 1), (1, 0, 3), (1, 1, 4), (0, 2, 2), (1, 2, 5))):
                a, m = CHUNKS[c]
                n = UNIT_FFN + h
                pe.wait_ge(wl_ready, n + 1)
                if h == 0:
                    pe.wait_ge(dve_evac, 3 * N_OUT - 2 + c)
                if r == 2:
                    pe.wait_ge(sq_used, 3 * KT + 3 * N_OUT)
                    sums(17, 2, acc[:, CHUNKS[2][0]:])
                for i, k in enumerate(range(KT)):
                    pe.wait_ge(lo_ready, 3 * KT + KT * c + k + 1)
                    for pas, (w, x) in enumerate(((0, 0), (0, 1), (1, 0))):
                        ins = pe.matmul(bank[at][:, 0:m], w_hl[:, SLOTS[n], w, k, :], act_hl[:, x, k, a:a + m],
                                        start=(k == pas == 0), stop=(k == KT - 1 and pas == 2))
                        if k == pas == 0 and r in (0, 5):
                            ins.then_inc(unit_done, 1)
                ins.then_inc(gemm_ready, 1)

            def ffn_unit(n, f, f_before, is_up, slot, units_before):
                pe.wait_ge(wl_ready, n + 1)
                for c in range(3):
                    a, m = CHUNKS[c]
                    if is_up:
                        pe.wait_ge(act_evac, GEMM_OUT + 3 * f + c + 1)
                    elif f_before is None:
                        pe.wait_ge(act_evac, GEMM_OUT + c + 1)
                    else:
                        pe.wait_ge(uf_ready, 3 * f_before + c + 1)
                    for pas, (w, x) in enumerate(((0, 0), (0, 1), (1, 0))):
                        for k in range(KT):
                            ins = pe.matmul(bank[c][:, 0:m], w_hl[:, slot, w, k, :], act_hl[:, x, k, a:a + m],
                                            start=(pas == 0 and k == 0), stop=(pas == 2 and k == KT - 1))
                            if c == pas == 0 and k < units_before:
                                ins.then_inc(unit_done, 1)
                    ins.then_inc(gemm_ready, 1)

            def final_sums(c):
                a, m = CHUNKS[c]
                last = c == 2
                if c > 0:
                    pe.wait_ge(std_ready, 18 + c)
                pe.wait_ge(sq_used, 6 * KT + KT * (c + 1) - last)
                ins = pe.matmul(bank[7][:, 0:m], ones[:, :], acc[:, a:a + m], start=True, stop=not last)
                if last:
                    pe.wait_ge(sq_ready, 9 * KT)
                    ins = pe.matmul(bank[7][:, 0:m], ones[:, :], sq[:, (KT - 1) % 2, 0:m], start=False, stop=True)
                ins.then_inc(sum_ready, 1)

            def down(g, n, slots, par, order, final=False):
                pe.wait_ge(wl_ready, n + 2 - final)
                pe.wait_ge(u_lo_ready, 6 * g + 6)
                for t in range(2) if final else ():
                    pe.wait_ge(wl_ready, n + 1 + t)
                    for r, (o, c) in enumerate(order[:4]):
                        a, m = CHUNKS[c]
                        if t == 0:
                            pe.wait_ge(down_free, 24 * g + r + 1)
                        for w, x in ((0, 0), (0, 1), (1, 0)):
                            ins = pe.matmul(bank[3 + r % 4][:, 0:m], w_hl[:, slots[t], w, o, :],
                                            u_hl[:, par, t, x, a:a + m], start=(t == w == x == 0), stop=(t == w == 1))
                        if t == 1:
                            ins.then_inc(down_ready, 1)
                for r, (o, c) in list(enumerate(order))[4 * final:]:
                    a, m = CHUNKS[c]
                    if final and o == FINAL_SUM_AT and c > 0:
                        final_sums(c - 1)
                    pe.wait_ge(down_free, 24 * g + r + 1)
                    i = 0
                    for t in range(2):
                        for w, x in ((0, 0), (0, 1), (1, 0)):
                            ins = pe.matmul(bank[3 + r % 4][:, 0:m], w_hl[:, slots[t], w, o, :],
                                            u_hl[:, par, t, x, a:a + m], start=(i == 0), stop=(i == 5))
                            if r == i == 0 and not final:
                                ins.then_inc(unit_done, 1)
                            i += 1
                    ins.then_inc(down_ready, 1)

            tile_order = [(o, c) for o in range(KT) for c in range(3)]
            ffn_unit(UNIT_FFN + 2, 1, None, 0, SLOTS[UNIT_FFN + 2], 1)
            ffn_unit(UNIT_FFN + 3, 1, None, 1, SLOTS[UNIT_FFN + 3], 0)
            with pe.Fori(0, (GROUPS - 1) // 2) as i:
                for h in range(2):
                    at = UNIT_FFN + 4 + 6 * h
                    for t in range(2):
                        for b in range(2):
                            ffn_unit(at + 2 * t + b + 12 * i, 2 + 4 * i + 2 * h + t, 1 + 2 * h + t + 4 * i, b, SLOTS[at + 2 * t + b],
                                     2 if t == b == 0 else 1)
                    down(2 * i + h, at + 4 + 12 * i, SLOTS[at + 4:at + 6], h, tile_order)
            pe.wait_ge(down_ready, 24 * (GROUPS - 1))
            pe.sem_inc(unit_done, 2)
            n = N_UNITS - 2
            down(GROUPS - 1, n, SLOTS[n:n + 2], 0, [(o, c) for c in range(3) for o in range(KT)], True)
            final_sums(2)


ADA_DVE = list(range(12)) + [14, 15]
ADA_DOTS_IN = {0: (7,), 1: (8,), 2: (9,), 3: (10,), 4: (11,), 5: (14,), 6: (15,)}
MIX_ORDER = [4, 5, 6, 7, 0, 1, 2, 3]
RET_PE_STEP = [28] + list(range(30, 39))
RET_SUM_STEP = [{41: (0, 1), 43: (2,)}, {40: (0, 1), 42: (2,)}]
MIX_LO_AFTER = {2: (0, (2, 4)), 3: (0, (4, 7)), 4: (1, (2, 4)), 5: (1, (4, 5)), 6: (1, (5, 7)), 7: (2, (2, 3)),
                8: (2, (3, 5)), 9: (2, (5, 7))}
OUT_ORDER = [(o, c) for o in range(5) for c in range(3)] + [(o, c) for c in range(3) for o in range(5, N_OUT)]
OUT_SPLITS = {2: UNIT_OUT + 2, 5: UNIT_OUT + 3, 8: UNIT_OUT + 4, 9: UNIT_OUT + 5, 11: UNIT_OUT + 6, 14: UNIT_OUT + 7,
              21: UNIT_FFN, 22: UNIT_FFN + 1}
NORM2_ITEMS = {19: (0, 1), 20: (2, 3, 4), 21: (5, 6, 7), 22: (8, 9), 23: tuple(range(10, 3 * KT))}
FINAL_SUM_AT = 3
FINAL_LAG = KT + FINAL_SUM_AT + 2
FINAL_POOL = [KT + 4, KT + 5, KT + 6, KT + 7, 2 * KT + 5, 2 * KT + 6, 2 * KT + 7]


def constants():
    q = np.arange(P)[:, None]
    k = np.arange(2 * P)[None, :]
    dist = np.abs(P + q - k).astype(np.float64)
    valid = np.where(q < 64, k < 192, k >= 64)
    slopes = 2.0 ** -np.arange(1, 9)
    bias = np.where(valid[None], -slopes[:, None, None] * dist[None], MASKED).astype(np.float32)
    att_bias = np.stack([np.concatenate([bias[j], bias[j + 4]], axis=1) for j in range(HEADS)])
    lg = np.log1p(-2.0 ** (-5.0 - np.arange(HEADS)))
    tab = np.zeros((HEADS, P, RT_COLS))
    i = np.arange(P)
    for h in range(HEADS):
        diff = i[None, :] - i[:, None]
        tab[h, :, RT_DECAY:RT_DECAY + P] = np.where(diff >= 0, np.exp(lg[h] * np.maximum(diff, 0)), 0.0)
        tab[h, :, RT_Q:RT_Q + P] = np.exp(lg[h] * (i[None, :] + 1.0))
        tab[h, :, RT_K] = np.exp(lg[h] * (P - 1.0 - i))
        tab[h, :64, RT_K + 1] = np.exp(lg[h] * (63.0 - i[:64]))
        tab[h, :, RT_K + 2] = np.exp(lg[h] * P)
        tab[h, :, RT_K + 3] = np.exp(lg[h] * 64)
    return np.eye(P, dtype=np.float32), att_bias, tab.astype(np.float32)


def unit_of(w):
    return w.reshape(KT, P, P).transpose(1, 0, 2).reshape(P, D)


def kernel(**inputs):
    import numpy as _np
    import concourse.bacc as _bacc
    from concourse import mybir as _mybir
    from concourse.bass_utils import run_bass_kernel_spmd as _run

    x = {k: _np.asarray(v) for k, v in inputs.items()}
    w_in, w_out, w_up, w_down = x["w_in"][0], x["w_out"][0], x["w_up"][0], x["w_down"][0]
    aq0, ak0, av0 = 2048, 2560, 2688

    def aq_cols(j):
        return _np.concatenate([w_in[:, aq0 + 64 * h:aq0 + 64 * h + 64] for h in (j, j + 4)], axis=1)

    units = [w_in[:, ak0:ak0 + P], w_in[:, av0:av0 + P], aq_cols(0)]
    for j in range(HEADS):
        units += [w_in[:, 512 * g + P * j:512 * g + P * (j + 1)] for g in range(4)]
        if j < HEADS - 1:
            units.append(aq_cols(j + 1))
    rows = list(range(512)) + [512 + 64 * h + i for j in range(HEADS) for h in (j, j + 4) for i in range(64)]
    w_out = w_out[rows]
    units += [w_out[:, P * o:P * (o + 1)] for o in range(N_OUT)]
    units = [unit_of(u) for u in units]

    def up(g):
        out = []
        for f in (2 * g, 2 * g + 1):
            out += [unit_of(w_up[:, P * f:P * (f + 1)]), unit_of(w_up[:, D_FF + P * f:D_FF + P * (f + 1)])]
        return out

    def down(g):
        return [w_down[P * f:P * (f + 1)] for f in (2 * g, 2 * g + 1)]

    units += up(0)
    for g in range(GROUPS - 1):
        units += up(g + 1) + down(g)
    units += down(GROUPS - 1)

    w_all = _np.concatenate([x["w_ada"][0], x["w_ada_f"]], axis=1)
    b_all = _np.concatenate([x["b_ada"][0], x["b_ada_f"]])
    sh1, sc1, g1, sh2, sc2, g2, shf, scf = (D * i for i in range(8))
    cols = []
    for a, b in ((sc1, sh1), (g1, None), (sc2, sh2), (g2, None), (scf, shf)):
        for k in range(KT):
            cols += [a + P * k] + ([b + P * k] if b is not None else [])
    tiles = _np.stack([w_all[:, c:c + P].T for c in cols])
    biases = _np.stack([b_all[c:c + P] for c in cols], axis=1)

    def by_tile(a):
        return a.reshape(a.shape[0], -1, P).transpose(2, 1, 0)

    ident, att_bias, ret_tab = constants()
    arrays = {
        "x_t": _np.concatenate([x["x_prompt"][0], x["x_sample"][0]]).T,
        "w_units": _np.stack(units),
        "w_ada_t": tiles,
        "b_ada_t": biases,
        "cond_rows": _np.concatenate([x["c_prompt"], x["c_sample"]]),
        "gains": _np.stack([x["norm1_g"][0], x["norm2_g"][0], x["normf_g"]]).reshape(3, KT, P).transpose(2, 0, 1),
        "conv_wb": by_tile(_np.concatenate([x["conv_w"][0], x["conv_b"]])),
        "conv_st": by_tile(x["state_conv"][0, 0]),
        "sinks": x["attn_sinks"][0].reshape(2, HEADS).T,
        "ck_t": x["cache_k"].reshape(P, P).T,
        "cv": x["cache_v"].reshape(P, P),
        "st_in": x["state_ret"].reshape(HEADS, P, P),
        "identity": ident, "att_bias": att_bias, "ret_tab": ret_tab,
    }
    outs = {"y_t": (D, T), "p_state": (HEADS, P, P), "pk_t": (P, P), "pv": (P, P), "conv_out_t": (P, FT, 4),
            "s_state": (HEADS, P, P), "sk_t": (P, S_SAMPLE), "sv": (S_SAMPLE, P)}

    nc = _bacc.Bacc("TRN2", target_bir_lowering=False, num_devices=1, dynamic_dma_scratch_size=1024)
    arrays = {k: _np.ascontiguousarray(v) for k, v in arrays.items()}
    args = [nc.dram_tensor(f"in_{k}", v.shape, _mybir.dt.from_np(v.dtype), kind="ExternalInput").ap() for k, v in arrays.items()]
    args += [nc.dram_tensor(f"out_{k}", s, F32, kind="ExternalOutput").ap() for k, s in outs.items()]
    hymba_step(nc, *args)
    r = _run(nc, [{f"in_{k}": v for k, v in arrays.items()}], core_ids=[0]).results[0]
    r = {k: r[f"out_{k}"] for k in outs}

    y = r["y_t"].T
    conv_rows = r["conv_out_t"].transpose(2, 1, 0).reshape(2, 2, D_FF)
    return (y[None, :S_PROMPT], y[None, S_PROMPT:], r["p_state"][None, None],
            r["pk_t"].T.reshape(1, 1, P, 2, 64), r["pv"].reshape(1, 1, P, 2, 64), conv_rows[0][None, None],
            r["s_state"][None, None], r["sk_t"].T.reshape(1, 1, S_SAMPLE, 2, 64), r["sv"].reshape(1, 1, S_SAMPLE, 2, 64),
            conv_rows[1][None, None])
```
